# Optimizing a Trainium2 kernel written in Bass

```python
import jax, jax.numpy as jnp
from jax import lax
import numpy as np
import math

D_MODEL = 1024
BATCH = 1
SEQ = 256
DEPTH = 2

HEAD_DIM = 64
N_HEADS = D_MODEL // HEAD_DIM
H_FOX = N_HEADS // 2
H_NSA = N_HEADS - H_FOX
NSA_GROUPS = 2
H_MOBA = N_HEADS
D_FF = -(-(8 * D_MODEL) // (3 * 256)) * 256
ROPE_THETA = 10000.0
RMS_EPS = 1e-6
Q_BLOCK = 128
CMP_STRIDE = 16
CMP_LEN = 2 * CMP_STRIDE
CMP_HIDDEN = 4 * HEAD_DIM
SLC_BLOCK = 64
SLC_TOPN = 16
WINDOW = 512
MOBA_BLOCK = 256
MOBA_TOPK = 3
MOBA_Q_CHUNK = 32
NEG_INF = -1e30

EVEN_SPLITS = (3 * [H_FOX * HEAD_DIM] + [H_FOX] + [H_NSA * HEAD_DIM]
               + 6 * [NSA_GROUPS * HEAD_DIM] + [3 * H_NSA])
EVEN_IN = sum(EVEN_SPLITS)
EVEN_SPLIT_IDX = [int(c) for c in np.cumsum(EVEN_SPLITS)[:-1]]


def rmsnorm(x, g):
    xf = x.astype(jnp.float32)
    y = xf * lax.rsqrt(jnp.mean(xf * xf, axis=-1, keepdims=True) + RMS_EPS)
    return (y * g.astype(jnp.float32)).astype(x.dtype)

def to_heads(t, n):
    b, s, _ = t.shape
    return t.reshape(b, s, n, HEAD_DIM).transpose(0, 2, 1, 3)

def from_heads(t):
    b, h, s, d = t.shape
    return t.transpose(0, 2, 1, 3).reshape(b, s, h * d)

def rope_tables(s):
    inv = ROPE_THETA ** (-jnp.arange(0, HEAD_DIM, 2, dtype=jnp.float32) / HEAD_DIM)
    ang = jnp.arange(s, dtype=jnp.float32)[:, None] * inv[None, :]
    return jnp.cos(ang), jnp.sin(ang)

def apply_rope(t, cos, sin):
    tf = t.astype(jnp.float32)
    t1, t2 = tf[..., :HEAD_DIM // 2], tf[..., HEAD_DIM // 2:]
    return jnp.concatenate([t1 * cos - t2 * sin, t2 * cos + t1 * sin], axis=-1).astype(t.dtype)

def masked_softmax(s, mask):
    s = jnp.where(mask, s, NEG_INF)
    e = jnp.where(mask, jnp.exp(s - jnp.max(s, axis=-1, keepdims=True)), 0.0)
    return e / jnp.maximum(jnp.sum(e, axis=-1, keepdims=True), 1e-30)

def sweep(fn, s, block):
    out = lax.map(fn, jnp.arange(s // block))
    nb, b, h, q, d = out.shape
    return out.transpose(1, 2, 0, 3, 4).reshape(b, h, nb * q, d)

def fox_attention(q, k, v, log_f):
    b, h, s, d = q.shape
    c = jnp.cumsum(log_f, axis=-1)
    kpos = jnp.arange(s)
    scale = d ** -0.5

    def block(i):
        qs = i * Q_BLOCK
        qb = lax.dynamic_slice_in_dim(q, qs, Q_BLOCK, axis=2)
        cb = lax.dynamic_slice_in_dim(c, qs, Q_BLOCK, axis=2)
        qpos = qs + jnp.arange(Q_BLOCK)
        sc = (jnp.einsum('bhqd,bhkd->bhqk', qb, k, preferred_element_type=jnp.float32) * scale
              + cb[..., :, None] - c[..., None, :])
        p = masked_softmax(sc, kpos[None, :] <= qpos[:, None])
        return jnp.einsum('bhqk,bhkd->bhqd', p.astype(v.dtype), v)

    return sweep(block, s, Q_BLOCK)

def nsa_compress(t, pe, w1, w2):
    b, g, s, d = t.shape
    ch = t.reshape(b, g, s // CMP_STRIDE, CMP_STRIDE, d)
    blk = jnp.concatenate([ch[:, :, :-1], ch[:, :, 1:]], axis=3) + pe
    blk = blk.reshape(b, g, blk.shape[2], CMP_LEN * d)
    return jax.nn.gelu(blk @ w1) @ w2

def nsa_attention(q, kc, vc, ks, vs, kw, vw, gates):
    b, h, s, d = q.shape
    g = ks.shape[1]
    r = h // g
    nc = kc.shape[2]
    ns = s // SLC_BLOCK
    n_sel = min(SLC_TOPN, ns)
    ratio = SLC_BLOCK // CMP_STRIDE
    scale = d ** -0.5
    cmp_end = jnp.arange(nc) * CMP_STRIDE + CMP_LEN - 1
    ks_blk = ks.reshape(b, g, ns, SLC_BLOCK, d)
    vs_blk = vs.reshape(b, g, ns, SLC_BLOCK, d)
    wpad = ((0, 0), (0, 0), (WINDOW, 0), (0, 0))
    kw_pad, vw_pad = jnp.pad(kw, wpad), jnp.pad(vw, wpad)
    bi = jnp.arange(b)[:, None, None, None]
    gi = jnp.arange(g)[None, :, None, None]
    sblk = jnp.arange(ns)

    def block(i):
        qs = i * Q_BLOCK
        qpos = qs + jnp.arange(Q_BLOCK)
        qb = lax.dynamic_slice_in_dim(q, qs, Q_BLOCK, axis=2).reshape(b, g, r, Q_BLOCK, d)
        gb = lax.dynamic_slice_in_dim(gates, qs, Q_BLOCK, axis=2).reshape(b, g, r, Q_BLOCK, 3)
        sc = jnp.einsum('bgrqd,bgcd->bgrqc', qb, kc, preferred_element_type=jnp.float32) * scale
        pc = masked_softmax(sc, cmp_end[None, :] <= qpos[:, None])
        oc = jnp.einsum('bgrqc,bgcd->bgrqd', pc.astype(vc.dtype), vc)
        imp = jnp.pad(pc.sum(axis=2), ((0, 0), (0, 0), (0, 0), (1, 1)))
        imp = imp[..., :ratio * ns].reshape(b, g, Q_BLOCK, ns, ratio).sum(-1) + imp[..., ratio::ratio]
        qblk = qpos // SLC_BLOCK
        forced = ((sblk[None, :] == 0) | (sblk[None, :] == qblk[:, None])
                  | (sblk[None, :] == qblk[:, None] - 1))
        imp = jnp.where(forced, 1e9, jnp.where(sblk[None, :] > qblk[:, None], -1e9, imp))
        _, idx = lax.top_k(imp, n_sel)
        ksel = ks_blk[bi, gi, idx].reshape(b, g, Q_BLOCK, n_sel * SLC_BLOCK, d)
        vsel = vs_blk[bi, gi, idx].reshape(b, g, Q_BLOCK, n_sel * SLC_BLOCK, d)
        spos = (idx[..., None] * SLC_BLOCK + jnp.arange(SLC_BLOCK)).reshape(b, g, 1, Q_BLOCK, n_sel * SLC_BLOCK)
        ss = jnp.einsum('bgrqd,bgqkd->bgrqk', qb, ksel, preferred_element_type=jnp.float32) * scale
        psl = masked_softmax(ss, spos <= qpos[:, None])
        osl = jnp.einsum('bgrqk,bgqkd->bgrqd', psl.astype(vsel.dtype), vsel)
        kwin = lax.dynamic_slice_in_dim(kw_pad, qs, WINDOW + Q_BLOCK, axis=2)
        vwin = lax.dynamic_slice_in_dim(vw_pad, qs, WINDOW + Q_BLOCK, axis=2)
        wpos = qs - WINDOW + jnp.arange(WINDOW + Q_BLOCK)
        dlt = qpos[:, None] - wpos[None, :]
        sw = jnp.einsum('bgrqd,bgkd->bgrqk', qb, kwin, preferred_element_type=jnp.float32) * scale
        pw = masked_softmax(sw, (dlt >= 0) & (dlt < WINDOW) & (wpos[None, :] >= 0))
        ow = jnp.einsum('bgrqk,bgkd->bgrqd', pw.astype(vwin.dtype), vwin)
        o = gb[..., 0:1] * oc + gb[..., 1:2] * osl + gb[..., 2:3] * ow
        return o.reshape(b, h, Q_BLOCK, d).astype(q.dtype)

    return sweep(block, s, Q_BLOCK)

def moba_attention(q, k, v):
    b, h, s, d = q.shape
    s_pad = -(-s // MOBA_BLOCK) * MOBA_BLOCK
    pad = ((0, 0), (0, 0), (0, s_pad - s), (0, 0))
    kp, vp = jnp.pad(k, pad), jnp.pad(v, pad)
    nb = s_pad // MOBA_BLOCK
    n_top = min(MOBA_TOPK, nb)
    n_s = n_top * MOBA_BLOCK
    kb = kp.reshape(b, h, nb, MOBA_BLOCK, d)
    vb = vp.reshape(b, h, nb, MOBA_BLOCK, d)
    kbar = jnp.mean(kb.astype(jnp.float32), axis=3)
    bi = jnp.arange(b)[:, None, None, None]
    hi = jnp.arange(h)[None, :, None, None]
    blk_ids = jnp.arange(nb)
    scale = d ** -0.5

    def chunk(i):
        qs = i * MOBA_Q_CHUNK
        cur = qs // MOBA_BLOCK
        qpos = qs + jnp.arange(MOBA_Q_CHUNK)
        qb = lax.dynamic_slice_in_dim(q, qs, MOBA_Q_CHUNK, axis=2)
        gate = jnp.einsum('bhqd,bhnd->bhqn', qb.astype(jnp.float32), kbar)
        gate = jnp.where(blk_ids < cur, gate, NEG_INF)
        _, idx = lax.top_k(gate, n_top)
        valid = jnp.broadcast_to((idx < cur)[..., None], idx.shape + (MOBA_BLOCK,))
        valid = valid.reshape(b, h, MOBA_Q_CHUNK, n_s)
        ksel = kb[bi, hi, idx].reshape(b, h, MOBA_Q_CHUNK, n_s, d)
        vsel = vb[bi, hi, idx].reshape(b, h, MOBA_Q_CHUNK, n_s, d)
        kown = lax.dynamic_slice_in_dim(kp, cur * MOBA_BLOCK, MOBA_BLOCK, axis=2)
        vown = lax.dynamic_slice_in_dim(vp, cur * MOBA_BLOCK, MOBA_BLOCK, axis=2)
        own_pos = cur * MOBA_BLOCK + jnp.arange(MOBA_BLOCK)
        own_mask = jnp.broadcast_to(own_pos[None, :] <= qpos[:, None], (b, h, MOBA_Q_CHUNK, MOBA_BLOCK))
        s_sel = jnp.einsum('bhqd,bhqkd->bhqk', qb, ksel, preferred_element_type=jnp.float32)
        s_own = jnp.einsum('bhqd,bhkd->bhqk', qb, kown, preferred_element_type=jnp.float32)
        p = masked_softmax(jnp.concatenate([s_sel, s_own], axis=-1) * scale,
                           jnp.concatenate([valid, own_mask], axis=-1)).astype(v.dtype)
        return (jnp.einsum('bhqk,bhqkd->bhqd', p[..., :n_s], vsel)
                + jnp.einsum('bhqk,bhkd->bhqd', p[..., n_s:], vown))

    return sweep(chunk, s, MOBA_Q_CHUNK)

def even_mixer(h, w_in, b_f, pe_k, w1_k, w2_k, pe_v, w1_v, w2_v, w_out, cos, sin):
    b, s, _ = h.shape
    (fq, fk, fv, f_logit, nq, kc, vc, ks, vs, kw, vw, g_logit) = jnp.split(h @ w_in, EVEN_SPLIT_IDX, axis=-1)
    log_f = jax.nn.log_sigmoid(f_logit.astype(jnp.float32) + b_f.astype(jnp.float32)).transpose(0, 2, 1)
    o_fox = fox_attention(to_heads(fq, H_FOX), to_heads(fk, H_FOX), to_heads(fv, H_FOX), log_f)
    rot = lambda t, n: apply_rope(to_heads(t, n), cos, sin)
    gates = jax.nn.sigmoid(g_logit.astype(jnp.float32)).reshape(b, s, H_NSA, 3).transpose(0, 2, 1, 3)
    o_nsa = nsa_attention(rot(nq, H_NSA),
                          nsa_compress(rot(kc, NSA_GROUPS), pe_k, w1_k, w2_k),
                          nsa_compress(to_heads(vc, NSA_GROUPS), pe_v, w1_v, w2_v),
                          rot(ks, NSA_GROUPS), to_heads(vs, NSA_GROUPS),
                          rot(kw, NSA_GROUPS), to_heads(vw, NSA_GROUPS), gates)
    return jnp.concatenate([from_heads(o_fox), from_heads(o_nsa)], axis=-1) @ w_out

def odd_mixer(h, w_in, w_out, cos, sin):
    q, k, v = jnp.split(h @ w_in, 3, axis=-1)
    o = moba_attention(apply_rope(to_heads(q, H_MOBA), cos, sin),
                       apply_rope(to_heads(k, H_MOBA), cos, sin),
                       to_heads(v, H_MOBA))
    return from_heads(o) @ w_out

def swiglu(h, w_gate, w_up, w_down):
    return (jax.nn.silu(h @ w_gate) * (h @ w_up)) @ w_down

def first_inputs(seed: int = 0) -> dict:
    key = jax.random.key(seed)
    ks = jax.random.split(key, 20)
    ne, no = (DEPTH + 1) // 2, DEPTH // 2
    f32 = jnp.float32

    def dense(k, shape, fan_in):
        return jax.random.normal(k, shape, f32) * fan_in ** -0.5

    def gain(k):
        return 1.0 + 0.05 * jax.random.normal(k, (DEPTH, D_MODEL), f32)

    cmp_in = CMP_LEN * HEAD_DIM
    return {
        'x': jax.random.normal(ks[0], (BATCH, SEQ, D_MODEL), f32),
        'ev_w_in': dense(ks[1], (ne, D_MODEL, EVEN_IN), D_MODEL),
        'ev_b_f': jax.random.uniform(ks[2], (ne, H_FOX), f32, 1.0, 6.0),
        'ev_cmp_pe_k': 0.5 * jax.random.normal(ks[3], (ne, CMP_LEN, HEAD_DIM), f32),
        'ev_cmp_w1_k': dense(ks[4], (ne, cmp_in, CMP_HIDDEN), cmp_in),
        'ev_cmp_w2_k': dense(ks[5], (ne, CMP_HIDDEN, HEAD_DIM), CMP_HIDDEN),
        'ev_cmp_pe_v': 0.5 * jax.random.normal(ks[6], (ne, CMP_LEN, HEAD_DIM), f32),
        'ev_cmp_w1_v': dense(ks[7], (ne, cmp_in, CMP_HIDDEN), cmp_in),
        'ev_cmp_w2_v': dense(ks[8], (ne, CMP_HIDDEN, HEAD_DIM), CMP_HIDDEN),
        'ev_w_out': dense(ks[9], (ne, (H_FOX + H_NSA) * HEAD_DIM, D_MODEL), (H_FOX + H_NSA) * HEAD_DIM),
        'od_w_in': dense(ks[10], (no, D_MODEL, 3 * H_MOBA * HEAD_DIM), D_MODEL),
        'od_w_out': dense(ks[11], (no, H_MOBA * HEAD_DIM, D_MODEL), H_MOBA * HEAD_DIM),
        'g_mix_pre': gain(ks[12]),
        'g_mix_post': gain(ks[13]),
        'g_ffn_pre': gain(ks[14]),
        'g_ffn_post': gain(ks[15]),
        'ffn_w_gate': dense(ks[16], (DEPTH, D_MODEL, D_FF), D_MODEL),
        'ffn_w_up': dense(ks[17], (DEPTH, D_MODEL, D_FF), D_MODEL),
        'ffn_w_down': dense(ks[18], (DEPTH, D_FF, D_MODEL), D_FF),
    }

def first_block(x, ev_w_in, ev_b_f, ev_cmp_pe_k, ev_cmp_w1_k, ev_cmp_w2_k, ev_cmp_pe_v,
              ev_cmp_w1_v, ev_cmp_w2_v, ev_w_out, od_w_in, od_w_out, g_mix_pre, g_mix_post,
              g_ffn_pre, g_ffn_post, ffn_w_gate, ffn_w_up, ffn_w_down):
    cos, sin = rope_tables(x.shape[1])
    for layer in range(DEPTH):
        h = rmsnorm(x, g_mix_pre[layer])
        if layer % 2 == 0:
            e = layer // 2
            y = even_mixer(h, ev_w_in[e], ev_b_f[e], ev_cmp_pe_k[e], ev_cmp_w1_k[e], ev_cmp_w2_k[e],
                           ev_cmp_pe_v[e], ev_cmp_w1_v[e], ev_cmp_w2_v[e], ev_w_out[e], cos, sin)
        else:
            o = layer // 2
            y = odd_mixer(h, od_w_in[o], od_w_out[o], cos, sin)
        x = x + rmsnorm(y, g_mix_post[layer])
        h = rmsnorm(x, g_ffn_pre[layer])
        x = x + rmsnorm(swiglu(h, ffn_w_gate[layer], ffn_w_up[layer], ffn_w_down[layer]), g_ffn_post[layer])
    return x


DEPTH_2 = 1

HGRN_HEADS = 8
HGRN_DK = 128
HGRN_DV = D_MODEL // HGRN_HEADS
HGRN_KEY_WIDTH = HGRN_HEADS * HGRN_DK
HGRN_WIDTH = HGRN_HEADS * HGRN_DV
HGRN_CHUNK = 64

HYENA_WIDTH = D_MODEL
HYENA_SHORT = 3
HYENA_BANDS = 16
HYENA_EMB = 1 + 2 * HYENA_BANDS
HYENA_FILTER_HIDDEN = 64
HYENA_MIN_DECAY = -math.log(1e-2) / 1.5
HYENA_MAX_DECAY = -math.log(1e-2) / 0.3

PEER_HEADS = 8
PEER_NKEYS = 128
PEER_EXPERTS = PEER_NKEYS * PEER_NKEYS
PEER_QDIM = 256
PEER_TOPK = 16
PEER_TOKEN_BLOCK = 128

N_BRANCHES = 2
IN_SPLITS = (HGRN_KEY_WIDTH, 2 * HGRN_KEY_WIDTH, 3 * HGRN_KEY_WIDTH,
             3 * HGRN_KEY_WIDTH + HGRN_WIDTH, 3 * HGRN_KEY_WIDTH + 2 * HGRN_WIDTH,
             3 * HGRN_KEY_WIDTH + 2 * HGRN_WIDTH + 3 * HYENA_WIDTH)
IN_COLS = 3 * HGRN_KEY_WIDTH + 2 * HGRN_WIDTH + 3 * HYENA_WIDTH + N_BRANCHES * D_MODEL


def rmsnorm_2(x, g):
    xf = x.astype(jnp.float32)
    y = xf * lax.rsqrt(jnp.mean(xf * xf, axis=-1, keepdims=True) + RMS_EPS)
    return (y * g.astype(jnp.float32)).astype(x.dtype)

def hgrn2_chunk_scan(q, k, logf, v):
    n, s, h, dk = q.shape
    dv = v.shape[-1]
    nc = s // HGRN_CHUNK

    def to_chunks(a):
        return a.reshape(n, nc, HGRN_CHUNK, h, a.shape[-1]).transpose(1, 0, 3, 2, 4)

    qc, kc, fc, vc = to_chunks(q), to_chunks(k), to_chunks(logf), to_chunks(v)
    incl = jnp.tril(jnp.ones((HGRN_CHUNK, HGRN_CHUNK), dtype=bool))[:, :, None]

    def step(state, inp):
        qb, kb, fb, vb = inp
        b = jnp.cumsum(fb, axis=2)
        b_last = b[:, :, -1:, :]
        inter = jnp.einsum('nhtk,nhkv->nhtv', qb * jnp.exp(b), state)
        diff = b[:, :, :, None, :] - b[:, :, None, :, :]
        decay = jnp.exp(jnp.where(incl, diff, -jnp.inf))
        scores = jnp.einsum('nhtk,nhsk,nhtsk->nhts', qb, kb, decay)
        intra = jnp.einsum('nhts,nhsv->nhtv', scores, vb)
        new_state = (jnp.exp(b_last[:, :, 0, :, None]) * state
                     + jnp.einsum('nhsk,nhsv->nhkv', kb * jnp.exp(b_last - b), vb))
        return new_state, inter + intra

    s0 = jnp.zeros((n, h, dk, dv), jnp.float32)
    _, out = lax.scan(step, s0, (qc, kc, fc, vc))
    return out.transpose(1, 0, 3, 2, 4).reshape(n, s, h, dv)

def centred_short_conv(x, w, b):
    L = x.shape[1]
    pad = HYENA_SHORT // 2
    xp = jnp.pad(x, ((0, 0), (pad, pad), (0, 0)))
    y = b
    for j in range(HYENA_SHORT):
        y = y + xp[:, j:j + L] * w[j]
    return y

def hyena_filters(seq_len, w1, b1, freq1, w2, b2, freq2, w3, decay_rate):
    f32 = jnp.float32
    pos = jnp.arange(seq_len, dtype=f32)
    t = pos / max(seq_len - 1, 1)
    bands = jnp.linspace(1e-4, HYENA_BANDS - 1, HYENA_BANDS, dtype=f32)
    ang = (2.0 * math.pi / seq_len) * pos[:, None] * bands[None, :]
    z = jnp.concatenate([t[:, None], jnp.cos(ang), -jnp.sin(ang)], axis=-1)
    hid = jnp.sin(freq1.astype(f32) * (z @ w1.astype(f32) + b1.astype(f32)))
    hid = jnp.sin(freq2.astype(f32) * (hid @ w2.astype(f32) + b2.astype(f32)))
    filt = (hid @ w3.astype(f32)) * jnp.exp(-t[:, None] * jnp.abs(decay_rate.astype(f32))[None, :])
    return filt[:, :HYENA_WIDTH], filt[:, HYENA_WIDTH:]

def bidirectional_fftconv(u, h_fwd, h_bwd, bias):
    L = u.shape[1]
    kern = jnp.concatenate([h_fwd, jnp.zeros_like(h_fwd[:1]), h_bwd[1:][::-1]], axis=0)
    uf32 = u.astype(jnp.float32)
    uf = jnp.fft.rfft(uf32, n=2 * L, axis=1)
    kf = jnp.fft.rfft(kern, n=2 * L, axis=0)
    y = jnp.fft.irfft(uf * kf[None], n=2 * L, axis=1)[:, :L]
    return (y + uf32 * bias.astype(jnp.float32)).astype(u.dtype)

def hybrid_mixer(xn, w_in, lb, hgrn_norm_g, conv_w, conv_b, filt_w1, filt_b1, filt_freq1,
                 filt_w2, filt_b2, filt_freq2, filt_w3, filt_decay, hyena_bias,
                 w_branch_a, w_branch_b, w_out):
    B, L, _ = xn.shape
    f32 = jnp.float32
    proj = jnp.einsum('bld,dc->blc', xn, w_in)
    q, zf_fwd, zf_bwd, inp, og, hy, gates = jnp.split(proj, IN_SPLITS, axis=-1)

    def heads(a, d):
        return a.astype(f32).reshape(B, L, HGRN_HEADS, d)

    lbh = lb.reshape(HGRN_HEADS, HGRN_DK)

    def forget(z):
        zh = heads(z, HGRN_DK)
        logf = jnp.log(lbh + (1.0 - lbh) * jax.nn.sigmoid(zh))
        k = (1.0 - lbh) * jax.nn.sigmoid(-zh)
        return logf, k

    logf_f, k_f = forget(zf_fwd)
    logf_b, k_b = forget(zf_bwd)
    qh = jax.nn.silu(heads(q, HGRN_DK))
    vh = heads(inp, HGRN_DV)
    rev = lambda a: a[:, ::-1]
    o2 = hgrn2_chunk_scan(jnp.concatenate([qh, rev(qh)], axis=0),
                          jnp.concatenate([k_f, rev(k_b)], axis=0),
                          jnp.concatenate([logf_f, rev(logf_b)], axis=0),
                          jnp.concatenate([vh, rev(vh)], axis=0))
    o = o2[:B] + rev(o2[B:])
    o = rmsnorm_2(o, hgrn_norm_g).reshape(B, L, HGRN_WIDTH)
    y_a = jnp.einsum('blc,cd->bld', (o * jax.nn.silu(og.astype(f32))).astype(xn.dtype), w_branch_a)

    hy = centred_short_conv(hy, conv_w, conv_b)
    x0, x1, v = jnp.split(hy, 3, axis=-1)
    h_f, h_b = hyena_filters(L, filt_w1, filt_b1, filt_freq1, filt_w2, filt_b2, filt_freq2,
                             filt_w3, filt_decay)
    y_b = x0 * bidirectional_fftconv(v * x1, h_f, h_b, hyena_bias)
    y_b = jnp.einsum('blc,cd->bld', y_b, w_branch_b)

    g_a, g_b = jnp.split(gates, N_BRANCHES, axis=-1)
    merged = jax.nn.sigmoid(g_a) * y_a + jax.nn.sigmoid(g_b) * y_b
    return jnp.einsum('bld,de->ble', merged, w_out)

def peer_ffn(xn, w_q, subkeys, u_tab, v_tab):
    B, L, D = xn.shape
    blocks = xn.reshape(-1, PEER_TOKEN_BLOCK, D)
    sk = subkeys.astype(jnp.float32)

    def block(xb):
        T = xb.shape[0]
        qh = (xb @ w_q).astype(jnp.float32).reshape(T, PEER_HEADS, 2, PEER_QDIM // 2)
        s = jnp.einsum('thpc,hpnc->thpn', qh, sk)
        s1, i1 = lax.top_k(s[:, :, 0], PEER_TOPK)
        s2, i2 = lax.top_k(s[:, :, 1], PEER_TOPK)
        cand_s = (s1[..., :, None] + s2[..., None, :]).reshape(T, PEER_HEADS, PEER_TOPK * PEER_TOPK)
        cand_i = (i1[..., :, None] * PEER_NKEYS + i2[..., None, :]).reshape(T, PEER_HEADS, PEER_TOPK * PEER_TOPK)
        top_s, pos = lax.top_k(cand_s, PEER_TOPK)
        experts = jnp.take_along_axis(cand_i, pos, axis=-1)
        g = jax.nn.softmax(top_s, axis=-1).astype(xb.dtype)
        u = jnp.take(u_tab, experts, axis=0)
        v = jnp.take(v_tab, experts, axis=0)
        act = jax.nn.gelu(jnp.einsum('td,thkd->thk', xb, u)) * g
        return jnp.einsum('thk,thkd->td', act, v)

    return lax.map(block, blocks).reshape(B, L, D)

def second_inputs(seed: int = 0) -> dict:
    key = jax.random.key(seed)
    ks = jax.random.split(key, 26)

    def nrm(k, shape, scale):
        return jax.random.normal(k, shape, jnp.float32) * scale

    decay_base = jnp.linspace(HYENA_MIN_DECAY, HYENA_MAX_DECAY, 2 * HYENA_WIDTH, dtype=jnp.float32)
    return {
        "x": nrm(ks[0], (BATCH, SEQ, D_MODEL), 1.0),
        "norm_mix_g": 1.0 + nrm(ks[1], (DEPTH_2, D_MODEL), 0.02),
        "w_in": nrm(ks[2], (DEPTH_2, D_MODEL, IN_COLS), D_MODEL ** -0.5),
        "hgrn_lb_logits": nrm(ks[3], (DEPTH_2 + 1, HGRN_KEY_WIDTH), 0.1),
        "hgrn_norm_g": 1.0 + nrm(ks[4], (DEPTH_2, HGRN_DV), 0.02),
        "hyena_conv_w": nrm(ks[5], (DEPTH_2, HYENA_SHORT, 3 * HYENA_WIDTH), HYENA_SHORT ** -0.5),
        "hyena_conv_b": nrm(ks[6], (DEPTH_2, 3 * HYENA_WIDTH), 0.02),
        "filt_w1": nrm(ks[7], (DEPTH_2, HYENA_EMB, HYENA_FILTER_HIDDEN), HYENA_EMB ** -0.5),
        "filt_b1": nrm(ks[8], (DEPTH_2, HYENA_FILTER_HIDDEN), 0.1),
        "filt_freq1": 1.0 + nrm(ks[9], (DEPTH_2, HYENA_FILTER_HIDDEN), 0.02),
        "filt_w2": nrm(ks[10], (DEPTH_2, HYENA_FILTER_HIDDEN, HYENA_FILTER_HIDDEN), HYENA_FILTER_HIDDEN ** -0.5),
        "filt_b2": nrm(ks[11], (DEPTH_2, HYENA_FILTER_HIDDEN), 0.1),
        "filt_freq2": 1.0 + nrm(ks[12], (DEPTH_2, HYENA_FILTER_HIDDEN), 0.02),
        "filt_w3": nrm(ks[13], (DEPTH_2, HYENA_FILTER_HIDDEN, 2 * HYENA_WIDTH), 0.02 * HYENA_FILTER_HIDDEN ** -0.5),
        "filt_decay": decay_base[None, :] + nrm(ks[14], (DEPTH_2, 2 * HYENA_WIDTH), 0.1),
        "hyena_bias": nrm(ks[15], (DEPTH_2, HYENA_WIDTH), 0.1),
        "w_branch_a": nrm(ks[16], (DEPTH_2, HGRN_WIDTH, D_MODEL), HGRN_WIDTH ** -0.5),
        "w_branch_b": nrm(ks[17], (DEPTH_2, HYENA_WIDTH, D_MODEL), HYENA_WIDTH ** -0.5),
        "w_out": nrm(ks[18], (DEPTH_2, D_MODEL, D_MODEL), D_MODEL ** -0.5),
        "norm_ffn_g": 1.0 + nrm(ks[19], (DEPTH_2, D_MODEL), 0.02),
        "peer_w_q": nrm(ks[20], (DEPTH_2, D_MODEL, PEER_HEADS * PEER_QDIM), D_MODEL ** -0.5),
        "peer_subkeys": nrm(ks[21], (DEPTH_2, PEER_HEADS, 2, PEER_NKEYS, PEER_QDIM // 2), (PEER_QDIM // 2) ** -0.5),
        "peer_u": nrm(ks[22], (DEPTH_2, PEER_EXPERTS, D_MODEL), D_MODEL ** -0.5),
        "peer_v": nrm(ks[23], (DEPTH_2, PEER_EXPERTS, D_MODEL), 0.2),
        "norm_final_g": 1.0 + nrm(ks[24], (D_MODEL,), 0.02),
    }

def second_block(x, norm_mix_g, w_in, hgrn_lb_logits, hgrn_norm_g, hyena_conv_w, hyena_conv_b,
              filt_w1, filt_b1, filt_freq1, filt_w2, filt_b2, filt_freq2, filt_w3, filt_decay,
              hyena_bias, w_branch_a, w_branch_b, w_out, norm_ffn_g, peer_w_q, peer_subkeys,
              peer_u, peer_v, norm_final_g):
    lb_table = jnp.cumsum(jax.nn.softmax(hgrn_lb_logits.astype(jnp.float32), axis=0), axis=0)
    h = x
    for layer in range(DEPTH_2):
        h = h + hybrid_mixer(rmsnorm_2(h, norm_mix_g[layer]), w_in[layer], lb_table[layer],
                             hgrn_norm_g[layer], hyena_conv_w[layer], hyena_conv_b[layer],
                             filt_w1[layer], filt_b1[layer], filt_freq1[layer],
                             filt_w2[layer], filt_b2[layer], filt_freq2[layer],
                             filt_w3[layer], filt_decay[layer], hyena_bias[layer],
                             w_branch_a[layer], w_branch_b[layer], w_out[layer])
        h = h + peer_ffn(rmsnorm_2(h, norm_ffn_g[layer]), peer_w_q[layer], peer_subkeys[layer],
                         peer_u[layer], peer_v[layer])
    return rmsnorm_2(h, norm_final_g)


def setup_inputs(seed=0):
    out = dict(first_inputs(seed))
    for name, value in second_inputs(seed + 1).items():
        if name != "x":
            out[name + "_2"] = value
    return out


def reference(
    x, ev_w_in, ev_b_f, ev_cmp_pe_k, ev_cmp_w1_k, ev_cmp_w2_k, ev_cmp_pe_v, ev_cmp_w1_v,
    ev_cmp_w2_v, ev_w_out, od_w_in, od_w_out, g_mix_pre, g_mix_post, g_ffn_pre, g_ffn_post,
    ffn_w_gate, ffn_w_up, ffn_w_down, norm_mix_g_2, w_in_2, hgrn_lb_logits_2, hgrn_norm_g_2,
    hyena_conv_w_2, hyena_conv_b_2, filt_w1_2, filt_b1_2, filt_freq1_2, filt_w2_2, filt_b2_2,
    filt_freq2_2, filt_w3_2, filt_decay_2, hyena_bias_2, w_branch_a_2, w_branch_b_2, w_out_2,
    norm_ffn_g_2, peer_w_q_2, peer_subkeys_2, peer_u_2, peer_v_2, norm_final_g_2,
):
    x = first_block(
        x, ev_w_in, ev_b_f, ev_cmp_pe_k, ev_cmp_w1_k, ev_cmp_w2_k, ev_cmp_pe_v, ev_cmp_w1_v,
        ev_cmp_w2_v, ev_w_out, od_w_in, od_w_out, g_mix_pre, g_mix_post, g_ffn_pre, g_ffn_post,
        ffn_w_gate, ffn_w_up, ffn_w_down,
    )
    return second_block(
        x, norm_mix_g_2, w_in_2, hgrn_lb_logits_2, hgrn_norm_g_2, hyena_conv_w_2,
        hyena_conv_b_2, filt_w1_2, filt_b1_2, filt_freq1_2, filt_w2_2, filt_b2_2, filt_freq2_2,
        filt_w3_2, filt_decay_2, hyena_bias_2, w_branch_a_2, w_branch_b_2, w_out_2,
        norm_ffn_g_2, peer_w_q_2, peer_subkeys_2, peer_u_2, peer_v_2, norm_final_g_2,
    )


_drawn_inputs = setup_inputs


def setup_inputs(seed=0):
    import zlib

    import numpy as np

    out = dict(_drawn_inputs(seed))
    spreads = {}
    factors = {'norm_mix_g_2': 8.0,
     'hgrn_lb_logits_2': 8.0,
     'hgrn_norm_g_2': 42.004,
     'hyena_conv_b_2': 28.657,
     'filt_w1_2': 3.328,
     'filt_b1_2': 8.0,
     'filt_freq1_2': 8.0,
     'filt_w2_2': 3.061,
     'filt_b2_2': 8.0,
     'filt_freq2_2': 8.0,
     'filt_w3_2': 3.058,
     'filt_decay_2': 8.0,
     'norm_ffn_g_2': 63.8,
     'norm_final_g_2': 22.893}
    for name, (base, spread) in spreads.items():
        noise = np.random.default_rng([zlib.crc32(name.encode()), seed]).standard_normal(out[name].shape)
        drawn = base * np.exp(spread * noise) if base else spread * noise
        out[name] = __import__('jax').numpy.asarray(drawn.astype(out[name].dtype))
    for name, factor in factors.items():
        out[name] = (out[name] * factor).astype(out[name].dtype)
    return out
```

```python
from contextlib import ExitStack

import numpy as np

import concourse.bass as bass
from concourse import mybir

ALU = mybir.AluOpType
ACT = mybir.ActivationFunctionType
F32 = mybir.dt.float32
BF16 = mybir.dt.bfloat16
I32 = mybir.dt.int32
U32 = mybir.dt.uint32
AX_X = mybir.AxisListType.X

P = 128
D = 1024
KC = D // P
T = 256
TT = T // P
HD = 64
FF = 2816
FC = FF // P
RING = 3
EPS = 1e-6
NEG = -1e30
NC = T // 16 - 1
NFFT = 511
HH = 8
LEVELS = 7
NKEYS = 128
TOPK = 16

N_FOX, N_NSA, N_OUT, N_FFN, N_MOBA = 4 * 3, 4 + 8 + 4 + 4, KC, 3 * FC, 8 * 3
N_HGRN, N_HYENA, N_PQ, N_PEER = HH * 6, KC * 4, 16, 2 * NKEYS
_at = 0
START = {}
for _name, _n in (("fox", N_FOX), ("nsa", N_NSA), ("out0", N_OUT), ("ffn0", N_FFN), ("moba", N_MOBA),
                  ("out1", N_OUT), ("ffn1", N_FFN), ("hgrn", N_HGRN), ("hyena", N_HYENA), ("wa", N_OUT),
                  ("wb", N_OUT), ("out2", N_OUT), ("pq", N_PQ), ("peer", N_PEER)):
    START[_name] = _at // 2
    _at += _n
N_BLOCKS = _at // 2

SMALL = {}
_at = 0
for _name, _n in (("wfg", KC * 40), ("w2k", 2 * HD), ("w2v", 2 * HD), ("pek", 16), ("pev", 16), ("bf", 1),
                  ("gains", 11 * KC), ("lbl", 2 * HH), ("hg", 1), ("convw", 24 * 3), ("convb", 24),
                  ("hbias", KC), ("fw1", 64), ("fvec", 4), ("fw2", 64)):
    SMALL[_name] = (_at, _n)
    _at += _n
N_SMALL = _at

TABLE = {}
_at = 0
for _name, _n in (("eye", P), ("iota", P), ("cos", 2 * T), ("sin", 2 * T), ("rot", P), ("causal", 384),
                  ("cmpadd", 4 * 16), ("cmpmul", 4 * 16), ("dft", 2 * 2 * T), ("idft", 4 * T),
                  ("zT", T), ("taprow", T), ("cmask", 2), ("ebot", 8), ("etop", 8), ("tapmask", 2)):
    TABLE[_name] = (_at, _n)
    _at += _n
N_TABLE = _at

G_MIX_PRE, G_MIX_POST, G_FFN_PRE, G_FFN_POST, G_MIX2, G_FFN2, G_FINAL = 0, 2, 4, 6, 8, 9, 10


class Own:

    def __init__(self, eng, sem, i=None, per=0, base=0):
        self.eng, self.sem, self.n, self.i, self.per = eng, sem, base, i, per

    def __call__(self, ins):
        self.n += 1
        ins.then_inc(self.sem, 1)
        self.eng.wait_ge(self.sem, self.n if self.i is None else self.i * self.per + self.n)

    def end(self):
        assert self.i is None or self.n == self.per, (self.n, self.per)


def build(nc, weights, small, tables, masks, w3, decay, subkeys, x, out):
    ctx = ExitStack()
    sems = {}

    def S(stage, what):
        name = f"{stage}_{what}"
        if name not in sems:
            sems[name] = ctx.enter_context(nc.semaphore(name))
        return sems[name]

    def sb(name, shape, dt=F32):
        return ctx.enter_context(nc.sbuf_tensor(name, shape, dt))

    ring = sb("ring", [P, RING, 2 * D])
    xT = sb("xT", [P, KC, T])
    hT = sb("hT", [P, KC, T])
    sm = sb("small_sb", [P, N_SMALL])
    ones = sb("ones", [P, P])
    zeros = sb("zeros", [1, 5 * P], BF16)
    eyeiota = sb("eyeiota", [P, 2 * P])
    root = sb("root", [P, T])
    rinv = sb("rinv", [P, T])
    gated = sb("gated", [P, 3, T])
    act_in = sb("act_in", [P, 3, T])
    sq = sb("sq", [P, KC, T])
    picks = sb("picks", [P, 3, T])
    hots = sb("hots", [P, 2, 2, 4, P])
    work = sb("work", [P, NKEYS * T])
    ps = ctx.enter_context(nc.psum_tensor("ps", [P, 8, 512], F32))

    pos = [0]

    def carve(*dims, dt=None):
        n = int(np.prod(dims))
        v = work[:, pos[0]:pos[0] + n]
        pos[0] += n
        if dt is not None:
            v = v.bitcast(dt)
        if len(dims) == 2:
            v = v.rearrange("p (a b) -> p a b", b=dims[1])
        if len(dims) == 3:
            v = v.rearrange("p (a b c) -> p a b c", b=dims[1], c=dims[2])
        if len(dims) == 4:
            v = v.rearrange("p (a b c d) -> p a b c d", b=dims[1], c=dims[2], d=dims[3])
        return v

    tab = carve(N_TABLE)
    level_masks = carve(LEVELS, P, dt=I32)
    filt_sum = carve(2, D)
    filt_dif = carve(2, D)
    sub = carve(16, P)
    era = pos[0]

    def small_(name, p=P):
        a, n = SMALL[name]
        return sm[0:p, a:a + n]

    def table(name, p=P):
        a, n = TABLE[name]
        return tab[0:p, a:a + n]

    eye, iota = eyeiota[:, 0:P], eyeiota[:, P:2 * P]

    def gain(g, c):
        a = SMALL["gains"][0] + g * KC + c
        return sm[:, a:a + 1]

    def strided(v, offset, dims, p0=0, np_=P):
        base = v[p0:p0 + np_]
        return bass.AP(base.tensor, base.offset + offset, [list(base.ap[0])] + [list(d) for d in dims])

    Y = ps[:, 0:4, :].rearrange("p a (b t) -> p (a b) t", t=T)
    YB = ps[:, 4:8, :].rearrange("p a (b t) -> p (a b) t", t=T)

    landed = [S("ring", f"landed{s}") for s in range(RING)]
    ring_used = S("ring", "used")

    def block_here(pe, b, i=None, n=0):
        v = 16 * (b // RING + 1)
        pe.wait_ge(landed[b % RING], v if i is None else i * (16 * n // RING) + v)

    def slab(b, half):
        return ring[:, b % RING, half * D:(half + 1) * D]

    def project(pe, dst, s, src, i=None, n=0, h_ready=None, hv=None):
        b, half = s // 2, s % 2
        if half == 0:
            block_here(pe, b, i, n)
        w = slab(b, half)
        for k in range(KC):
            if h_ready is not None:
                pe.wait_ge(h_ready, k + 1)
            mm = pe.matmul(dst, w[:, k * P:(k + 1) * P], src[:, k, :], start=(k == 0), stop=(k == KC - 1))
            if half == 0 and k == 0:
                mm.then_inc(ring_used, 1)
        return mm

    def project_rows(pe, dst, s, src, i=None, n=0):
        b, half = s // 2, s % 2
        if half == 0:
            block_here(pe, b, i, n)
        w = slab(b, half)
        for tt in range(TT):
            for k in range(KC):
                mm = pe.matmul(dst[:, tt, :], src[:, k, tt * P:(tt + 1) * P], w[:, k * P:(k + 1) * P],
                               start=(k == 0), stop=(k == KC - 1))
                if half == 0 and tt == 0 and k == 0:
                    mm.then_inc(ring_used, 1)
        return mm

    def out_project(pe, s0, src, dst, sem):
        for j in range(KC):
            project(pe, dst[:, j, :], s0 + j, src).then_inc(sem, 1)

    NORMS = ("n0", "p0", "n1", "p1", "n2", "p2", "n3", "p3", "n4", "n5", "n6")

    def nth(st, kind=""):
        return sum(x.startswith(kind) for x in NORMS[:NORMS.index(st)])

    def own_steps(st):
        return nth(st, "n") + nth(st, "p") * (KC + 1)

    def wait_h(eng, st, k=KC):
        eng.wait_ge(S("norm", "h"), KC * nth(st, "n") + k)

    def norm_scalar(act, st, src, ready, value, n=KC, bank=7):
        act.wait_ge(ready, value)
        act.activation(sq[:, 0:n, :], src, ACT.Square).then_inc(S("norm", "squares"), 1)
        act.wait_ge(S("norm", "sums"), nth(st) + 1)
        act.activation(root[:, :], ps[:, bank, 0:T], ACT.Sqrt, scale=1.0 / D, bias=eps_col).then_inc(S("norm", "root"), 1)

    def norm_tensor(pe, st, bank=7):
        pe.wait_ge(S("norm", "squares"), nth(st) + 1)
        for k in range(KC):
            mm = pe.matmul(ps[:, bank, 0:T], ones[:, :], sq[:, k, :], start=(k == 0), stop=(k == KC - 1))
        mm.then_inc(S("norm", "sums"), 1)

    def pre_norm_vector(v, st, g):
        own = Own(v, S("norm", "own"), base=own_steps(st))
        v.wait_ge(S("norm", "root"), nth(st) + 1)
        own(v.reciprocal(rinv[:, :], root[:, :]))
        for c in range(KC):
            v.scalar_tensor_tensor(hT[:, c, :], xT[:, c, :], gain(g, c), rinv[:, :], ALU.mult,
                                   ALU.mult).then_inc(S("norm", "h"), 1)

    def post_norm_vector(v, st, g):
        own = Own(v, S("norm", "own"), base=own_steps(st))
        v.wait_ge(S("norm", "root"), nth(st) + 1)
        own(v.reciprocal(rinv[:, :], root[:, :]))
        for c in range(KC):
            own(v.scalar_tensor_tensor(sq[:, c, :], Y[:, c, :], gain(g, c), rinv[:, :], ALU.mult, ALU.mult))
        v.tensor_tensor(xT[:, :, :], xT[:, :, :], sq[:, :, :], ALU.add).then_inc(S("norm", "x"), 1)

    def ffn_tensor(pe, layer, pre, s0):
        wait_h(pe, pre, 1)
        for y in range(4):
            pe.matmul(ps[:, y, :], zeros[0:1, 0:P], zeros[0:1, P:5 * P], start=True, stop=False, skip_group_check=True)
        wait_h(pe, pre)
        with pe.Fori(0, FC // 2) as i:
            for u in range(2):
                project(pe, ps[:, 4 + u, 0:T], s0 + 2 * u, hT, i, 3)
                project(pe, ps[:, 4 + u, T:2 * T], s0 + 2 * u + 1, hT, i, 3).then_inc(S("ffn", "gate_up"), 1)
            for u in range(2):
                b = s0 // 2 + 2
                if u == 0:
                    block_here(pe, b, i, 3)
                pe.wait_ge(S("ffn", "act"), i * 2 + (layer * FC + u + 1))
                w = slab(b, u)
                for j in range(KC):
                    mm = pe.matmul(Y[:, j, :], w[:, j * P:(j + 1) * P], gated[:, u, :], start=False, stop=False,
                                   skip_group_check=True)
                    if u == 0 and j == 0:
                        mm.then_inc(ring_used, 1)
        for y in range(4):
            mm = pe.matmul(ps[:, y, :], zeros[0:1, 0:P], zeros[0:1, P:5 * P], start=False, stop=True,
                           skip_group_check=True)
        mm.then_inc(S("ffn", "y"), 1)

    def ffn_scalar(act, layer):
        with act.Fori(0, FC // 2) as i:
            for u in range(2):
                act.wait_ge(S("ffn", "gate_up"), i * 2 + (layer * FC + u + 1))
                act.activation(act_in[:, u, :], ps[:, 4 + u, 0:T], ACT.Silu).then_inc(S("ffn", "silu"), 1)

    def ffn_vector(v, layer):
        with v.Fori(0, FC // 2) as i:
            for u in range(2):
                v.wait_ge(S("ffn", "silu"), i * 2 + (layer * FC + u + 1))
                v.tensor_tensor(gated[:, u, :], ps[:, 4 + u, T:2 * T], act_in[:, u, :],
                                ALU.mult).then_inc(S("ffn", "act"), 1)

    SEGS = ((1, 0, T), (0, T, P))
    pos[0] = era
    attnT = carve(KC, T)
    qk_raw, qk_turn, qk_tmp = carve(2, T), carve(2, T), carve(2, T)
    vrows = carve(TT, P)
    sc_sb, pr = carve(2, 2, 384), carve(2, 2, 384)
    prT = carve(2, 2, 384)
    top, ntop, total, scale_ = carve(8), carve(8), carve(8), carve(8)
    logit, labs, lexp, lln, lf, csum = (carve(T) for _ in range(6))
    gates = carve(TT, 24)
    shared = pos[0]
    bias_q, bias_k = carve(8, T), carve(8, T)
    pos[0] = shared
    nraw, nrope = carve(4, 2 * T), carve(4, 2 * T)
    vcomp_raw = carve(2, T)
    nv = carve(4, P)
    Xk, Xv = carve(16, 2, NC), carve(16, 2, NC)
    hid, hidT = carve(2, T), carve(4, 32)
    kcT, vcmp = carve(16), carve(HD)
    cs, cp = carve(4, 16), carve(TT, 2, 32)
    ctop, csumc, cscale = carve(4), carve(4), carve(4)
    pcT = carve(T)
    att_end = pos[0]
    causal = table("causal").unsqueeze(1).to_broadcast([P, 2, 384])
    cos2 = table("cos").rearrange("p (a t) -> p a t", a=2)
    sin2 = table("sin").rearrange("p (a t) -> p a t", a=2)

    def scores_tensor(pe, q, k, bank0, bias=None):
        for hh in range(2):
            h_ = slice(HD * hh, HD * hh + HD)
            for tt, c0, keys in SEGS:
                dst = ps[:, bank0 + hh, c0:c0 + keys]
                mm = pe.matmul(dst, q[h_, tt * P:(tt + 1) * P], k[h_, 0:keys], start=True, stop=bias is None)
                if bias is not None:
                    head = bias * 2 + hh
                    mm = pe.matmul(dst, bias_q[0:16, head, tt * P:(tt + 1) * P], bias_k[0:16, head, 0:keys],
                                   start=False, stop=True)
        return mm

    def turn_probs_tensor(pe, br, bank0):
        for hh in range(2):
            for c_out, c_in in ((0, T), (P, 0), (T, P)):
                mm = pe.transpose(ps[:, bank0 + hh, c_out:c_out + P], pr[:, br, hh, c_in:c_in + P], eye)
        return mm

    def values_tensor(pe, br, v0, v1, first, last):
        for hh in range(2):
            h_ = slice(HD * hh, HD * hh + HD)
            pe.matmul(ps[h_, 7, 0:T], v0[:, h_], prT[:, br, hh, 0:T], start=first, stop=False)
            mm = pe.matmul(ps[h_, 7, P:T], v1[:, h_], prT[:, br, hh, T:T + P], start=False, stop=last)
        return mm

    BEFORE = {"fox": 0, "moba": 4}

    def pair_tensor(pe, st, s0, i, u, last, rope):
        n = i * 2 + u
        m = i * 2 + (u + BEFORE[st])
        if rope:
            pe.wait_ge(S("pair", "qk_sb"), m + 1)
            pe.matmul(ps[:, 2, :], table("rot"), qk_raw[:, :, :].rearrange("p a t -> p (a t)"), start=True,
                      stop=True).then_inc(S(st, "turned"), 1)
        project_rows(pe, ps[:, 1, 0:T].rearrange("p (a c) -> p a c", a=TT), s0 + 3 * u + 2, hT, i,
                     3).then_inc(S("pair", "v"), 1)
        pe.wait_ge(S(st, "qk_turn") if rope else S("pair", "qk_sb"), (n if rope else m) + 1)
        scores_tensor(pe, qk_turn[:, 0, :], qk_turn[:, 1, :], 3, None if rope else n).then_inc(S("pair", "scores"), 1)
        if not last:
            query_key_tensor(pe, st, s0 + 3 * (u + 1), i)
        pe.wait_ge(S("pair", "probs"), m + 1)
        turn_probs_tensor(pe, 0, 5).then_inc(S("pair", "probsT"), 1)
        pe.wait_ge(S("pair", "v_sb"), m + 1)
        pe.wait_ge(S("pair", "probsT_sb"), m + 1)
        values_tensor(pe, 0, vrows[:, 0, :], vrows[:, 1, :], True, True).then_inc(S("pair", "o"), 1)

    def query_key_tensor(pe, st, s, i):
        project(pe, ps[:, 0, 0:T], s, hT, i, 3)
        project(pe, ps[:, 0, T:2 * T], s + 1, hT, i, 3).then_inc(S("pair", "qk"), 1)

    def query_key_scalar(act, st, n, rope):
        m = n + BEFORE[st]
        act.wait_ge(S("pair", "qk"), m + 1)
        if rope:
            act.activation(qk_raw[:, :, :].rearrange("p a t -> p (a t)"), ps[:, 0, :], ACT.Copy).then_inc(S("pair", "qk_sb"), 1)
        else:
            act.activation(qk_turn[:, 0, :], ps[:, 0, 0:T], ACT.Copy, scale=HD ** -0.5)
            act.activation(qk_turn[:, 1, :], ps[:, 0, T:2 * T], ACT.Copy).then_inc(S("pair", "qk_sb"), 1)

    def exps_scalar(act, br):
        for hh in range(2):
            for g, (tt, c0, keys) in enumerate(SEGS):
                m = (br * 2 + hh) * 2 + g
                ins = act.activation(pr[:, br, hh, c0:c0 + keys], sc_sb[:, br, hh, c0:c0 + keys], ACT.Exp,
                                     bias=ntop[:, m:m + 1], accum_out=total[:, m:m + 1])
        return ins

    def pair_scalar(act, st, i, u, last, rope, chunk0):
        n = i * 2 + u
        m = i * 2 + (u + BEFORE[st])
        act.wait_ge(S("pair", "v"), m + 1)
        act.activation(vrows[:, :, :].rearrange("p a c -> p (a c)"), ps[:, 1, 0:T], ACT.Copy).then_inc(S("pair", "v_sb"), 1)
        act.wait_ge(S("pair", "tops"), m + 1)
        exps_scalar(act, 0).then_inc(S("pair", "exps"), 1)
        if not last:
            query_key_scalar(act, st, n + 1, rope)
        act.wait_ge(S("pair", "o"), m + 1)
        act.activation(attnT[:, bass.ds(n + chunk0, 1), :].rearrange("p a t -> p (a t)"), ps[:, 7, 0:T],
                       ACT.Copy).then_inc(S("pair", "o_sb"), 1)

    def tops_vector(v, own, br, bank0):
        own(v.tensor_tensor(sc_sb[:, br, :, :], ps[:, bank0:bank0 + 2, 0:384], causal, ALU.add))
        m = 4 * br
        for g, (tt, c0, keys) in enumerate(SEGS):
            ins = v.tensor_reduce(top[:, m + g:m + 4:2], sc_sb[:, br, :, c0:c0 + keys], AX_X, ALU.max)
            own(ins)
        return v.tensor_scalar(ntop[:, m:m + 4], top[:, m:m + 4], -1.0, None, ALU.mult)

    def scale_probs_vector(v, br):
        for hh in range(2):
            for g, (tt, c0, keys) in enumerate(SEGS):
                m = (br * 2 + hh) * 2 + g
                p_ = pr[:, br, hh, c0:c0 + keys]
                ins = v.tensor_scalar(p_, p_, scale_[:, m:m + 1], None, ALU.mult)
        return ins

    def pair_vector(v, st, own, i, u, rope):
        n = i * 2 + u
        m = i * 2 + (u + BEFORE[st])
        if rope:
            v.wait_ge(S(st, "turned"), n + 1)
            own(v.tensor_tensor(qk_turn[:, :, :], qk_raw[:, :, :], cos2, ALU.mult))
            own(v.tensor_tensor(qk_tmp[:, :, :], ps[:, 2, :].rearrange("p (a t) -> p a t", a=2), sin2, ALU.mult))
            v.tensor_tensor(qk_turn[:, :, :], qk_turn[:, :, :], qk_tmp[:, :, :], ALU.add).then_inc(S(st, "qk_turn"), 1)
        v.wait_ge(S("pair", "scores"), m + 1)
        tops_vector(v, own, 0, 3).then_inc(S("pair", "tops"), 1)
        v.wait_ge(S("pair", "exps"), m + 1)
        own(v.reciprocal(scale_[:, 0:4], total[:, 0:4]))
        scale_probs_vector(v, 0).then_inc(S("pair", "probs"), 1)
        v.wait_ge(S("pair", "probsT"), m + 1)
        v.tensor_copy(prT[:, 0, :, :], ps[:, 5:7, 0:384]).then_inc(S("pair", "probsT_sb"), 1)

    def fox_tensor(pe, st, pre, s0):
        pe.wait_ge(S("load", "small"), 16)
        for k in range(KC):
            wait_h(pe, pre, k + 1)
            mm = pe.matmul(ps[0:16, 6, 0:T], small_("wfg")[:, k * 40:k * 40 + 16], hT[:, k, :], start=(k == 0), stop=(k == KC - 1))
        for g, tt in enumerate((1, 0)):
            for k in range(KC):
                mm = pe.matmul(ps[:, 6, T + 32 * g:T + 32 * g + 24], hT[:, k, tt * P:(tt + 1) * P],
                               small_("wfg")[:, k * 40 + 16:k * 40 + 40], start=(k == 0), stop=(k == KC - 1))
        mm.then_inc(S(st, "logits"), 1)
        query_key_tensor(pe, st, s0, 0)
        pe.wait_ge(S(st, "biases"), 1)
        for i in range(2):
            for u in range(2):
                pair_tensor(pe, st, s0, i, u, i == 1 and u == 1, False)

    def fox_scalar(act, st):
        act.wait_ge(S(st, "logits"), 1)
        act.activation(logit[0:16, :], ps[0:16, 6, 0:T], ACT.Identity, bias=small_("bf", 16)).then_inc(S(st, "logit_sb"), 1)
        act.activation(gates[:, :, :], ps[:, 6, T:T + 64].rearrange("p (a c) -> p a c", a=2)[:, :, 0:24], ACT.Sigmoid)
        act.activation(labs[0:16, :], ps[0:16, 6, 0:T], ACT.Abs, bias=small_("bf", 16)).then_inc(S(st, "labs"), 1)
        act.wait_ge(S(st, "labs"), 1)
        act.activation(lexp[0:16, :], labs[0:16, :], ACT.Exp, scale=-1.0).then_inc(S(st, "lexp"), 1)
        act.wait_ge(S(st, "lexp1"), 1)
        act.activation(lln[0:16, :], lexp[0:16, :], ACT.Ln).then_inc(S(st, "lln"), 1)
        query_key_scalar(act, st, 0, False)
        for i in range(2):
            for u in range(2):
                pair_scalar(act, st, i, u, i == 1 and u == 1, False, 0)

    def fox_vector(v, st):
        own = Own(v, S(st, "own"))
        v.wait_ge(S(st, "logit_sb"), 1)
        v.wait_ge(S(st, "lexp"), 1)
        v.tensor_scalar(lexp[0:16, :], lexp[0:16, :], 1.0, None, ALU.add).then_inc(S(st, "lexp1"), 1)
        own(v.tensor_scalar(logit[0:16, :], logit[0:16, :], 0.0, None, ALU.min))
        v.wait_ge(S(st, "lln"), 1)
        own(v.tensor_tensor(lf[0:16, :], logit[0:16, :], lln[0:16, :], ALU.subtract))
        own(v.memset(labs[0:16, :], 1.0))
        own(v.tensor_tensor_scan(csum[0:16, :], labs[0:16, :], lf[0:16, :], 0.0, ALU.mult, ALU.add))
        for h in range(8):
            v.tensor_scalar(bias_q[0:16, h, :], csum[0:16, :], table("cmask", 16)[:, 0:1], table("ebot", 16)[:, h:h + 1],
                            ALU.mult, ALU.add)
            ins = v.tensor_scalar(bias_k[0:16, h, :], csum[0:16, :], table("cmask", 16)[:, 1:2],
                                  table("etop", 16)[:, h:h + 1], ALU.mult, ALU.add)
        ins.then_inc(S(st, "biases"), 1)
        for i in range(2):
            for u in range(2):
                pair_vector(v, st, own, i, u, False)

    def moba_tensor(pe, st, pre, s0):
        wait_h(pe, pre)
        query_key_tensor(pe, st, s0, 0)
        with pe.Fori(0, 3) as i:
            for u in range(2):
                pair_tensor(pe, st, s0, i, u, False, True)
        for u in range(2):
            pair_tensor(pe, st, s0, 3, u, u == 1, True)

    def moba_scalar(act, st):
        query_key_scalar(act, st, 0, True)
        with act.Fori(0, 3) as i:
            for u in range(2):
                pair_scalar(act, st, i, u, False, True, 0)
        for u in range(2):
            pair_scalar(act, st, 3, u, u == 1, True, 0)

    def moba_vector(v, st):
        def turn(i):
            own = Own(v, S(st, "own"), i, 12)
            for u in range(2):
                pair_vector(v, st, own, i, u, True)
            own.end()
        with v.Fori(0, 3) as i:
            turn(i)
        turn(3)

    RAW = (0, "v", 1, 2, 3)

    def nsa_tensor(pe, st, s0):
        def two(bank, s, row):
            project(pe, ps[:, bank, 0:T], s, hT)
            project(pe, ps[:, bank, T:2 * T], s + 1, hT).then_inc(S(st, "raw"), 1)

        def turn(row, bank):
            pe.wait_ge(S(st, "raw_sb"), RAW.index(row) + 1)
            pe.matmul(ps[:, bank, :], table("rot"), nraw[:, row, :], start=True, stop=True).then_inc(S(st, "turned"), 1)

        pe.wait_ge(S("pair", "o_sb"), 4)
        two(0, s0, 0)
        two(1, s0 + 2, "v")
        two(2, s0 + 4, 1)
        turn(0, 6)
        project_rows(pe, ps[:, 3, 0:T].rearrange("p (a c) -> p a c", a=TT), s0 + 6, hT)
        project_rows(pe, ps[:, 3, T:2 * T].rearrange("p (a c) -> p a c", a=TT), s0 + 7, hT).then_inc(S(st, "nv"), 1)
        turn(1, 7)
        two(4, s0 + 8, 2)
        pe.wait_ge(S(st, "rope"), 2)
        two(5, s0 + 10, 3)
        turn(2, 6)
        turn(3, 7)
        for kv, X in ((0, Xk), (1, Xv)):
            pe.wait_ge(S(st, "X"), kv + 1)
            for j in range(16):
                s = s0 + 12 + 4 * kv + j // 4
                b, half = s // 2, s % 2
                if half == 0 and j % 4 == 0:
                    block_here(pe, b)
                w = slab(b, half)[:, (j % 4) * T:(j % 4 + 1) * T]
                mm = pe.matmul(ps[0:2 * NC, kv, 0:T], X[:, j, :, :].rearrange("p g c -> p (g c)"), w,
                               start=(j == 0), stop=(j == 15))
                if half == 0 and j % 4 == 0:
                    mm.then_inc(ring_used, 1)
            mm.then_inc(S(st, "hidden"), 1)
        for kv in range(2):
            pe.wait_ge(S(st, "gelu"), kv + 1)
            for kt in range(2):
                c = (kv * 2 + kt) * 32
                mm = pe.transpose(ps[:, 2, c:c + 2 * NC], hid[0:2 * NC, kv, kt * P:(kt + 1) * P], eye[0:2 * NC, 0:2 * NC])
        mm.then_inc(S(st, "hiddenT"), 1)
        pe.wait_ge(S(st, "hiddenT_sb"), 1)
        for g in range(2):
            for kt in range(2):
                pe.matmul(ps[HD * g:HD * g + HD, 3, 0:NC], small_("w2k")[:, kt * HD:(kt + 1) * HD],
                          hidT[:, kt, g * NC:(g + 1) * NC], start=(kt == 0), stop=(kt == 1))
        for g in range(2):
            for kt in range(2):
                mm = pe.matmul(ps[32 * g:32 * g + NC, 3, HD:2 * HD], hidT[:, 2 + kt, g * NC:(g + 1) * NC],
                               small_("w2v")[:, kt * HD:(kt + 1) * HD], start=(kt == 0), stop=(kt == 1))
        mm.then_inc(S(st, "comp"), 1)
        pe.wait_ge(S(st, "comp_sb"), 1)
        pe.wait_ge(S(st, "rope"), 4)
        for j in range(4):
            q = nrope[:, 2 + j // 2, (j % 2) * T:(j % 2 + 1) * T]
            for hh in range(2):
                h_ = slice(HD * hh, HD * hh + HD)
                for g, tt in enumerate((1, 0)):
                    mm = pe.matmul(ps[:, hh, 16 * g:16 * g + NC], q[h_, tt * P:(tt + 1) * P], kcT[h_, 0:NC], start=True, stop=True)
            mm.then_inc(S(st, "cscores"), 1)
            scores_tensor(pe, q, nrope[:, 1, 0:T], 3).then_inc(S(st, "scores"), 1)
            scores_tensor(pe, q, nrope[:, 1, T:2 * T], 5).then_inc(S(st, "scores"), 1)
            pe.wait_ge(S(st, "cprobs"), j + 1)
            for g, tt in enumerate((1, 0)):
                mm = pe.transpose(ps[0:HD, 0, T + tt * P:T + (tt + 1) * P], cp[:, g, :, :].rearrange("p h c -> p (h c)"), eye)
            mm.then_inc(S(st, "cprobsT"), 1)
            for br in range(2):
                pe.wait_ge(S(st, "probs"), 2 * j + br + 1)
                turn_probs_tensor(pe, br, 1 + 2 * br).then_inc(S(st, "probsT"), 1)
            for br in range(2):
                pe.wait_ge(S(st, "probsT_sb"), 2 * j + br + 1)
                if br == 0 and j > 0:
                    pe.wait_ge(S(st, "o_sb"), j)
                values_tensor(pe, br, nv[:, 2 * br, :], nv[:, 2 * br + 1, :], br == 0, False)
            pe.wait_ge(S(st, "cprobsT_sb"), j + 1)
            for hh in range(2):
                mm = pe.matmul(ps[HD * hh:HD * hh + HD, 7, 0:T], vcmp[32 * hh:32 * hh + NC, :],
                               pcT[32 * hh:32 * hh + NC, :], start=False, stop=True)
            mm.then_inc(S(st, "o"), 1)

    def nsa_scalar(act, st):
        def take(row, bank, dst):
            act.wait_ge(S(st, "raw"), RAW.index(row) + 1)
            act.activation(dst, ps[:, bank, :], ACT.Copy).then_inc(S(st, "raw_sb"), 1)

        take(0, 0, nraw[:, 0, :])
        take("v", 1, vcomp_raw[:, :, :].rearrange("p a t -> p (a t)"))
        take(1, 2, nraw[:, 1, :])
        act.wait_ge(S(st, "nv"), 1)
        act.activation(nv[:, :, :].rearrange("p a c -> p (a c)"), ps[:, 3, :], ACT.Copy)
        take(2, 4, nraw[:, 2, :])
        take(3, 5, nraw[:, 3, :])
        for kv in range(2):
            act.wait_ge(S(st, "hidden"), kv + 1)
            act.activation(hid[0:2 * NC, kv, :], ps[0:2 * NC, kv, 0:T], ACT.Gelu_apprx_tanh).then_inc(S(st, "gelu"), 1)
        act.wait_ge(S(st, "comp"), 1)
        act.activation(kcT[:, 0:NC], ps[:, 3, 0:NC], ACT.Copy)
        act.activation(vcmp[0:NC, :], ps[0:NC, 3, HD:2 * HD], ACT.Copy)
        act.activation(vcmp[32:32 + NC, :], ps[32:32 + NC, 3, HD:2 * HD], ACT.Copy).then_inc(S(st, "comp_sb"), 1)
        for j in range(4):
            act.wait_ge(S(st, "ctops"), j + 1)
            act.activation(cs[:, :, 0:NC], cs[:, :, 0:NC], ACT.Exp).then_inc(S(st, "cexps"), 1)
            for br in range(2):
                act.wait_ge(S(st, "tops"), 2 * j + br + 1)
                exps_scalar(act, br).then_inc(S(st, "exps"), 1)
            act.wait_ge(S(st, "cprobsT"), j + 1)
            act.activation(pcT[0:HD, :], ps[0:HD, 0, T:2 * T], ACT.Copy).then_inc(S(st, "cprobsT_sb"), 1)
            act.wait_ge(S(st, "o"), j + 1)
            act.activation(attnT[:, 4 + j, :], ps[:, 7, 0:T], ACT.Copy).then_inc(S(st, "o_sb"), 1)

    def nsa_vector(v, st):
        own = Own(v, S(st, "own"))
        own(v.memset(cp[:, :, :, :], 0.0))

        def rope(row, bank, half):
            v.wait_ge(S(st, "turned"), row + 1)
            co = cos2[:, half:half + 1, :].to_broadcast([P, 2, T])
            si = sin2[:, half:half + 1, :].to_broadcast([P, 2, T])
            y = nrope[:, row, :].rearrange("p (a t) -> p a t", a=2)
            own(v.tensor_tensor(y, nraw[:, row, :].rearrange("p (a t) -> p a t", a=2), co, ALU.mult))
            own(v.tensor_tensor(qk_tmp[:, :, :], ps[:, bank, :].rearrange("p (a t) -> p a t", a=2), si, ALU.mult))
            ins = v.tensor_tensor(y, y, qk_tmp[:, :, :], ALU.add)
            ins.then_inc(S(st, "rope"), 1)
            v.wait_ge(S(st, "rope"), row + 1)

        def unfold(X, src, pe_name):
            for half in range(2):
                for jh in range(2):
                    h_ = slice(HD * half, HD * half + HD)
                    for jj in range(0, 8):
                        j = 8 * jh + jj
                        a = SMALL[pe_name][0] + j
                        ins = v.tensor_scalar(X[h_, j, :, :], strided(src, 2 * j + half, [[T, 2], [16, NC]], HD * half, HD),
                                              sm[h_, a:a + 1], None, ALU.add)
            return ins

        rope(0, 6, 1)
        unfold(Xk, nrope[:, 0, :], "pek").then_inc(S(st, "X"), 1)
        v.wait_ge(S(st, "raw_sb"), RAW.index("v") + 1)
        unfold(Xv, vcomp_raw[:, :, :].rearrange("p a t -> p (a t)"), "pev").then_inc(S(st, "X"), 1)
        rope(1, 7, 1)
        rope(2, 6, 0)
        rope(3, 7, 0)
        v.wait_ge(S(st, "hiddenT"), 1)
        v.tensor_copy(hidT[:, :, 0:2 * NC], ps[:, 2, 0:P].rearrange("p (a c) -> p a c", a=4)[:, :, 0:2 * NC]).then_inc(S(st, "hiddenT_sb"), 1)
        for j in range(4):
            v.wait_ge(S(st, "cscores"), j + 1)
            add_ = table("cmpadd").rearrange("p (a c) -> p a c", a=4)[:, :, 0:NC]
            mul_ = table("cmpmul").rearrange("p (a c) -> p a c", a=4)[:, :, 0:NC]
            c4 = cs[:, :, 0:NC]
            own(v.tensor_tensor(c4.rearrange("p (g h) c -> p g h c", g=2),
                                ps[:, 0:2, 0:32].rearrange("p h (g c) -> p g h c", g=2)[:, :, :, 0:NC],
                                add_.rearrange("p (g h) c -> p g h c", g=2), ALU.add))
            own(v.tensor_reduce(ctop[:, :], c4, AX_X, ALU.max))
            v.tensor_tensor(c4, c4, ctop[:, :].unsqueeze(2).to_broadcast([P, 4, NC]), ALU.subtract).then_inc(S(st, "ctops"), 1)
            for br in range(2):
                v.wait_ge(S(st, "scores"), 2 * j + br + 1)
                tops_vector(v, own, br, 3 + 2 * br).then_inc(S(st, "tops"), 1)
            v.wait_ge(S(st, "cexps"), j + 1)
            own(v.tensor_tensor(c4, c4, mul_, ALU.mult))
            own(v.tensor_reduce(csumc[:, :], c4, AX_X, ALU.add))
            own(v.tensor_scalar(csumc[:, :], csumc[:, :], 1e-30, None, ALU.max))
            own(v.reciprocal(cscale[:, :], csumc[:, :]))
            own(v.tensor_tensor(cscale[:, :].rearrange("p (g h) -> p g h", g=2), cscale[:, :].rearrange("p (g h) -> p g h", g=2),
                                gates[:, :, 2 * j:2 * j + 2], ALU.mult))
            v.tensor_tensor(cp[:, :, :, 0:NC], cs[:, :, 0:NC].rearrange("p (g h) c -> p g h c", g=2),
                            cscale[:, :].rearrange("p (g h) -> p g h", g=2).unsqueeze(3).to_broadcast([P, 2, 2, NC]),
                            ALU.mult).then_inc(S(st, "cprobs"), 1)
            for br in range(2):
                v.wait_ge(S(st, "exps"), 2 * j + br + 1)
                m = scale_[:, 4 * br:4 * br + 4]
                own(v.reciprocal(m, total[:, 4 * br:4 * br + 4]))
                c = 8 * (br + 1) + 2 * j
                own(v.tensor_tensor(m.rearrange("p (h g) -> p g h", g=2), m.rearrange("p (h g) -> p g h", g=2),
                                    gates[:, :, c:c + 2], ALU.mult))
                scale_probs_vector(v, br).then_inc(S(st, "probs"), 1)
            for br in range(2):
                v.wait_ge(S(st, "probsT"), 2 * j + br + 1)
                v.tensor_copy(prT[:, br, :, :], ps[:, 1 + 2 * br:3 + 2 * br, 0:384]).then_inc(S(st, "probsT_sb"), 1)
    pos[0] = era
    w3_sb = carve(2 * D)
    decay_sb = carve(2 * D)
    farg, fk, fred, fhid = carve(T), carve(T), carve(T), carve(T)
    fwin, ftap = carve(2, 512), carve(2, 512)
    MAGIC = 12582912.0
    TAU1 = 6.28125
    TAU2 = float(np.float32(np.round((2 * np.pi - TAU1) * 2 ** 20) / 2 ** 20))
    TAU3 = float(np.float32(2 * np.pi - TAU1 - TAU2))

    def filters_tensor(pe, st):
        pe.wait_ge(S("load", "small"), 16)
        pe.wait_ge(S("load", "tables"), 16)
        pe.matmul(ps[0:64, 0, 0:T], small_("fw1", 33), table("zT", 33), start=True, stop=True).then_inc(S(st, "pre"), 1)
        pe.wait_ge(S(st, "hid"), 1)
        pe.matmul(ps[0:64, 1, 0:T], small_("fw2", 64), fhid[0:64, :], start=True, stop=True).then_inc(S(st, "pre"), 1)
        pe.wait_ge(S(st, "hid"), 2)
        pe.wait_ge(S("load", "w3"), 16)
        pe.wait_ge(S(st, "decay"), 1)
        for n in range(4):
            pt, half = n // 2, n % 2
            if n > 0:
                pe.wait_ge(S(st, "taps"), n)
            for d in range(2):
                c = d * D + half * 512
                pe.matmul(ps[:, 2 + d, :], fhid[0:64, pt * P:(pt + 1) * P], w3_sb[0:64, c:c + 512], start=True, stop=True)
                mm = pe.matmul(ps[:, 4 + d, :], table("taprow", 1)[:, pt * P:(pt + 1) * P], decay_sb[0:1, c:c + 512],
                               start=True, stop=True)
            mm.then_inc(S(st, "filt"), 1)

    def filters_scalar(act, st):
        for n in range(2):
            act.wait_ge(S(st, "reduced"), n + 1)
            act.activation(fhid[0:64, :], fred[0:64, :], ACT.Sin).then_inc(S(st, "hid"), 1)
        act.wait_ge(S("load", "decay"), 16)
        act.activation(decay_sb[0:1, :], decay_sb[0:1, :], ACT.Abs).then_inc(S(st, "decay"), 1)
        for n in range(4):
            act.wait_ge(S(st, "filt"), n + 1)
            act.activation(fwin[:, :, :], ps[:, 4:6, :], ACT.Exp, scale=-1.0).then_inc(S(st, "window"), 1)

    def filters_vector(v, st):
        own = Own(v, S(st, "own"))
        for n in range(2):
            v.wait_ge(S(st, "pre"), n + 1)
            fv = small_("fvec", 64)
            own(v.tensor_scalar(farg[0:64, :], ps[0:64, n, 0:T], fv[:, 2 * n:2 * n + 1], fv[:, 2 * n + 1:2 * n + 2],
                                ALU.add, ALU.mult))
            own(v.tensor_scalar(fk[0:64, :], farg[0:64, :], 1 / (2 * np.pi), MAGIC, ALU.mult, ALU.add))
            own(v.tensor_scalar(fk[0:64, :], fk[0:64, :], -MAGIC, None, ALU.add))
            for tau in (TAU1, TAU2, TAU3):
                own(v.scalar_tensor_tensor(farg[0:64, :], fk[0:64, :], -tau, farg[0:64, :], ALU.mult, ALU.add))
            v.tensor_scalar(fred[0:64, :], farg[0:64, :], 3.1415925, -3.1415925, ALU.min,
                            ALU.max).then_inc(S(st, "reduced"), 1)
        for n in range(4):
            pt, half = n // 2, n % 2
            v.wait_ge(S(st, "window"), n + 1)
            own(v.tensor_tensor(ftap[:, 0, :], ps[:, 2, :], fwin[:, 0, :], ALU.mult))
            own(v.scalar_tensor_tensor(ftap[:, 1, :], ps[:, 3, :], table("tapmask")[:, pt:pt + 1], fwin[:, 1, :], ALU.mult, ALU.mult))
            own(v.tensor_tensor(filt_sum[:, pt, half * 512:(half + 1) * 512], ftap[:, 0, :], ftap[:, 1, :], ALU.add))
            v.tensor_tensor(filt_dif[:, pt, half * 512:(half + 1) * 512], ftap[:, 0, :], ftap[:, 1, :],
                            ALU.subtract).then_inc(S(st, "taps"), 1)

    pos[0] = era
    oall, silu_og, gate_a, gate_b, yb, merged = (carve(HH, T) for _ in range(6))
    sig_q, sig_og, qh, ksum = (carve(T) for _ in range(4))
    sig_f, sig_n = carve(2, T), carve(2, T)
    forget = carve(3, T)
    qa, kb = carve(2, T), carve(2, T)
    totals = [forget.rearrange("p a t -> p (a t)")] + [carve(3 * (T >> l)) for l in range(1, LEVELS)]
    kmix = carve(T)
    sT = carve(TT, T)
    hv = carve(TT, P)
    lbd, lbe, lbs, lb, oml = carve(2, HH), carve(2, HH), carve(HH), carve(HH), carve(HH)
    diag = strided(sT, 0, [[T + P, 2], [1, P]])

    def halves(v, h, off, n):
        return strided(v, off, [[2 * h, n], [T + h, 2], [1, h]])

    def mix_keys(v, h):
        n = T // (2 * h)
        return v.tensor_copy(strided(kmix, 0, [[2 * h, n], [h, 2], [1, h]]), halves(kb, h, 0, n))

    def hgrn_slab(pe, st, s, k, i):
        if k == 3:
            return project_rows(pe, ps[:, 1, T:2 * T].rearrange("p (a c) -> p a c", a=TT), s + 3, hT, i, 3).then_inc(S(st, "in1"), 1)
        mm = project(pe, ps[:, k // 2, (k % 2) * T:(k % 2 + 1) * T], s + k, hT, i, 3)
        if k in (1, 5):
            mm.then_inc(S(st, f"in{k // 2}"), 1)

    def hgrn_head_tensor(pe, st, s0, i, last):
        pe.wait_ge(S(st, "prep"), i + 1)
        pe.wait_ge(S(st, "staged"), i + 1)
        for k in range(LEVELS + 2):
            dst = ps[:, 3 + 2 * (k % 2), 0:T].rearrange("p (a c) -> p a c", a=2)
            if k >= 2:
                pe.wait_ge(S(st, "grown"), i * LEVELS + (k - 1))
            for a in range(2):
                if k == 0:
                    mm = pe.matmul(dst[:, a, :], ksum[:, a * P:(a + 1) * P], qh[:, a * P:(a + 1) * P], start=True, stop=True)
                elif k <= LEVELS:
                    h = 1 << (k - 1)
                    mm = pe.matmul(dst[:, a, :], kmix[:, a * P:(a + 1) * P], halves(qa, h, a * P, P // (2 * h)),
                                   start=True, stop=True)
                else:
                    mm = pe.matmul(dst[:, a, :], kb[:, a, a * P:(a + 1) * P], qa[:, 1 - a, (1 - a) * P:(2 - a) * P],
                                   start=True, stop=True)
            mm.then_inc(S(st, "level"), 1)
            if not last and 1 <= k <= 6:
                if k == 3:
                    pe.wait_ge(S(st, "v_sb"), i + 1)
                hgrn_slab(pe, st, s0 + 6, k - 1, i)
        pe.wait_ge(S(st, "scores"), i + 1)
        pe.wait_ge(S(st, "v_sb"), i + 1)
        for a in range(TT):
            mm = pe.matmul(ps[:, 4, 0:T], hv[:, a, :], sT[:, a, :], start=(a == 0), stop=(a == 1))
        mm.then_inc(S(st, "o"), 1)

    def hgrn_tensor(pe, st, pre, s0):
        wait_h(pe, pre)
        for k in range(6):
            hgrn_slab(pe, st, s0, k, None)
        with pe.Fori(0, HH - 1) as i:
            hgrn_head_tensor(pe, st, s0, i, False)
        hgrn_head_tensor(pe, st, s0, HH - 1, True)

    def hgrn_stage_scalar(act, st, n):
        act.wait_ge(S(st, "in0"), n + 1)
        act.activation(sig_q[:, :], ps[:, 0, 0:T], ACT.Sigmoid)
        act.activation(sig_f[:, 1, :], ps[:, 0, T:2 * T], ACT.Sigmoid)
        act.activation(sig_n[:, 0, :], ps[:, 0, T:2 * T], ACT.Sigmoid, scale=-1.0)
        act.wait_ge(S(st, "in1"), n + 1)
        act.activation(sig_f[:, 0, :], ps[:, 1, 0:T], ACT.Sigmoid)
        act.activation(sig_n[:, 1, :], ps[:, 1, 0:T], ACT.Sigmoid, scale=-1.0)
        act.wait_ge(S(st, "in2"), n + 1)
        act.activation(sig_og[:, :], ps[:, 2, 0:T], ACT.Sigmoid)
        act.activation(gate_a[:, bass.ds(n, 1), :].rearrange("p a t -> p (a t)"), ps[:, 2, T:2 * T],
                       ACT.Sigmoid).then_inc(S(st, "staged"), 1)

    def hgrn_value_scalar(act, st):
        act.activation(hv[:, :, :].rearrange("p a c -> p (a c)"), ps[:, 1, T:2 * T], ACT.Copy).then_inc(S(st, "v_sb"), 1)

    def hgrn_out_scalar(act, st, n):
        act.wait_ge(S(st, "o"), n + 1)
        act.activation(oall[:, bass.ds(n, 1), :].rearrange("p a t -> p (a t)"), ps[:, 4, 0:T], ACT.Copy).then_inc(S(st, "o_sb"), 1)

    def hgrn_scalar(act, st):
        act.wait_ge(S(st, "lbd"), 1)
        act.activation(lbe[:, :, :], lbd[:, :, :], ACT.Exp).then_inc(S(st, "lbe"), 1)
        hgrn_stage_scalar(act, st, 0)
        hgrn_value_scalar(act, st)
        with act.Fori(0, HH - 1) as i:
            hgrn_stage_scalar(act, st, i + 1)
            hgrn_out_scalar(act, st, i)
            hgrn_value_scalar(act, st)
        hgrn_out_scalar(act, st, HH - 1)

    def hgrn_head_vector(v, st, i):
        own = Own(v, S(st, "own"), i, 3 + LEVELS)
        v.wait_ge(S(st, "staged"), i + 1)
        l_, m_ = lb[:, bass.ds(i, 1)], oml[:, bass.ds(i, 1)]
        v.tensor_tensor(qh[:, :], ps[:, 0, 0:T], sig_q[:, :], ALU.mult)
        v.tensor_scalar(forget[:, 0:2, :], sig_f[:, :, :], m_, l_, ALU.mult, ALU.add)
        v.tensor_scalar(forget[:, 2, :], sig_f[:, 0, :], m_, l_, ALU.mult, ALU.add)
        own(v.tensor_scalar(kb[:, :, :], sig_n[:, :, :], m_, None, ALU.mult))
        own(v.tensor_tensor(silu_og[:, bass.ds(i, 1), :].rearrange("p a t -> p (a t)"), ps[:, 2, 0:T], sig_og[:, :], ALU.mult))
        mix_keys(v, 1)
        own(v.tensor_tensor(ksum[:, :], kb[:, 0, :], kb[:, 1, :], ALU.add))
        v.tensor_tensor(qa[:, :, :], forget[:, 0:2, :], qh[:, :].unsqueeze(1).to_broadcast([P, 2, T]),
                        ALU.mult).then_inc(S(st, "prep"), 1)
        v.wait_ge(S(st, "level"), i * (LEVELS + 2) + 1)
        own(v.tensor_tensor(diag, ps[:, 3, 0:T].rearrange("p (a c) -> p a c", a=2), eye.unsqueeze(1).to_broadcast([P, 2, P]), ALU.mult))
        for l in range(LEVELS):
            h = 1 << l
            n, nt = T // (2 * h), T // h
            bank = 3 + 2 * ((l + 1) % 2)
            v.wait_ge(S(st, "level"), i * (LEVELS + 2) + (l + 2))
            t_ = totals[l]
            q_, k_ = (strided(x_, 0, [[T + h, 2], [2 * h, n], [1, h]]) for x_ in (qa, kb))
            v.tensor_tensor(q_, q_, strided(t_, 1, [[nt - 1, 2], [2, n], [0, h]]), ALU.mult)
            v.copy_predicated(diag, level_masks[:, l, :].unsqueeze(1).to_broadcast([P, 2, P]),
                              ps[:, bank, 0:T].rearrange("p (a c) -> p a c", a=2))
            ins = v.tensor_tensor(k_, k_, strided(t_, nt + 1, [[nt - 1, 2], [2, n], [0, h]]), ALU.mult)
            if l < LEVELS - 1:
                own(v.tensor_tensor(strided(totals[l + 1], 0, [[n, 3], [1, n]]), strided(t_, 0, [[nt, 3], [2, n]]),
                                    strided(t_, 1, [[nt, 3], [2, n]]), ALU.mult))
                ins = mix_keys(v, 2 * h)
            ins.then_inc(S(st, "grown"), 1)
        v.wait_ge(S(st, "level"), i * (LEVELS + 2) + (LEVELS + 2))
        v.tensor_copy(strided(sT, P, [[1, T]]), ps[:, 3 + 2 * ((LEVELS + 1) % 2), 0:T]).then_inc(S(st, "scores"), 1)
        own.end()

    def hgrn_vector(v, st):
        pre = Own(v, S(st, "lb"))
        l2 = small_("lbl").rearrange("p (a h) -> p a h", a=2)
        pre(v.tensor_tensor(lbs[:, :], l2[:, 0, :], l2[:, 1, :], ALU.max))
        v.tensor_tensor(lbd[:, :, :], l2, lbs[:, :].unsqueeze(1).to_broadcast([P, 2, HH]), ALU.subtract).then_inc(S(st, "lbd"), 1)
        v.wait_ge(S(st, "lbe"), 1)
        pre(v.tensor_tensor(lbs[:, :], lbe[:, 0, :], lbe[:, 1, :], ALU.add))
        pre(v.reciprocal(lbs[:, :], lbs[:, :]))
        pre(v.tensor_tensor(lb[:, :], lbe[:, 0, :], lbs[:, :], ALU.mult))
        pre(v.tensor_scalar(oml[:, :], lb[:, :], -1.0, 1.0, ALU.mult, ALU.add))
        with v.Fori(0, HH) as i:
            hgrn_head_vector(v, st, i)

    def hgrn_norm_scalar(act, st):
        act.wait_ge(S("hgrn", "o_sb"), HH)
        act.activation(sq[:, :, :], oall[:, :, :], ACT.Square).then_inc(S(st, "squares"), 1)
        act.wait_ge(S(st, "sums"), 1)
        act.activation(merged[:, :, :], YB, ACT.Sqrt, scale=1.0 / P, bias=eps_col).then_inc(S(st, "root"), 1)

    def hgrn_norm_tensor(pe, st):
        pe.wait_ge(S(st, "squares"), 1)
        for c in range(4):
            mm = pe.matmul(ps[:, 4 + c, :], ones[:, :], sq[:, 2 * c:2 * c + 2, :].rearrange("p a t -> p (a t)"), start=True, stop=True)
        mm.then_inc(S(st, "sums"), 1)

    def hgrn_norm_vector(v, st):
        own = Own(v, S(st, "own"))
        v.wait_ge(S(st, "root"), 1)
        own(v.reciprocal(merged[:, :, :], merged[:, :, :]))
        f = lambda z: z[:, :, :].rearrange("p a t -> p (a t)")
        own(v.scalar_tensor_tensor(f(oall), f(oall), small_("hg"), f(merged), ALU.mult, ALU.mult))
        v.tensor_tensor(f(oall), f(oall), f(silu_og), ALU.mult).then_inc(S(st, "o"), 1)

    pos[0] = era + 6 * HH * T
    hy = carve(3, T + 2)
    conv = carve(3, T)
    u = carve(T)
    uT = carve(TT, P)
    taps_now = carve(2, 2, P)
    kspec = carve(3, T)
    prod_a, prod_b = carve(2, T), carve(2, T)
    yspec = carve(4, P)
    yspecT = carve(4, P)
    conv_y = carve(T)
    dft = table("dft").rearrange("p (a f) -> p a f", a=2)
    idft = table("idft").rearrange("p (a f) -> p a f", a=4)

    def hyena_slab(pe, st, s, k, i):
        mm = project(pe, ps[:, k // 2, (k % 2) * T:(k % 2 + 1) * T], s + k, hT, i, 6)
        if k % 2:
            mm.then_inc(S(st, f"in{k // 2}"), 1)

    def hyena_tile_tensor(pe, st, s0, i, u_, last):
        n = i * 3 + u_
        s = s0 + 4 * (u_ + 1)
        pe.wait_ge(S(st, "u"), n + 1)
        for a in range(TT):
            mm = pe.transpose(ps[:, 2, a * P:(a + 1) * P], u[:, a * P:(a + 1) * P], eye)
        mm.then_inc(S(st, "uT"), 1)
        if not last:
            hyena_slab(pe, st, s, 0, i)
        pe.wait_ge(S(st, "uT_sb"), n + 1)
        pe.wait_ge(S(st, "taps"), n + 1)
        for a in range(TT):
            pe.matmul(ps[:, 3, :], uT[:, a, :], dft[:, a, :], start=(a == 0), stop=(a == 1))
        for part in range(2):
            for a in range(2):
                mm = pe.matmul(ps[:, 4, part * T:(part + 1) * T], taps_now[:, part, a, :], dft[:, a, part * T:(part + 1) * T],
                               start=(a == 0), stop=(a == 1))
        mm.then_inc(S(st, "spectra"), 1)
        if not last:
            hyena_slab(pe, st, s, 1, i)
            hyena_slab(pe, st, s, 2, i)
        pe.wait_ge(S(st, "yspec"), n + 1)
        for f in range(4):
            mm = pe.transpose(ps[:, 5, f * P:(f + 1) * P], yspec[:, f, :], eye)
        mm.then_inc(S(st, "yspecT"), 1)
        if not last:
            hyena_slab(pe, st, s, 3, i)
        pe.wait_ge(S(st, "yspecT_sb"), n + 1)
        for f in range(4):
            mm = pe.matmul(ps[:, 6, 0:T], yspecT[:, f, :], idft[:, f, :], start=(f == 0), stop=(f == 3))
        mm.then_inc(S(st, "conv"), 1)

    def hyena_tensor(pe, st, s0):
        pe.wait_ge(S("hgrn", "o_sb"), HH)
        for k in range(4):
            hyena_slab(pe, st, s0, k, None)
        hgrn_norm_tensor(pe, "hnorm")
        pe.wait_ge(S("hnorm", "root"), 1)
        with pe.Fori(0, 2) as i:
            for u_ in range(3):
                hyena_tile_tensor(pe, st, s0, i, u_, False)
        hyena_tile_tensor(pe, st, s0, 2, 0, False)
        hyena_tile_tensor(pe, st, s0, 2, 1, True)

    def hyena_stage_scalar(act, st, n, part):
        act.wait_ge(S(st, f"in{part}"), n + 1)
        if part == 0:
            act.activation(hy[:, 0:2, 1:T + 1], ps[:, 0, :].rearrange("p (a t) -> p a t", a=2), ACT.Copy)
        else:
            act.activation(hy[:, 2, 1:T + 1], ps[:, 1, 0:T], ACT.Copy)
            act.activation(gate_b[:, bass.ds(n, 1), :].rearrange("p a t -> p (a t)"), ps[:, 1, T:2 * T],
                           ACT.Sigmoid).then_inc(S(st, "staged"), 1)

    def hyena_scalar(act, st):
        act.wait_ge(S(st, "pads"), 1)
        hyena_stage_scalar(act, st, 0, 0)
        hyena_stage_scalar(act, st, 0, 1)
        hgrn_norm_scalar(act, "hnorm")

        def tile(n, last):
            act.wait_ge(S(st, "uT"), n + 1)
            act.activation(uT[:, :, :].rearrange("p a c -> p (a c)"), ps[:, 2, 0:T], ACT.Copy).then_inc(S(st, "uT_sb"), 1)
            act.wait_ge(S(st, "spectra"), n + 1)
            act.activation(kspec[:, 0:2, :].rearrange("p a t -> p (a t)"), ps[:, 4, :], ACT.Copy)
            act.activation(kspec[:, 2, :], ps[:, 4, 0:T], ACT.Copy).then_inc(S(st, "kspec"), 1)
            if not last:
                hyena_stage_scalar(act, st, n + 1, 0)
            act.wait_ge(S(st, "yspecT"), n + 1)
            act.activation(yspecT[:, :, :].rearrange("p a c -> p (a c)"), ps[:, 5, :], ACT.Copy).then_inc(S(st, "yspecT_sb"), 1)
            if not last:
                hyena_stage_scalar(act, st, n + 1, 1)
        with act.Fori(0, HH - 1) as n:
            tile(n, False)
        tile(HH - 1, True)

    def hyena_gpsimd(pool, st):
        pool.wait_ge(S(st, "pads"), 1)
        with pool.Fori(0, KC) as n:
            pool.tensor_copy(taps_now[:, 0, :, :], filt_sum[:, :, bass.ds(n * P, P)])
            pool.tensor_copy(taps_now[:, 1, :, :], filt_dif[:, :, bass.ds(n * P, P)]).then_inc(S(st, "taps"), 1)
            pool.wait_ge(S(st, "spectra"), n + 1)

    def hyena_pads_vector(v, st):
        v.memset(hy[:, :, :], 0.0).then_inc(S(st, "pads"), 1)

    def hyena_vector(v, st):
        with v.Fori(0, KC) as n:
            own = Own(v, S(st, "own"), n, 6)
            v.wait_ge(S(st, "staged"), n + 1)

            def w(q, j):
                return sm[:, bass.ds(n * 3 + (SMALL["convw"][0] + q * 24 + j), 1)]
            for q in range(3):
                b_ = sm[:, bass.ds(n + (SMALL["convb"][0] + q * KC), 1)]
                ins = v.tensor_scalar(conv[:, q, :], hy[:, q, 1:T + 1], w(q, 1), b_, ALU.mult, ALU.add)
            own(ins)
            for q in range(3):
                ins = v.scalar_tensor_tensor(conv[:, q, :], hy[:, q, 0:T], w(q, 0), conv[:, q, :], ALU.mult, ALU.add)
            own(ins)
            for q in range(3):
                ins = v.scalar_tensor_tensor(conv[:, q, :], hy[:, q, 2:T + 2], w(q, 2), conv[:, q, :], ALU.mult, ALU.add)
            own(ins)
            v.tensor_tensor(u[:, :], conv[:, 2, :], conv[:, 1, :], ALU.mult).then_inc(S(st, "u"), 1)
            v.wait_ge(S(st, "kspec"), n + 1)
            uspec = ps[:, 3, :].rearrange("p (a t) -> p a t", a=2)
            v.tensor_tensor(prod_a[:, :, :], uspec, kspec[:, 0:2, :], ALU.mult)
            own(v.tensor_tensor(prod_b[:, :, :], uspec, kspec[:, 1:3, :], ALU.mult))
            f = yspec[:, :, :].rearrange("p a c -> p (a c)")
            v.tensor_tensor(f[:, 0:T], prod_a[:, 0, :], prod_a[:, 1, :], ALU.subtract)
            v.tensor_tensor(f[:, T:2 * T], prod_b[:, 0, :], prod_b[:, 1, :], ALU.add).then_inc(S(st, "yspec"), 1)
            v.wait_ge(S(st, "conv"), n + 1)
            own(v.scalar_tensor_tensor(conv_y[:, :], u[:, :], sm[:, bass.ds(n + SMALL["hbias"][0], 1)], ps[:, 6, 0:T],
                                       ALU.mult, ALU.add))
            own(v.tensor_tensor(yb[:, bass.ds(n, 1), :].rearrange("p a t -> p (a t)"), conv_y[:, :], conv[:, 0, :], ALU.mult))
            own.end()

    def merge_tensor(pe, st, sa, sbb, so):
        pe.wait_ge(S("hnorm", "o"), 1)
        out_project(pe, sa, oall, Y, S(st, "ya"))
        pe.wait_ge(S("hyena", "own"), KC * 6)
        out_project(pe, sbb, yb, YB, S(st, "yb"))
        pe.wait_ge(S(st, "merged"), KC)
        out_project(pe, so, merged, Y, S(st, "y"))

    def merge_vector(v, st):
        own = Own(v, S(st, "own"))
        for j in range(0, KC, 2):
            v.wait_ge(S(st, "ya"), j + 2)
            own(v.tensor_tensor(merged[:, j:j + 2, :], gate_a[:, j:j + 2, :], Y[:, j:j + 2, :], ALU.mult))
        for j in range(0, KC, 2):
            v.wait_ge(S(st, "yb"), j + 2)
            own(v.tensor_tensor(prod_a[:, :, :], gate_b[:, j:j + 2, :], YB[:, j:j + 2, :], ALU.mult))
            v.tensor_tensor(merged[:, j:j + 2, :], merged[:, j:j + 2, :], prod_a[:, :, :], ALU.add).then_inc(S(st, "merged"), 2)
            v.wait_ge(S(st, "merged"), j + 2)
        v.wait_ge(S(st, "y"), KC)
        v.tensor_tensor(xT[:, :, :], xT[:, :, :], Y, ALU.add).then_inc(S(st, "x"), 1)
    pos[0] = era
    s_all = carve(TT, 16, NKEYS)
    s_left = carve(NKEYS)
    best = carve(TT, 16, TOPK)
    best_at = carve(TT, 16, TOPK, dt=U32)
    best_key = carve(TT, 16, TOPK)
    cand = carve(TT, 8, TOPK * TOPK)
    c_left = carve(TOPK * TOPK)
    pick_s = carve(TT, 8, TOPK)
    pick_at = carve(TT, 8, TOPK, dt=U32)
    rank_u = carve(2, TT * 8 * TOPK, dt=U32)
    rank = carve(2, TT * 8 * TOPK)
    match = carve(TT * 8 * TOPK, TOPK)
    pick = carve(3, TT, 8 * TOPK)
    psum_ = carve(TT * 8)
    qsb = carve(2, T)
    assert pos[0] <= NKEYS * T
    peer_w = work[:, :].rearrange("p (n t) -> p n t", t=T)

    def pq_tensor(pe, st, pre, s0):
        wait_h(pe, pre)
        pe.wait_ge(S("load", "sub"), 16)

        def query(i, u):
            project(pe, ps[:, 4 + u % 2, 0:T], s0 + u, hT, i, 3).then_inc(S(st, "q"), 1)

        def score(i, u):
            pe.wait_ge(S(st, "q_sb"), i * 6 + (u + 1))
            for tt in range(TT):
                mm = pe.matmul(ps[:, 6 + u % 2, tt * P:(tt + 1) * P], qsb[:, u % 2, tt * P:(tt + 1) * P],
                               sub[:, bass.ds(i * 6 + u, 1), :].rearrange("p a k -> p (a k)"), start=True, stop=True)
            mm.then_inc(S(st, "s"), 1)

        def turn(i, n):
            query(i, 0)
            for u in range(1, n):
                query(i, u)
                score(i, u - 1)
            score(i, n - 1)
        with pe.Fori(0, 2) as i:
            turn(i, 6)
        turn(2, 4)

    def pq_scalar(act, st):
        def query(i, u):
            act.wait_ge(S(st, "q"), i * 6 + (u + 1))
            act.activation(qsb[:, u % 2, :], ps[:, 4 + u % 2, 0:T], ACT.Copy).then_inc(S(st, "q_sb"), 1)

        def score(i, u):
            act.wait_ge(S(st, "s"), i * 6 + (u + 1))
            act.activation(s_all[:, :, bass.ds(i * 6 + u, 1), :].rearrange("p t a k -> p t (a k)"),
                           ps[:, 6 + u % 2, 0:T].rearrange("p (t k) -> p t k", t=TT), ACT.Copy).then_inc(S(st, "s_sb"), 1)

        def turn(i, n):
            query(i, 0)
            for u in range(1, n):
                query(i, u)
                score(i, u - 1)
            score(i, n - 1)
        with act.Fori(0, 2) as i:
            turn(i, 6)
        turn(2, 4)

    def best16(v, own, values, left, out_v, out_at):
        own(v.max(out=out_v[:, 0:8], in_=values))
        own(v.max_index(out=out_at[:, 0:8], in_max=out_v[:, 0:8], in_values=values))
        own(v.match_replace(out=left, in_to_replace=out_v[:, 0:8], in_values=values, imm_value=-3e38))
        own(v.max(out=out_v[:, 8:16], in_=left))
        own(v.max_index(out=out_at[:, 8:16], in_max=out_v[:, 8:16], in_values=left))

    def picks_vector(v, st):
        own = Own(v, S(st, "own"))
        for hp in range(16):
            v.wait_ge(S("pq", "s_sb"), hp + 1)
            for tt in range(TT):
                best16(v, own, s_all[:, tt, hp, :], s_left[:, :], best[:, tt, hp, :], best_at[:, tt, hp, :])
        own(v.tensor_copy(best_key[:, :, :, :], best_at[:, :, :, :]))
        for tt in range(TT):
            own(v.tensor_tensor(cand[:, tt, :, :].rearrange("p h (a b) -> p h a b", b=TOPK),
                                strided(best, tt * 256, [[32, 8], [1, 16], [0, 16]]),
                                strided(best, tt * 256 + 16, [[32, 8], [0, 16], [1, 16]]), ALU.add))
        for tt in range(TT):
            for h in range(8):
                best16(v, own, cand[:, tt, h, :], c_left[:, :], pick_s[:, tt, h, :], pick_at[:, tt, h, :])
        at = pick_at[:, :, :, :].rearrange("p t h k -> p (t h k)")
        own(v.tensor_scalar(rank_u[:, 0, :], at, 4, None, ALU.logical_shift_right))
        own(v.tensor_scalar(rank_u[:, 1, :], at, 15, None, ALU.bitwise_and))
        own(v.tensor_copy(rank[:, :, :], rank_u[:, :, :]))
        n = TT * 8 * TOPK
        for half in range(2):
            own(v.tensor_tensor(match[:, :, :], strided(rank, half * n, [[1, n], [0, TOPK]]), strided(iota, 0, [[0, n], [1, TOPK]]),
                                ALU.is_equal))
            m4 = strided(match, 0, [[256, 16], [16, 16], [1, 16]])
            own(v.tensor_tensor(m4, m4, strided(best_key, 16 * half, [[32, 16], [0, 16], [1, 16]]), ALU.mult))
            own(v.tensor_reduce(pick[:, half, :, :].rearrange("p t k -> p (t k)"), match[:, :, :], AX_X, ALU.add))
        w4 = pick[:, 2, :, :].rearrange("p t (h k) -> p (t h) k", k=TOPK)
        s4 = pick_s[:, :, :, :].rearrange("p t h k -> p (t h) k")
        v.tensor_tensor(w4, s4, s4[:, :, 0:1].to_broadcast([P, 16, TOPK]), ALU.subtract).then_inc(S(st, "shifted"), 1)
        v.wait_ge(S(st, "exp"), 1)
        own(v.tensor_reduce(psum_[:, :], w4, AX_X, ALU.add))
        own(v.reciprocal(psum_[:, :], psum_[:, :]))
        v.tensor_tensor(w4, w4, psum_[:, :].unsqueeze(2).to_broadcast([P, 16, TOPK]), ALU.mult).then_inc(S(st, "picks"), 1)
        v.wait_ge(S(st, "picksT"), 1)
        v.tensor_copy(picks[:, 0:2, :].rearrange("p a t -> p (a t)"), ps[:, 4, :])
        v.tensor_copy(picks[:, 2, :], ps[:, 5, 0:T]).then_inc(S(st, "picksT_sb"), 1)
        v.wait_ge(S(st, "picksT_sb"), 1)

    def picks_scalar(act, st):
        act.wait_ge(S(st, "shifted"), 1)
        w_ = pick[:, 2, :, :].rearrange("p t k -> p (t k)")
        act.activation(w_, w_, ACT.Exp).then_inc(S(st, "exp"), 1)

    def picks_tensor(pe, st):
        pe.wait_ge(S(st, "picks"), 1)
        for a in range(3):
            for tt in range(TT):
                mm = pe.transpose(ps[:, 4 + a // 2, (a % 2) * T + tt * P:(a % 2) * T + (tt + 1) * P], pick[:, a, tt, :], eye)
        mm.then_inc(S(st, "picksT"), 1)

    BATCHES = T // 4

    def spread(eng, step):
        for u in range(2):
            step(0, u, True)
        with eng.Fori(1, BATCHES // 2) as i:
            for u in range(2):
                step(i, u, False)

    def spread_vector(v, st):
        def step(i, u, first):
            if not first:
                v.wait_ge(S(st, "weights"), i * 2 + (u - 1))
            for k in range(4):
                t = i * 8 + (u * 4 + k)
                v.tensor_scalar(hots[:, u, 1, k, :], iota, picks[:, 1, bass.ds(t, 1)], None, ALU.is_equal)
                ins = v.tensor_scalar(hots[:, u, 0, k, :], iota, picks[:, 0, bass.ds(t, 1)], picks[:, 2, bass.ds(t, 1)],
                                      ALU.is_equal, ALU.mult)
            ins.then_inc(S(st, "hot"), 1)
        spread(v, step)

    def spread_tensor(pe, st):
        def step(i, u, first):
            pe.wait_ge(S(st, "hot"), i * 2 + (u + 1))
            if not first:
                pe.wait_ge(S(st, "weights_sb"), i * 2 + (u - 1))
            for k in range(4):
                mm = pe.matmul(ps[:, 6 + u, k * P:(k + 1) * P], hots[:, u, 1, k, :], hots[:, u, 0, k, :], start=True, stop=True)
            mm.then_inc(S(st, "weights"), 1)
        spread(pe, step)

    def spread_scalar(act, st):
        def step(i, u, first):
            act.wait_ge(S(st, "weights"), i * 2 + (u + 1))
            act.activation(peer_w[:, :, bass.ds(i * 8 + u * 4, 4)], ps[:, 6 + u, :].rearrange("p (k n) -> p n k", k=4),
                           ACT.Copy).then_inc(S(st, "weights_sb"), 1)
        spread(act, step)

    def peer_tensor(pe, st, s0):
        def hidden(s, i, slot):
            project(pe, ps[:, 4 + slot, 0:T], s, hT, i, 3).then_inc(S(st, "hidden"), 1)

        def output(s, i, slot, value):
            b, half = s // 2, s % 2
            if half == 0:
                block_here(pe, b, i, 3)
            pe.wait_ge(S(st, "act"), value)
            w = slab(b, half)
            for j in range(KC):
                mm = pe.matmul(Y[:, j, :], w[:, j * P:(j + 1) * P], gated[:, slot, :], start=False, stop=False,
                               skip_group_check=True)
                if half == 0 and j == 0:
                    mm.then_inc(ring_used, 1)

        for y in range(4):
            pe.matmul(ps[:, y, :], zeros[0:1, 0:P], zeros[0:1, P:5 * P], start=True, stop=False, skip_group_check=True)
        pe.wait_ge(S("spread", "weights_sb"), BATCHES)
        hidden(s0, None, 0)
        hidden(s0 + 1, None, 1)
        with pe.Fori(0, (NKEYS - 2) // 3) as i:
            for u in range(3):
                output(s0 + 2 + 2 * u, i, u, i * 3 + (u + 1))
                hidden(s0 + 3 + 2 * u, i, (u + 2) % 3)
        output(s0 + 2 * NKEYS - 2, None, 0, NKEYS - 1)
        output(s0 + 2 * NKEYS - 1, None, 1, NKEYS)
        for y in range(4):
            mm = pe.matmul(ps[:, y, :], zeros[0:1, 0:P], zeros[0:1, P:5 * P], start=False, stop=True, skip_group_check=True)
        mm.then_inc(S(st, "y"), 1)

    def peer_chunks(eng, step):
        with eng.Fori(0, (NKEYS - 2) // 3) as i:
            for u in range(3):
                step(i, u)
        for u in range(2):
            step((NKEYS - 2) // 3, u)

    def peer_scalar(act, st):
        def step(i, u):
            act.wait_ge(S(st, "hidden"), i * 3 + (u + 1))
            act.activation(act_in[:, u, :], ps[:, 4 + u, 0:T], ACT.Gelu_apprx_tanh).then_inc(S(st, "gelu"), 1)
        peer_chunks(act, step)

    def peer_vector(v, st):
        def step(i, u):
            v.wait_ge(S(st, "gelu"), i * 3 + (u + 1))
            v.tensor_tensor(gated[:, u, :], act_in[:, u, :], peer_w[:, bass.ds(i * 3 + u, 1), :].rearrange("p a t -> p (a t)"),
                            ALU.mult).then_inc(S(st, "act"), 1)
        peer_chunks(v, step)
        v.wait_ge(S(st, "y"), 1)
        v.tensor_tensor(xT[:, :, :], xT[:, :, :], Y, ALU.add).then_inc(S(st, "x"), 1)
    eps_tile = sb("eps_tile", [P, 1])
    eps_col = eps_tile[:, 0:1]
    block = ctx.enter_context(nc.Block())
    B0 = {k: 2 * v for k, v in START.items()}

    @block.sync
    def _(sp):
        def load(dst, src, name):
            sp.dma_start(dst, src).then_inc(S("load", name), 16)

        def load_block(b, src):
            sp.dma_start(ring[:, b % RING, :], src).then_inc(landed[b % RING], 16)

        load(tab, tables, "tables")
        load(sm[:, :], small, "small")
        load(xT[:, :, :], x, "x")
        load(w3_sb[0:64, :], w3, "w3")
        load(decay_sb[0:1, :], decay, "decay")
        for b in range(RING):
            load_block(b, weights[b])
        load(level_masks, masks, "masks")
        load(sub, subkeys, "sub")
        with sp.Fori(1, N_BLOCKS // RING) as i:
            for s in range(RING):
                sp.wait_ge(ring_used, i * RING + (s - 1))
                load_block(s, weights[bass.ds(i * RING + s, 1)].rearrange("a p n -> (a p) n"))
        for b in range(N_BLOCKS // RING * RING, N_BLOCKS):
            sp.wait_ge(ring_used, b - 1)
            load_block(b, weights[b])
        wait_h(sp, "n6")
        sp.dma_start(out, hT[:, :, :]).then_inc(S("store", "out"), 16)
        sp.wait_ge(S("store", "out"), 16)

    @block.tensor
    def _(pe):
        pe.wait_ge(S("load", "eye"), 1)
        filters_tensor(pe, "filters")
        norm_tensor(pe, "n0")
        fox_tensor(pe, "fox", "n0", B0["fox"])
        nsa_tensor(pe, "nsa", B0["nsa"])
        pe.wait_ge(S("nsa", "o_sb"), 4)
        out_project(pe, B0["out0"], attnT, Y, S("out", "y"))
        norm_tensor(pe, "p0")
        norm_tensor(pe, "n1")
        ffn_tensor(pe, 0, "n1", B0["ffn0"])
        norm_tensor(pe, "p1")
        norm_tensor(pe, "n2")
        moba_tensor(pe, "moba", "n2", B0["moba"])
        pe.wait_ge(S("pair", "o_sb"), 4 + 8)
        out_project(pe, B0["out1"], attnT, Y, S("out", "y"))
        norm_tensor(pe, "p2")
        norm_tensor(pe, "n3")
        ffn_tensor(pe, 1, "n3", B0["ffn1"])
        norm_tensor(pe, "p3")
        norm_tensor(pe, "n4")
        hgrn_tensor(pe, "hgrn", "n4", B0["hgrn"])
        hyena_tensor(pe, "hyena", B0["hyena"])
        merge_tensor(pe, "merge", B0["wa"], B0["wb"], B0["out2"])
        norm_tensor(pe, "n5")
        pq_tensor(pe, "pq", "n5", B0["pq"])
        picks_tensor(pe, "picks")
        spread_tensor(pe, "spread")
        peer_tensor(pe, "peer", B0["peer"])
        norm_tensor(pe, "n6")

    @block.scalar
    def _(act):
        filters_scalar(act, "filters")
        norm_scalar(act, "n0", xT[:, :, :], S("load", "x"), 16)
        fox_scalar(act, "fox")
        nsa_scalar(act, "nsa")
        norm_scalar(act, "p0", Y, S("out", "y"), KC)
        norm_scalar(act, "n1", xT[:, :, :], S("norm", "x"), 1)
        ffn_scalar(act, 0)
        norm_scalar(act, "p1", Y, S("ffn", "y"), 1)
        norm_scalar(act, "n2", xT[:, :, :], S("norm", "x"), 2)
        moba_scalar(act, "moba")
        norm_scalar(act, "p2", Y, S("out", "y"), 2 * KC)
        norm_scalar(act, "n3", xT[:, :, :], S("norm", "x"), 3)
        ffn_scalar(act, 1)
        norm_scalar(act, "p3", Y, S("ffn", "y"), 2)
        norm_scalar(act, "n4", xT[:, :, :], S("norm", "x"), 4)
        hgrn_scalar(act, "hgrn")
        hyena_scalar(act, "hyena")
        norm_scalar(act, "n5", xT[:, :, :], S("merge", "x"), 1)
        pq_scalar(act, "pq")
        picks_scalar(act, "picks")
        spread_scalar(act, "spread")
        peer_scalar(act, "peer")
        norm_scalar(act, "n6", xT[:, :, :], S("peer", "x"), 1)

    @block.vector
    def _(v):
        v.memset(ones[:, :], 1.0)
        v.memset(zeros[:, :], 0.0)
        v.memset(eps_tile[:, :], EPS)
        v.wait_ge(S("load", "tables"), 16)
        v.wait_ge(S("load", "small"), 16)
        v.tensor_copy(eyeiota[:, :], tab[:, 0:2 * P]).then_inc(S("load", "eye"), 1)
        v.wait_ge(S("load", "eye"), 1)
        filters_vector(v, "filters")
        pre_norm_vector(v, "n0", G_MIX_PRE)
        fox_vector(v, "fox")
        nsa_vector(v, "nsa")
        post_norm_vector(v, "p0", G_MIX_POST)
        pre_norm_vector(v, "n1", G_FFN_PRE)
        ffn_vector(v, 0)
        post_norm_vector(v, "p1", G_FFN_POST)
        pre_norm_vector(v, "n2", G_MIX_PRE + 1)
        moba_vector(v, "moba")
        post_norm_vector(v, "p2", G_MIX_POST + 1)
        pre_norm_vector(v, "n3", G_FFN_PRE + 1)
        ffn_vector(v, 1)
        post_norm_vector(v, "p3", G_FFN_POST + 1)
        pre_norm_vector(v, "n4", G_MIX2)
        v.wait_ge(S("load", "masks"), 16)
        hgrn_vector(v, "hgrn")
        hyena_pads_vector(v, "hyena")
        hgrn_norm_vector(v, "hnorm")
        hyena_vector(v, "hyena")
        merge_vector(v, "merge")
        pre_norm_vector(v, "n5", G_FFN2)
        picks_vector(v, "picks")
        spread_vector(v, "spread")
        peer_vector(v, "peer")
        pre_norm_vector(v, "n6", G_FINAL)

    @block.gpsimd
    def _(pool):
        hyena_gpsimd(pool, "hyena")

    ctx.close()



def shape_tables():
    t = {}
    pp = np.arange(P)
    t["eye"] = np.eye(P)
    t["iota"] = np.tile(np.arange(P), (P, 1))
    inv = (np.float32(10000.0) ** (-np.arange(0, HD, 2, dtype=np.float32) / np.float32(HD))).astype(np.float32)
    ang = np.arange(T, dtype=np.float32)[:, None] * inv[None, :]
    cos, sin = np.cos(ang.astype(np.float64)).T, np.sin(ang.astype(np.float64)).T
    c4, s4 = np.tile(cos, (4, 1)), np.tile(sin, (4, 1))
    q = HD ** -0.5
    t["cos"] = np.concatenate([c4 * q, c4], 1)
    t["sin"] = np.concatenate([s4 * q, s4], 1)
    rot = np.zeros((P, P))
    for h in range(2):
        for d in range(32):
            rot[h * 64 + 32 + d, h * 64 + d] = -1.0
            rot[h * 64 + d, h * 64 + 32 + d] = 1.0
    t["rot"] = rot
    causal = np.zeros((P, 384))
    causal[:, 0:T] = np.where(np.arange(T)[None] <= P + pp[:, None], 0, NEG)
    causal[:, T:] = np.where(pp[None] <= pp[:, None], 0, NEG)
    t["causal"] = causal
    add, mul = np.zeros((P, 4, 16)), np.zeros((P, 4, 16))
    for g, tt in enumerate((1, 0)):
        ok = (np.arange(NC)[None] * 16 + 31) <= (tt * P + pp[:, None])
        for hh in range(2):
            add[:, g * 2 + hh, :NC] = np.where(ok, 0, NEG)
            mul[:, g * 2 + hh, :NC] = ok
    t["cmpadd"], t["cmpmul"] = add.reshape(P, -1), mul.reshape(P, -1)
    th = 2 * np.pi * ((np.arange(T)[:, None] * np.arange(T)[None, :]) % NFFT) / NFFT
    f = np.concatenate([np.cos(th), -np.sin(th)], 1)
    t["dft"] = f.reshape(2, P, 2 * T).transpose(1, 0, 2).reshape(P, -1)
    wgt = np.where(np.arange(T) == 0, 1.0, 2.0)[:, None] / NFFT
    g = np.concatenate([np.cos(th) * wgt, -np.sin(th) * wgt], 0)
    t["idft"] = g.reshape(4, P, T).transpose(1, 0, 2).reshape(P, -1)
    posn = np.arange(T, dtype=np.float32)
    tpos = posn / np.float32(T - 1)
    bands = np.linspace(1e-4, 15, 16, dtype=np.float32)
    a2 = (np.float32(2.0 * np.pi / T) * posn)[:, None] * bands[None, :]
    z = np.concatenate([tpos[:, None], np.cos(a2), -np.sin(a2)], 1)
    t["zT"] = np.pad(z.T, ((0, P - 33), (0, 0)))
    t["taprow"] = np.pad(tpos[None], ((0, P - 1), (0, 0)))
    cm = np.zeros((P, 2))
    cm[0:8, 0], cm[8:16, 1] = 1, -1
    t["cmask"] = cm
    eb, et = np.zeros((P, 8)), np.zeros((P, 8))
    for h in range(8):
        eb[8 + h, h], et[h, h] = 1, 1
    t["ebot"], t["etop"] = eb, et
    tm = np.ones((P, 2))
    tm[0, 0] = 0
    t["tapmask"] = tm
    out = np.zeros((P, N_TABLE), np.float32)
    for k, (a, n) in TABLE.items():
        out[:, a:a + n] = t[k]
    s, c = np.meshgrid(pp, pp, indexing="ij")
    m = [((s >> (l + 1)) == (c >> (l + 1))) & ((s >> l) != (c >> l)) for l in range(LEVELS)]
    return out, np.stack(m, 1).astype(np.int32)


def pack(a):
    f = lambda k: np.asarray(a[k])
    parts = []

    def cols(w):
        m = w.shape[1] // P
        parts.append(w.reshape(KC, P, m, P).transpose(2, 1, 0, 3).reshape(m, P, D))

    def rows(w):
        parts.append(w.reshape(-1, P, D))

    win = f("ev_w_in")[0]
    e = 0
    o = {}
    for name, n in (("fq", 512), ("fk", 512), ("fv", 512), ("f", 8), ("nq", 512), ("kc", 128), ("vc", 128), ("ks", 128),
                    ("vs", 128), ("kw", 128), ("vw", 128), ("g", 24)):
        o[name] = win[:, e:e + n]
        e += n
    for p in range(4):
        for name in ("fq", "fk", "fv"):
            cols(o[name][:, p * P:(p + 1) * P])
    pairs = np.concatenate([np.r_[j * HD:(j + 1) * HD, (j + 4) * HD:(j + 5) * HD] for j in range(4)])
    for name in ("kc", "vc"):
        for g in range(2):
            cols(np.concatenate([o[name][:, g * HD:(g + 1) * HD]] * 2, 1))
    for name in ("ks", "kw", "vs", "vw"):
        cols(o[name])
    cols(o["nq"][:, pairs])
    for name in ("ev_cmp_w1_k", "ev_cmp_w1_v"):
        parts.append(f(name)[0].reshape(4, 4, P, T).transpose(0, 2, 1, 3).reshape(4, P, D))
    cols(f("ev_w_out")[0][np.concatenate([np.arange(512), 512 + pairs])])

    def ffn(layer):
        g, u, dn = f("ffn_w_gate")[layer], f("ffn_w_up")[layer], f("ffn_w_down")[layer]
        for c in range(0, FC, 2):
            for cc in (c, c + 1):
                cols(g[:, cc * P:(cc + 1) * P])
                cols(u[:, cc * P:(cc + 1) * P])
            rows(dn[c * P:(c + 2) * P])

    ffn(0)
    wo = f("od_w_in")[0]
    for p in range(8):
        for n in range(3):
            cols(wo[:, n * D + p * P:n * D + (p + 1) * P])
    cols(f("od_w_out")[0])
    ffn(1)
    w = f("w_in_2")[0]
    seg = lambda n, j: w[:, n * D + j * P:n * D + (j + 1) * P]
    for h in range(HH):
        for n in (0, 1, 2, 3, 4, 8):
            cols(seg(n, h))
    for j in range(KC):
        for n in (5, 6, 7, 9):
            cols(seg(n, j))
    for name in ("w_branch_a_2", "w_branch_b_2", "w_out_2"):
        cols(f(name)[0])
    cols(f("peer_w_q_2")[0])
    u = f("peer_u_2")[0].reshape(NKEYS, P, KC, P).transpose(0, 3, 2, 1).reshape(NKEYS, P, D)
    v = f("peer_v_2")[0].reshape(NKEYS, P, D)
    both = np.stack([u[2:], v[:-2]], 1)[:, ::-1].reshape(-1, P, D)
    parts += [u[0:2], both, v[-2:]]
    weights = np.concatenate(parts).reshape(N_BLOCKS, 2, P, D).transpose(0, 2, 1, 3).reshape(N_BLOCKS, P, 2 * D)

    small = np.zeros((P, N_SMALL), np.float32)

    def put(name, v):
        a0, n = SMALL[name]
        assert v.shape[1] == n, (name, v.shape)
        small[0:v.shape[0], a0:a0 + n] = v

    gp = np.concatenate([np.stack([o["g"][:, (j + 4 * hh) * 3 + b] for j in range(4) for hh in range(2)], 1) for b in range(3)], 1)
    wfg = np.concatenate([o["f"], o["f"], gp], 1)
    put("wfg", wfg.reshape(KC, P, 40).transpose(1, 0, 2).reshape(P, -1))
    for k in "kv":
        put("w2" + k, f("ev_cmp_w2_" + k)[0].reshape(2, P, HD).transpose(1, 0, 2).reshape(P, -1))
        put("pe" + k, f("ev_cmp_pe_" + k)[0].reshape(16, 2, HD).transpose(1, 2, 0).reshape(P, 16))
    put("bf", np.tile(f("ev_b_f")[0], 2)[:, None])
    gs = np.concatenate([f("g_mix_pre"), f("g_mix_post"), f("g_ffn_pre"), f("g_ffn_post"), f("norm_mix_g_2"),
                         f("norm_ffn_g_2"), f("norm_final_g_2")[None]])
    put("gains", gs.reshape(11, KC, P).transpose(2, 0, 1).reshape(P, -1))
    put("lbl", f("hgrn_lb_logits_2").reshape(2, HH, P).transpose(2, 0, 1).reshape(P, -1))
    put("hg", f("hgrn_norm_g_2").reshape(P, 1))
    put("convw", f("hyena_conv_w_2")[0].reshape(3, 24, P).transpose(2, 1, 0).reshape(P, -1))
    put("convb", f("hyena_conv_b_2")[0].reshape(24, P).T)
    put("hbias", f("hyena_bias_2")[0].reshape(KC, P).T)
    put("fw1", f("filt_w1_2")[0])
    put("fvec", np.stack([f("filt_b1_2")[0], f("filt_freq1_2")[0], f("filt_b2_2")[0], f("filt_freq2_2")[0]], 1))
    put("fw2", f("filt_w2_2")[0])
    tables, masks = shape_tables()
    return {
        "weights": weights, "small": small, "tables": tables, "masks": masks,
        "w3": f("filt_w3_2")[0], "decay": f("filt_decay_2"),
        "subkeys": f("peer_subkeys_2")[0].transpose(3, 0, 1, 2).reshape(P, 16, NKEYS),
        "x": f("x")[0].T.reshape(KC, P, T).transpose(1, 0, 2),
    }


def kernel(**inputs):
    import concourse.bacc as _bacc
    from concourse.bass_utils import run_bass_kernel_spmd as _run

    nc = _bacc.Bacc("TRN2", target_bir_lowering=False, num_devices=1)
    arrays, args = {}, {}
    for name, a in pack(inputs).items():
        a = np.ascontiguousarray(a)
        arrays[f"in_{name}"] = a
        args[name] = nc.dram_tensor(f"in_{name}", a.shape, mybir.dt.from_np(a.dtype), kind="ExternalInput").ap()
    out = nc.dram_tensor("out_x", (P, KC, T), F32, kind="ExternalOutput").ap()
    build(nc, out=out, **args)
    r = _run(nc, [arrays], core_ids=[0])
    y = np.asarray(r.results[0]["out_x"])
    return np.ascontiguousarray(y.transpose(2, 1, 0).reshape(1, T, D))
```

```python
from contextlib import ExitStack

import numpy as np

import concourse.bass as bass
from concourse import mybir

ALU = mybir.AluOpType
ACT = mybir.ActivationFunctionType
F32 = mybir.dt.float32
F32R = mybir.dt.float32r
BF16 = mybir.dt.bfloat16
I32 = mybir.dt.int32
U32 = mybir.dt.uint32
AX_X = mybir.AxisListType.X

P = 128
D = 1024
KC = D // P
T = 256
TT = T // P
HD = 64
FF = 2816
FC = FF // P
RING = 3
TERMS = ((0, 0), (0, 1), (1, 0))
EPS = 1e-6
NEG = -1e30
NC = T // 16 - 1
NFFT = 511
HH = 8
LEVELS = 7
NKEYS = 128
TOPK = 16

N_FOX, N_NSA, N_OUT, N_FFN, N_MOBA = 4 * 3, 4 + 8 + 4 + 4, KC, 3 * FC, 8 * 3
N_HGRN, N_HYENA, N_PQ, N_PEER = HH * 6, KC * 4, 16, 2 * NKEYS
_at = 0
START = {}
for _name, _n in (("fox", N_FOX), ("nsa", N_NSA), ("out0", N_OUT), ("ffn0", N_FFN), ("moba", N_MOBA),
                  ("out1", N_OUT), ("ffn1", N_FFN), ("hgrn", N_HGRN), ("hyena", N_HYENA), ("wa", N_OUT),
                  ("wb", N_OUT), ("out2", N_OUT), ("pq", N_PQ), ("peer", N_PEER)):
    START[_name] = _at
    _at += _n
N_SLABS = _at
SPLIT = {"ffn0": 0, "ffn1": N_FFN, "peer": 2 * N_FFN}

SMALL = {}
_at = 0
for _name, _n in (("wfg", KC * 40), ("w2k", 2 * HD), ("w2v", 2 * HD), ("pek", 16), ("pev", 16), ("bf", 1),
                  ("gains", 11 * KC), ("lbl", 2 * HH), ("hg", 1), ("convw", 24 * 3), ("convb", 24),
                  ("hbias", KC), ("fw1", 64), ("fvec", 4), ("fw2", 64)):
    SMALL[_name] = (_at, _n)
    _at += _n
N_SMALL = _at

TABLE = {}
_at = 0
for _name, _n in (("eye", P), ("iota", P), ("cos", 2 * T), ("sin", 2 * T), ("rot", P), ("causal", 384),
                  ("cmpadd", 4 * 16), ("cmpmul", 4 * 16), ("dft", 2 * 2 * T), ("idft", 4 * T),
                  ("zT", T), ("taprow", T), ("cmask", 2), ("ebot", 8), ("etop", 8), ("tapmask", 2)):
    TABLE[_name] = (_at, _n)
    _at += _n
N_TABLE = _at

G_MIX_PRE, G_MIX_POST, G_FFN_PRE, G_FFN_POST, G_MIX2, G_FFN2, G_FINAL = 0, 2, 4, 6, 8, 9, 10


class Own:

    def __init__(self, eng, sem, i=None, per=0, base=0):
        self.eng, self.sem, self.n, self.i, self.per, self.base = eng, sem, base, i, per, base

    def __call__(self, ins):
        self.n += 1
        ins.then_inc(self.sem, 1)
        self.eng.wait_ge(self.sem, self.n if self.i is None else self.i * self.per + self.n)

    def end(self):
        assert self.i is None or self.n == self.per + self.base, (self.n, self.per)


def build(nc, weights, small, tables, masks, w3, decay, subkeys, x, out):
    ctx = ExitStack()
    sems = {}

    def S(stage, what):
        name = f"{stage}_{what}"
        if name not in sems:
            sems[name] = ctx.enter_context(nc.semaphore(name))
        return sems[name]

    def sb(name, shape, dt=F32):
        return ctx.enter_context(nc.sbuf_tensor(name, shape, dt))

    ring = sb("ring", [P, RING, D])
    wsplit = sb("wsplit", [P, RING, 2, D], F32R)
    hsplit = sb("hsplit", [P, 2, KC, T], F32R)
    gsplit = sb("gsplit", [P, 3, 2, T], F32R)
    xT = sb("xT", [P, KC, T])
    gains_sb = sb("gains_sb", [P, 11 * KC])
    ones = sb("ones", [P, P])
    zeros = sb("zeros", [1, P], BF16)
    eyeiota = sb("eyeiota", [P, 2 * P])
    sq = sb("sq", [P, KC, T])
    picks = sb("picks", [P, 3, T])
    root, rinv = picks[:, 0, :], picks[:, 1, :]
    act_in, gated = sq[:, 0:3, :], sq[:, 3:6, :]
    work = sb("work", [P, NKEYS * T])
    ps = ctx.enter_context(nc.psum_tensor("ps", [P, 8, 512], F32))

    pos = [0]

    def carve(*dims, dt=None):
        n = int(np.prod(dims))
        v = work[:, pos[0]:pos[0] + n]
        pos[0] += n
        if dt is not None:
            v = v.bitcast(dt)
        if len(dims) == 2:
            v = v.rearrange("p (a b) -> p a b", b=dims[1])
        if len(dims) == 3:
            v = v.rearrange("p (a b c) -> p a b c", b=dims[1], c=dims[2])
        if len(dims) == 4:
            v = v.rearrange("p (a b c d) -> p a b c d", b=dims[1], c=dims[2], d=dims[3])
        return v

    tab = carve(N_TABLE)
    sm = carve(N_SMALL)
    hT = carve(KC, T)
    level_masks = carve(LEVELS, P, dt=I32)
    filt_sum = carve(2, D)
    filt_dif = carve(2, D)
    sub = carve(16, P)
    era = pos[0]

    def small_(name, p=P):
        a, n = SMALL[name]
        return sm[0:p, a:a + n]

    def table(name, p=P):
        a, n = TABLE[name]
        return tab[0:p, a:a + n]

    eye, iota = eyeiota[:, 0:P], eyeiota[:, P:2 * P]

    def gain(g, c):
        return gains_sb[:, g * KC + c:g * KC + c + 1]

    def strided(v, offset, dims, p0=0, np_=P):
        base = v[p0:p0 + np_]
        return bass.AP(base.tensor, base.offset + offset, [list(base.ap[0])] + [list(d) for d in dims])

    Y = ps[:, 0:4, :].rearrange("p a (b t) -> p (a b) t", t=T)
    YB = ps[:, 4:8, :].rearrange("p a (b t) -> p (a b) t", t=T)

    landed = [S("ring", f"landed{s}") for s in range(RING)]
    ring_used = S("ring", "used")

    def slab_here(eng, s, i=None, n=0):
        v = 16 * (s // RING + 1)
        eng.wait_ge(landed[s % RING], v if i is None else i * (16 * n // RING) + v)

    def slab(s):
        return ring[:, s % RING, :]

    def zero_rows():
        return strided(zeros, 0, [[0, 4], [1, P]], 0, 1)

    def project(pe, dst, s, src, i=None, n=0, h_ready=None, hv=None):
        slab_here(pe, s, i, n)
        w = slab(s)
        for k in range(KC):
            if h_ready is not None:
                pe.wait_ge(h_ready, k + 1)
            mm = pe.matmul(dst, w[:, k * P:(k + 1) * P], src[:, k, :], start=(k == 0), stop=(k == KC - 1))
            if k == 0:
                mm.then_inc(ring_used, 1)
        return mm

    def project_rows(pe, dst, s, src, i=None, n=0):
        slab_here(pe, s, i, n)
        w = slab(s)
        for tt in range(TT):
            for k in range(KC):
                mm = pe.matmul(dst[:, tt, :], src[:, k, tt * P:(tt + 1) * P], w[:, k * P:(k + 1) * P],
                               start=(k == 0), stop=(k == KC - 1))
                if tt == 0 and k == 0:
                    mm.then_inc(ring_used, 1)
        return mm

    def split_index(stream, k):
        return SPLIT[stream] + k

    def lead_scalar(act, stream, k, i=0):
        s, n = START[stream] + k, split_index(stream, k)
        slab_here(act, s, i, 6)
        act.wait_ge(ring_used, i * 6 + (s - 1))
        act.activation(wsplit[:, n % RING, 0, :], slab(s), ACT.Copy).then_inc(S("split", "lead"), 1)

    def rest_vector(v, stream, k, i=0):
        s, n = START[stream] + k, split_index(stream, k)
        v.wait_ge(S("split", "lead"), i * 6 + (n + 1))
        v.tensor_tensor(wsplit[:, n % RING, 1, :], slab(s), wsplit[:, n % RING, 0, :],
                        ALU.subtract).then_inc(S("split", "rest"), 1)

    def split_project(pe, dst, stream, k, i=0):
        n = split_index(stream, k)
        pe.wait_ge(S("split", "rest"), i * 6 + (n + 1))
        for c in range(KC):
            for t, (a, b) in enumerate(TERMS):
                mm = pe.matmul(dst, wsplit[:, n % RING, a, c * P:(c + 1) * P], hsplit[:, b, c, :],
                               start=(c == 0 and t == 0), stop=(c == KC - 1 and t == 2))
                if c == 0 and t == 0:
                    mm.then_inc(ring_used, 1)
        return mm

    def split_output(pe, stream, k, slot, i=0):
        n = split_index(stream, k)
        pe.wait_ge(S("split", "rest"), i * 6 + (n + 1))
        for j in range(KC):
            for t, (a, b) in enumerate(TERMS):
                mm = pe.matmul(Y[:, j, :], wsplit[:, n % RING, a, j * P:(j + 1) * P], gsplit[:, slot, b, :],
                               start=False, stop=False, skip_group_check=True)
                if j == 0 and t == 0:
                    mm.then_inc(ring_used, 1)

    def gate_vector(v, own, slot, up, sem):
        own(v.tensor_tensor(gated[:, slot, :], act_in[:, slot, :], up, ALU.mult))
        own(v.tensor_copy(gsplit[:, slot, 0, :], gated[:, slot, :]))
        v.tensor_tensor(gsplit[:, slot, 1, :], gated[:, slot, :], gsplit[:, slot, 0, :], ALU.subtract).then_inc(sem, 1)

    HSPLITS = ("n1", "n3", "n5")

    def lead_h_scalar(act, st):
        for c in range(0, KC, 2):
            wait_h(act, st, c + 2)
            act.activation(hsplit[:, 0, c:c + 2, :], hT[:, c:c + 2, :], ACT.Copy).then_inc(S("split", "h_lead"), 1)

    def rest_h_vector(v, st):
        for c in range(0, KC, 2):
            v.wait_ge(S("split", "h_lead"), HSPLITS.index(st) * 4 + c // 2 + 1)
            v.tensor_tensor(hsplit[:, 1, c:c + 2, :], hT[:, c:c + 2, :], hsplit[:, 0, c:c + 2, :],
                            ALU.subtract).then_inc(S("split", "h_rest"), 1)

    def wait_h_split(pe, st):
        pe.wait_ge(S("split", "h_rest"), (HSPLITS.index(st) + 1) * 4)

    def out_project(pe, s0, src, dst, sem):
        for j in range(KC):
            project(pe, dst[:, j, :], s0 + j, src).then_inc(sem, 1)

    NORMS = ("n0", "p0", "n1", "p1", "n2", "p2", "n3", "p3", "n4", "n5", "n6")

    def nth(st, kind=""):
        return sum(x.startswith(kind) for x in NORMS[:NORMS.index(st)])

    def own_steps(st):
        return nth(st, "n") + nth(st, "p") * (KC + 1)

    def wait_h(eng, st, k=KC):
        eng.wait_ge(S("norm", "h"), KC * nth(st, "n") + k)

    def norm_scalar(act, st, src, ready, value, n=KC, bank=7):
        act.wait_ge(ready, value)
        act.activation(sq[:, 0:n, :], src, ACT.Square).then_inc(S("norm", "squares"), 1)
        act.wait_ge(S("norm", "sums"), nth(st) + 1)
        act.activation(root, ps[:, bank, 0:T], ACT.Sqrt, scale=1.0 / D, bias=eps_col).then_inc(S("norm", "root"), 1)

    def norm_tensor(pe, st, bank=7):
        pe.wait_ge(S("norm", "squares"), nth(st) + 1)
        for k in range(KC):
            mm = pe.matmul(ps[:, bank, 0:T], ones[:, :], sq[:, k, :], start=(k == 0), stop=(k == KC - 1))
        mm.then_inc(S("norm", "sums"), 1)

    def pre_norm_vector(v, st, g):
        own = Own(v, S("norm", "own"), base=own_steps(st))
        v.wait_ge(S("norm", "root"), nth(st) + 1)
        own(v.reciprocal(rinv, root))
        for c in range(KC):
            v.scalar_tensor_tensor(hT[:, c, :], xT[:, c, :], gain(g, c), rinv, ALU.mult,
                                   ALU.mult).then_inc(S("norm", "h"), 1)

    def post_norm_vector(v, st, g):
        own = Own(v, S("norm", "own"), base=own_steps(st))
        v.wait_ge(S("norm", "root"), nth(st) + 1)
        own(v.reciprocal(rinv, root))
        for c in range(KC):
            own(v.scalar_tensor_tensor(sq[:, c, :], Y[:, c, :], gain(g, c), rinv, ALU.mult, ALU.mult))
        v.tensor_tensor(xT[:, :, :], xT[:, :, :], sq[:, :, :], ALU.add).then_inc(S("norm", "x"), 1)

    def ffn_tensor(pe, layer, pre):
        stream = f"ffn{layer}"
        wait_h(pe, pre, 1)
        for y in range(4):
            pe.matmul(ps[:, y, :], zeros[:, :], zero_rows(), start=True, stop=False, skip_group_check=True)
        wait_h_split(pe, pre)
        with pe.Fori(0, FC // 2) as i:
            for u in range(2):
                split_project(pe, ps[:, 4 + u, 0:T], stream, 2 * u, i)
                split_project(pe, ps[:, 4 + u, T:2 * T], stream, 2 * u + 1, i).then_inc(S("ffn", "gate_up"), 1)
            for u in range(2):
                pe.wait_ge(S("ffn", "act"), i * 2 + (layer * FC + u + 1))
                split_output(pe, stream, 4 + u, u, i)
        for y in range(4):
            mm = pe.matmul(ps[:, y, :], zeros[:, :], zero_rows(), start=False, stop=True, skip_group_check=True)
        mm.then_inc(S("ffn", "y"), 1)

    def ffn_turn(layer, i, split, act, last):
        for k in (2, 3):
            split(k, i)
        act(i, 0)
        for k in (4, 5):
            split(k, i)
        act(i, 1)
        if not last:
            for k in (6, 7):
                split(k, i)

    def ffn_scalar(act, layer, pre):
        lead_h_scalar(act, pre)

        def split(k, i=0):
            lead_scalar(act, f"ffn{layer}", k, i)

        def silu(i, u):
            act.wait_ge(S("ffn", "gate_up"), i * 2 + (layer * FC + u + 1))
            act.activation(act_in[:, u, :], ps[:, 4 + u, 0:T], ACT.Silu).then_inc(S("ffn", "silu"), 1)
        split(0)
        split(1)
        with act.Fori(0, FC // 2 - 1) as i:
            ffn_turn(layer, i, split, silu, False)
        ffn_turn(layer, FC // 2 - 1, split, silu, True)

    def ffn_vector(v, layer, pre):
        rest_h_vector(v, pre)

        def split(k, i=0):
            rest_vector(v, f"ffn{layer}", k, i)

        def turn(i, last):
            own = Own(v, S("ffn", "own"), i, 4, layer * (FC // 2) * 4)

            def gate(i, u):
                v.wait_ge(S("ffn", "silu"), i * 2 + (layer * FC + u + 1))
                gate_vector(v, own, u, ps[:, 4 + u, T:2 * T], S("ffn", "act"))
            ffn_turn(layer, i, split, gate, last)
            own.end()
        split(0)
        split(1)
        with v.Fori(0, FC // 2 - 1) as i:
            turn(i, False)
        turn(FC // 2 - 1, True)

    SEGS = ((1, 0, T), (0, T, P))
    pos[0] = era
    attnT = carve(KC, T)
    qk_raw, qk_turn, qk_tmp = carve(2, T), carve(2, T), carve(2, T)
    vrows = carve(TT, P)
    sc_sb, pr = carve(2, 2, 384), carve(2, 2, 384)
    prT = carve(2, 2, 384)
    top, ntop, total, scale_ = carve(8), carve(8), carve(8), carve(8)
    logit, labs, lexp, lln, lf, csum = (carve(T) for _ in range(6))
    gates = carve(TT, 24)
    shared = pos[0]
    bias_q, bias_k = carve(8, T), carve(8, T)
    pos[0] = shared
    nraw, nrope = carve(4, 2 * T), carve(4, 2 * T)
    vcomp_raw = carve(2, T)
    nv = carve(4, P)
    Xk, Xv = carve(16, 2, NC), carve(16, 2, NC)
    hid, hidT = carve(2, T), carve(4, 32)
    kcT, vcmp = carve(16), carve(HD)
    cs, cp = carve(4, 16), carve(TT, 2, 32)
    ctop, csumc, cscale = carve(4), carve(4), carve(4)
    pcT = carve(T)
    att_end = pos[0]
    causal = table("causal").unsqueeze(1).to_broadcast([P, 2, 384])
    cos2 = table("cos").rearrange("p (a t) -> p a t", a=2)
    sin2 = table("sin").rearrange("p (a t) -> p a t", a=2)

    def scores_tensor(pe, q, k, bank0, bias=None):
        for hh in range(2):
            h_ = slice(HD * hh, HD * hh + HD)
            for tt, c0, keys in SEGS:
                dst = ps[:, bank0 + hh, c0:c0 + keys]
                mm = pe.matmul(dst, q[h_, tt * P:(tt + 1) * P], k[h_, 0:keys], start=True, stop=bias is None)
                if bias is not None:
                    head = bias * 2 + hh
                    mm = pe.matmul(dst, bias_q[0:16, head, tt * P:(tt + 1) * P], bias_k[0:16, head, 0:keys],
                                   start=False, stop=True)
        return mm

    def turn_probs_tensor(pe, br, bank0):
        for hh in range(2):
            for c_out, c_in in ((0, T), (P, 0), (T, P)):
                mm = pe.transpose(ps[:, bank0 + hh, c_out:c_out + P], pr[:, br, hh, c_in:c_in + P], eye)
        return mm

    def values_tensor(pe, br, v0, v1, first, last):
        for hh in range(2):
            h_ = slice(HD * hh, HD * hh + HD)
            pe.matmul(ps[h_, 7, 0:T], v0[:, h_], prT[:, br, hh, 0:T], start=first, stop=False)
            mm = pe.matmul(ps[h_, 7, P:T], v1[:, h_], prT[:, br, hh, T:T + P], start=False, stop=last)
        return mm

    BEFORE = {"fox": 0, "moba": 4}

    def pair_tensor(pe, st, s0, i, u, last, rope):
        n = i * 2 + u
        m = i * 2 + (u + BEFORE[st])
        if rope:
            pe.wait_ge(S("pair", "qk_sb"), m + 1)
            pe.matmul(ps[:, 2, :], table("rot"), qk_raw[:, :, :].rearrange("p a t -> p (a t)"), start=True,
                      stop=True).then_inc(S(st, "turned"), 1)
        project_rows(pe, ps[:, 1, 0:T].rearrange("p (a c) -> p a c", a=TT), s0 + 3 * u + 2, hT, i,
                     6).then_inc(S("pair", "v"), 1)
        pe.wait_ge(S(st, "qk_turn") if rope else S("pair", "qk_sb"), (n if rope else m) + 1)
        scores_tensor(pe, qk_turn[:, 0, :], qk_turn[:, 1, :], 3, None if rope else n).then_inc(S("pair", "scores"), 1)
        if not last:
            query_key_tensor(pe, st, s0 + 3 * (u + 1), i)
        pe.wait_ge(S("pair", "probs"), m + 1)
        turn_probs_tensor(pe, 0, 5).then_inc(S("pair", "probsT"), 1)
        pe.wait_ge(S("pair", "v_sb"), m + 1)
        pe.wait_ge(S("pair", "probsT_sb"), m + 1)
        values_tensor(pe, 0, vrows[:, 0, :], vrows[:, 1, :], True, True).then_inc(S("pair", "o"), 1)

    def query_key_tensor(pe, st, s, i):
        project(pe, ps[:, 0, 0:T], s, hT, i, 6)
        project(pe, ps[:, 0, T:2 * T], s + 1, hT, i, 6).then_inc(S("pair", "qk"), 1)

    def query_key_scalar(act, st, n, rope):
        m = n + BEFORE[st]
        act.wait_ge(S("pair", "qk"), m + 1)
        if rope:
            act.activation(qk_raw[:, :, :].rearrange("p a t -> p (a t)"), ps[:, 0, :], ACT.Copy).then_inc(S("pair", "qk_sb"), 1)
        else:
            act.activation(qk_turn[:, 0, :], ps[:, 0, 0:T], ACT.Copy, scale=HD ** -0.5)
            act.activation(qk_turn[:, 1, :], ps[:, 0, T:2 * T], ACT.Copy).then_inc(S("pair", "qk_sb"), 1)

    def exps_scalar(act, br):
        for hh in range(2):
            for g, (tt, c0, keys) in enumerate(SEGS):
                m = (br * 2 + hh) * 2 + g
                ins = act.activation(pr[:, br, hh, c0:c0 + keys], sc_sb[:, br, hh, c0:c0 + keys], ACT.Exp,
                                     bias=ntop[:, m:m + 1], accum_out=total[:, m:m + 1])
        return ins

    def pair_scalar(act, st, i, u, last, rope, chunk0):
        n = i * 2 + u
        m = i * 2 + (u + BEFORE[st])
        act.wait_ge(S("pair", "v"), m + 1)
        act.activation(vrows[:, :, :].rearrange("p a c -> p (a c)"), ps[:, 1, 0:T], ACT.Copy).then_inc(S("pair", "v_sb"), 1)
        act.wait_ge(S("pair", "tops"), m + 1)
        exps_scalar(act, 0).then_inc(S("pair", "exps"), 1)
        if not last:
            query_key_scalar(act, st, n + 1, rope)
        act.wait_ge(S("pair", "o"), m + 1)
        act.activation(attnT[:, bass.ds(n + chunk0, 1), :].rearrange("p a t -> p (a t)"), ps[:, 7, 0:T],
                       ACT.Copy).then_inc(S("pair", "o_sb"), 1)

    def tops_vector(v, own, br, bank0):
        own(v.tensor_tensor(sc_sb[:, br, :, :], ps[:, bank0:bank0 + 2, 0:384], causal, ALU.add))
        m = 4 * br
        for g, (tt, c0, keys) in enumerate(SEGS):
            ins = v.tensor_reduce(top[:, m + g:m + 4:2], sc_sb[:, br, :, c0:c0 + keys], AX_X, ALU.max)
            own(ins)
        return v.tensor_scalar(ntop[:, m:m + 4], top[:, m:m + 4], -1.0, None, ALU.mult)

    def scale_probs_vector(v, br):
        for hh in range(2):
            for g, (tt, c0, keys) in enumerate(SEGS):
                m = (br * 2 + hh) * 2 + g
                p_ = pr[:, br, hh, c0:c0 + keys]
                ins = v.tensor_scalar(p_, p_, scale_[:, m:m + 1], None, ALU.mult)
        return ins

    def pair_vector(v, st, own, i, u, rope):
        n = i * 2 + u
        m = i * 2 + (u + BEFORE[st])
        if rope:
            v.wait_ge(S(st, "turned"), n + 1)
            own(v.tensor_tensor(qk_turn[:, :, :], qk_raw[:, :, :], cos2, ALU.mult))
            own(v.tensor_tensor(qk_tmp[:, :, :], ps[:, 2, :].rearrange("p (a t) -> p a t", a=2), sin2, ALU.mult))
            v.tensor_tensor(qk_turn[:, :, :], qk_turn[:, :, :], qk_tmp[:, :, :], ALU.add).then_inc(S(st, "qk_turn"), 1)
        v.wait_ge(S("pair", "scores"), m + 1)
        tops_vector(v, own, 0, 3).then_inc(S("pair", "tops"), 1)
        v.wait_ge(S("pair", "exps"), m + 1)
        own(v.reciprocal(scale_[:, 0:4], total[:, 0:4]))
        scale_probs_vector(v, 0).then_inc(S("pair", "probs"), 1)
        v.wait_ge(S("pair", "probsT"), m + 1)
        v.tensor_copy(prT[:, 0, :, :], ps[:, 5:7, 0:384]).then_inc(S("pair", "probsT_sb"), 1)

    def fox_tensor(pe, st, pre, s0):
        pe.wait_ge(S("load", "small"), 16)
        for k in range(KC):
            wait_h(pe, pre, k + 1)
            mm = pe.matmul(ps[0:16, 6, 0:T], small_("wfg")[:, k * 40:k * 40 + 16], hT[:, k, :], start=(k == 0), stop=(k == KC - 1))
        for g, tt in enumerate((1, 0)):
            for k in range(KC):
                mm = pe.matmul(ps[:, 6, T + 32 * g:T + 32 * g + 24], hT[:, k, tt * P:(tt + 1) * P],
                               small_("wfg")[:, k * 40 + 16:k * 40 + 40], start=(k == 0), stop=(k == KC - 1))
        mm.then_inc(S(st, "logits"), 1)
        query_key_tensor(pe, st, s0, 0)
        pe.wait_ge(S(st, "biases"), 1)
        for i in range(2):
            for u in range(2):
                pair_tensor(pe, st, s0, i, u, i == 1 and u == 1, False)

    def fox_scalar(act, st):
        act.wait_ge(S(st, "logits"), 1)
        act.activation(logit[0:16, :], ps[0:16, 6, 0:T], ACT.Identity, bias=small_("bf", 16)).then_inc(S(st, "logit_sb"), 1)
        act.activation(gates[:, :, :], ps[:, 6, T:T + 64].rearrange("p (a c) -> p a c", a=2)[:, :, 0:24], ACT.Sigmoid)
        act.activation(labs[0:16, :], ps[0:16, 6, 0:T], ACT.Abs, bias=small_("bf", 16)).then_inc(S(st, "labs"), 1)
        act.wait_ge(S(st, "labs"), 1)
        act.activation(lexp[0:16, :], labs[0:16, :], ACT.Exp, scale=-1.0).then_inc(S(st, "lexp"), 1)
        act.wait_ge(S(st, "lexp1"), 1)
        act.activation(lln[0:16, :], lexp[0:16, :], ACT.Ln).then_inc(S(st, "lln"), 1)
        query_key_scalar(act, st, 0, False)
        for i in range(2):
            for u in range(2):
                pair_scalar(act, st, i, u, i == 1 and u == 1, False, 0)

    def fox_vector(v, st):
        own = Own(v, S(st, "own"))
        v.wait_ge(S(st, "logit_sb"), 1)
        v.wait_ge(S(st, "lexp"), 1)
        v.tensor_scalar(lexp[0:16, :], lexp[0:16, :], 1.0, None, ALU.add).then_inc(S(st, "lexp1"), 1)
        own(v.tensor_scalar(logit[0:16, :], logit[0:16, :], 0.0, None, ALU.min))
        v.wait_ge(S(st, "lln"), 1)
        own(v.tensor_tensor(lf[0:16, :], logit[0:16, :], lln[0:16, :], ALU.subtract))
        own(v.memset(labs[0:16, :], 1.0))
        own(v.tensor_tensor_scan(csum[0:16, :], labs[0:16, :], lf[0:16, :], 0.0, ALU.mult, ALU.add))
        for h in range(8):
            v.tensor_scalar(bias_q[0:16, h, :], csum[0:16, :], table("cmask", 16)[:, 0:1], table("ebot", 16)[:, h:h + 1],
                            ALU.mult, ALU.add)
            ins = v.tensor_scalar(bias_k[0:16, h, :], csum[0:16, :], table("cmask", 16)[:, 1:2],
                                  table("etop", 16)[:, h:h + 1], ALU.mult, ALU.add)
        ins.then_inc(S(st, "biases"), 1)
        for i in range(2):
            for u in range(2):
                pair_vector(v, st, own, i, u, False)

    def moba_tensor(pe, st, pre, s0):
        wait_h(pe, pre)
        query_key_tensor(pe, st, s0, 0)
        with pe.Fori(0, 3) as i:
            for u in range(2):
                pair_tensor(pe, st, s0, i, u, False, True)
        for u in range(2):
            pair_tensor(pe, st, s0, 3, u, u == 1, True)

    def moba_scalar(act, st):
        query_key_scalar(act, st, 0, True)
        with act.Fori(0, 3) as i:
            for u in range(2):
                pair_scalar(act, st, i, u, False, True, 0)
        for u in range(2):
            pair_scalar(act, st, 3, u, u == 1, True, 0)

    def moba_vector(v, st):
        def turn(i):
            own = Own(v, S(st, "own"), i, 12)
            for u in range(2):
                pair_vector(v, st, own, i, u, True)
            own.end()
        with v.Fori(0, 3) as i:
            turn(i)
        turn(3)

    RAW = (0, "v", 1, 2, 3)

    def nsa_tensor(pe, st, s0):
        def two(bank, s, row):
            project(pe, ps[:, bank, 0:T], s, hT)
            project(pe, ps[:, bank, T:2 * T], s + 1, hT).then_inc(S(st, "raw"), 1)

        def turn(row, bank):
            pe.wait_ge(S(st, "raw_sb"), RAW.index(row) + 1)
            pe.matmul(ps[:, bank, :], table("rot"), nraw[:, row, :], start=True, stop=True).then_inc(S(st, "turned"), 1)

        pe.wait_ge(S("pair", "o_sb"), 4)
        two(0, s0, 0)
        two(1, s0 + 2, "v")
        two(2, s0 + 4, 1)
        turn(0, 6)
        project_rows(pe, ps[:, 3, 0:T].rearrange("p (a c) -> p a c", a=TT), s0 + 6, hT)
        project_rows(pe, ps[:, 3, T:2 * T].rearrange("p (a c) -> p a c", a=TT), s0 + 7, hT).then_inc(S(st, "nv"), 1)
        turn(1, 7)
        two(4, s0 + 8, 2)
        pe.wait_ge(S(st, "rope"), 2)
        two(5, s0 + 10, 3)
        turn(2, 6)
        turn(3, 7)
        for kv, X in ((0, Xk), (1, Xv)):
            pe.wait_ge(S(st, "X"), kv + 1)
            for j in range(16):
                s = s0 + 12 + 4 * kv + j // 4
                if j % 4 == 0:
                    slab_here(pe, s)
                w = slab(s)[:, (j % 4) * T:(j % 4 + 1) * T]
                mm = pe.matmul(ps[0:2 * NC, kv, 0:T], X[:, j, :, :].rearrange("p g c -> p (g c)"), w,
                               start=(j == 0), stop=(j == 15))
                if j % 4 == 0:
                    mm.then_inc(ring_used, 1)
            mm.then_inc(S(st, "hidden"), 1)
        for kv in range(2):
            pe.wait_ge(S(st, "gelu"), kv + 1)
            for kt in range(2):
                c = (kv * 2 + kt) * 32
                mm = pe.transpose(ps[:, 2, c:c + 2 * NC], hid[0:2 * NC, kv, kt * P:(kt + 1) * P], eye[0:2 * NC, 0:2 * NC])
        mm.then_inc(S(st, "hiddenT"), 1)
        pe.wait_ge(S(st, "hiddenT_sb"), 1)
        for g in range(2):
            for kt in range(2):
                pe.matmul(ps[HD * g:HD * g + HD, 3, 0:NC], small_("w2k")[:, kt * HD:(kt + 1) * HD],
                          hidT[:, kt, g * NC:(g + 1) * NC], start=(kt == 0), stop=(kt == 1))
        for g in range(2):
            for kt in range(2):
                mm = pe.matmul(ps[32 * g:32 * g + NC, 3, HD:2 * HD], hidT[:, 2 + kt, g * NC:(g + 1) * NC],
                               small_("w2v")[:, kt * HD:(kt + 1) * HD], start=(kt == 0), stop=(kt == 1))
        mm.then_inc(S(st, "comp"), 1)
        pe.wait_ge(S(st, "comp_sb"), 1)
        pe.wait_ge(S(st, "rope"), 4)
        for j in range(4):
            q = nrope[:, 2 + j // 2, (j % 2) * T:(j % 2 + 1) * T]
            for hh in range(2):
                h_ = slice(HD * hh, HD * hh + HD)
                for g, tt in enumerate((1, 0)):
                    mm = pe.matmul(ps[:, hh, 16 * g:16 * g + NC], q[h_, tt * P:(tt + 1) * P], kcT[h_, 0:NC], start=True, stop=True)
            mm.then_inc(S(st, "cscores"), 1)
            scores_tensor(pe, q, nrope[:, 1, 0:T], 3).then_inc(S(st, "scores"), 1)
            scores_tensor(pe, q, nrope[:, 1, T:2 * T], 5).then_inc(S(st, "scores"), 1)
            pe.wait_ge(S(st, "cprobs"), j + 1)
            for g, tt in enumerate((1, 0)):
                mm = pe.transpose(ps[0:HD, 0, T + tt * P:T + (tt + 1) * P], cp[:, g, :, :].rearrange("p h c -> p (h c)"), eye)
            mm.then_inc(S(st, "cprobsT"), 1)
            for br in range(2):
                pe.wait_ge(S(st, "probs"), 2 * j + br + 1)
                turn_probs_tensor(pe, br, 1 + 2 * br).then_inc(S(st, "probsT"), 1)
            for br in range(2):
                pe.wait_ge(S(st, "probsT_sb"), 2 * j + br + 1)
                if br == 0 and j > 0:
                    pe.wait_ge(S(st, "o_sb"), j)
                values_tensor(pe, br, nv[:, 2 * br, :], nv[:, 2 * br + 1, :], br == 0, False)
            pe.wait_ge(S(st, "cprobsT_sb"), j + 1)
            for hh in range(2):
                mm = pe.matmul(ps[HD * hh:HD * hh + HD, 7, 0:T], vcmp[32 * hh:32 * hh + NC, :],
                               pcT[32 * hh:32 * hh + NC, :], start=False, stop=True)
            mm.then_inc(S(st, "o"), 1)

    def nsa_scalar(act, st):
        def take(row, bank, dst):
            act.wait_ge(S(st, "raw"), RAW.index(row) + 1)
            act.activation(dst, ps[:, bank, :], ACT.Copy).then_inc(S(st, "raw_sb"), 1)

        take(0, 0, nraw[:, 0, :])
        take("v", 1, vcomp_raw[:, :, :].rearrange("p a t -> p (a t)"))
        take(1, 2, nraw[:, 1, :])
        act.wait_ge(S(st, "nv"), 1)
        act.activation(nv[:, :, :].rearrange("p a c -> p (a c)"), ps[:, 3, :], ACT.Copy)
        take(2, 4, nraw[:, 2, :])
        take(3, 5, nraw[:, 3, :])
        for kv in range(2):
            act.wait_ge(S(st, "hidden"), kv + 1)
            act.activation(hid[0:2 * NC, kv, :], ps[0:2 * NC, kv, 0:T], ACT.Gelu_apprx_tanh).then_inc(S(st, "gelu"), 1)
        act.wait_ge(S(st, "comp"), 1)
        act.activation(kcT[:, 0:NC], ps[:, 3, 0:NC], ACT.Copy)
        act.activation(vcmp[0:NC, :], ps[0:NC, 3, HD:2 * HD], ACT.Copy)
        act.activation(vcmp[32:32 + NC, :], ps[32:32 + NC, 3, HD:2 * HD], ACT.Copy).then_inc(S(st, "comp_sb"), 1)
        for j in range(4):
            act.wait_ge(S(st, "ctops"), j + 1)
            act.activation(cs[:, :, 0:NC], cs[:, :, 0:NC], ACT.Exp).then_inc(S(st, "cexps"), 1)
            for br in range(2):
                act.wait_ge(S(st, "tops"), 2 * j + br + 1)
                exps_scalar(act, br).then_inc(S(st, "exps"), 1)
            act.wait_ge(S(st, "cprobsT"), j + 1)
            act.activation(pcT[0:HD, :], ps[0:HD, 0, T:2 * T], ACT.Copy).then_inc(S(st, "cprobsT_sb"), 1)
            act.wait_ge(S(st, "o"), j + 1)
            act.activation(attnT[:, 4 + j, :], ps[:, 7, 0:T], ACT.Copy).then_inc(S(st, "o_sb"), 1)

    def nsa_vector(v, st):
        own = Own(v, S(st, "own"))
        own(v.memset(cp[:, :, :, :], 0.0))

        def rope(row, bank, half):
            v.wait_ge(S(st, "turned"), row + 1)
            co = cos2[:, half:half + 1, :].to_broadcast([P, 2, T])
            si = sin2[:, half:half + 1, :].to_broadcast([P, 2, T])
            y = nrope[:, row, :].rearrange("p (a t) -> p a t", a=2)
            own(v.tensor_tensor(y, nraw[:, row, :].rearrange("p (a t) -> p a t", a=2), co, ALU.mult))
            own(v.tensor_tensor(qk_tmp[:, :, :], ps[:, bank, :].rearrange("p (a t) -> p a t", a=2), si, ALU.mult))
            ins = v.tensor_tensor(y, y, qk_tmp[:, :, :], ALU.add)
            ins.then_inc(S(st, "rope"), 1)
            v.wait_ge(S(st, "rope"), row + 1)

        def unfold(X, src, pe_name):
            for half in range(2):
                for jh in range(2):
                    h_ = slice(HD * half, HD * half + HD)
                    for jj in range(0, 8):
                        j = 8 * jh + jj
                        a = SMALL[pe_name][0] + j
                        ins = v.tensor_scalar(X[h_, j, :, :], strided(src, 2 * j + half, [[T, 2], [16, NC]], HD * half, HD),
                                              sm[h_, a:a + 1], None, ALU.add)
            return ins

        rope(0, 6, 1)
        unfold(Xk, nrope[:, 0, :], "pek").then_inc(S(st, "X"), 1)
        v.wait_ge(S(st, "raw_sb"), RAW.index("v") + 1)
        unfold(Xv, vcomp_raw[:, :, :].rearrange("p a t -> p (a t)"), "pev").then_inc(S(st, "X"), 1)
        rope(1, 7, 1)
        rope(2, 6, 0)
        rope(3, 7, 0)
        v.wait_ge(S(st, "hiddenT"), 1)
        v.tensor_copy(hidT[:, :, 0:2 * NC], ps[:, 2, 0:P].rearrange("p (a c) -> p a c", a=4)[:, :, 0:2 * NC]).then_inc(S(st, "hiddenT_sb"), 1)
        for j in range(4):
            v.wait_ge(S(st, "cscores"), j + 1)
            add_ = table("cmpadd").rearrange("p (a c) -> p a c", a=4)[:, :, 0:NC]
            mul_ = table("cmpmul").rearrange("p (a c) -> p a c", a=4)[:, :, 0:NC]
            c4 = cs[:, :, 0:NC]
            own(v.tensor_tensor(c4.rearrange("p (g h) c -> p g h c", g=2),
                                ps[:, 0:2, 0:32].rearrange("p h (g c) -> p g h c", g=2)[:, :, :, 0:NC],
                                add_.rearrange("p (g h) c -> p g h c", g=2), ALU.add))
            own(v.tensor_reduce(ctop[:, :], c4, AX_X, ALU.max))
            v.tensor_tensor(c4, c4, ctop[:, :].unsqueeze(2).to_broadcast([P, 4, NC]), ALU.subtract).then_inc(S(st, "ctops"), 1)
            for br in range(2):
                v.wait_ge(S(st, "scores"), 2 * j + br + 1)
                tops_vector(v, own, br, 3 + 2 * br).then_inc(S(st, "tops"), 1)
            v.wait_ge(S(st, "cexps"), j + 1)
            own(v.tensor_tensor(c4, c4, mul_, ALU.mult))
            own(v.tensor_reduce(csumc[:, :], c4, AX_X, ALU.add))
            own(v.tensor_scalar(csumc[:, :], csumc[:, :], 1e-30, None, ALU.max))
            own(v.reciprocal(cscale[:, :], csumc[:, :]))
            own(v.tensor_tensor(cscale[:, :].rearrange("p (g h) -> p g h", g=2), cscale[:, :].rearrange("p (g h) -> p g h", g=2),
                                gates[:, :, 2 * j:2 * j + 2], ALU.mult))
            v.tensor_tensor(cp[:, :, :, 0:NC], cs[:, :, 0:NC].rearrange("p (g h) c -> p g h c", g=2),
                            cscale[:, :].rearrange("p (g h) -> p g h", g=2).unsqueeze(3).to_broadcast([P, 2, 2, NC]),
                            ALU.mult).then_inc(S(st, "cprobs"), 1)
            for br in range(2):
                v.wait_ge(S(st, "exps"), 2 * j + br + 1)
                m = scale_[:, 4 * br:4 * br + 4]
                own(v.reciprocal(m, total[:, 4 * br:4 * br + 4]))
                c = 8 * (br + 1) + 2 * j
                own(v.tensor_tensor(m.rearrange("p (h g) -> p g h", g=2), m.rearrange("p (h g) -> p g h", g=2),
                                    gates[:, :, c:c + 2], ALU.mult))
                scale_probs_vector(v, br).then_inc(S(st, "probs"), 1)
            for br in range(2):
                v.wait_ge(S(st, "probsT"), 2 * j + br + 1)
                v.tensor_copy(prT[:, br, :, :], ps[:, 1 + 2 * br:3 + 2 * br, 0:384]).then_inc(S(st, "probsT_sb"), 1)
    pos[0] = era
    w3_sb = carve(2 * D)
    decay_sb = carve(2 * D)
    farg, fk, fred, fhid = carve(T), carve(T), carve(T), carve(T)
    fwin, ftap = carve(2, 512), carve(2, 512)
    MAGIC = 12582912.0
    TAU1 = 6.28125
    TAU2 = float(np.float32(np.round((2 * np.pi - TAU1) * 2 ** 20) / 2 ** 20))
    TAU3 = float(np.float32(2 * np.pi - TAU1 - TAU2))

    def filters_tensor(pe, st):
        pe.wait_ge(S("load", "small"), 16)
        pe.wait_ge(S("load", "tables"), 16)
        pe.matmul(ps[0:64, 0, 0:T], small_("fw1", 33), table("zT", 33), start=True, stop=True).then_inc(S(st, "pre"), 1)
        pe.wait_ge(S(st, "hid"), 1)
        pe.matmul(ps[0:64, 1, 0:T], small_("fw2", 64), fhid[0:64, :], start=True, stop=True).then_inc(S(st, "pre"), 1)
        pe.wait_ge(S(st, "hid"), 2)
        pe.wait_ge(S("load", "w3"), 16)
        pe.wait_ge(S(st, "decay"), 1)
        for n in range(4):
            pt, half = n // 2, n % 2
            if n > 0:
                pe.wait_ge(S(st, "taps"), n)
            for d in range(2):
                c = d * D + half * 512
                pe.matmul(ps[:, 2 + d, :], fhid[0:64, pt * P:(pt + 1) * P], w3_sb[0:64, c:c + 512], start=True, stop=True)
                mm = pe.matmul(ps[:, 4 + d, :], table("taprow", 1)[:, pt * P:(pt + 1) * P], decay_sb[0:1, c:c + 512],
                               start=True, stop=True)
            mm.then_inc(S(st, "filt"), 1)

    def filters_scalar(act, st):
        for n in range(2):
            act.wait_ge(S(st, "reduced"), n + 1)
            act.activation(fhid[0:64, :], fred[0:64, :], ACT.Sin).then_inc(S(st, "hid"), 1)
        act.wait_ge(S("load", "decay"), 16)
        act.activation(decay_sb[0:1, :], decay_sb[0:1, :], ACT.Abs).then_inc(S(st, "decay"), 1)
        for n in range(4):
            act.wait_ge(S(st, "filt"), n + 1)
            act.activation(fwin[:, :, :], ps[:, 4:6, :], ACT.Exp, scale=-1.0).then_inc(S(st, "window"), 1)

    def filters_vector(v, st):
        own = Own(v, S(st, "own"))
        for n in range(2):
            v.wait_ge(S(st, "pre"), n + 1)
            fv = small_("fvec", 64)
            own(v.tensor_scalar(farg[0:64, :], ps[0:64, n, 0:T], fv[:, 2 * n:2 * n + 1], fv[:, 2 * n + 1:2 * n + 2],
                                ALU.add, ALU.mult))
            own(v.tensor_scalar(fk[0:64, :], farg[0:64, :], 1 / (2 * np.pi), MAGIC, ALU.mult, ALU.add))
            own(v.tensor_scalar(fk[0:64, :], fk[0:64, :], -MAGIC, None, ALU.add))
            for tau in (TAU1, TAU2, TAU3):
                own(v.scalar_tensor_tensor(farg[0:64, :], fk[0:64, :], -tau, farg[0:64, :], ALU.mult, ALU.add))
            v.tensor_scalar(fred[0:64, :], farg[0:64, :], 3.1415925, -3.1415925, ALU.min,
                            ALU.max).then_inc(S(st, "reduced"), 1)
        for n in range(4):
            pt, half = n // 2, n % 2
            v.wait_ge(S(st, "window"), n + 1)
            own(v.tensor_tensor(ftap[:, 0, :], ps[:, 2, :], fwin[:, 0, :], ALU.mult))
            own(v.scalar_tensor_tensor(ftap[:, 1, :], ps[:, 3, :], table("tapmask")[:, pt:pt + 1], fwin[:, 1, :], ALU.mult, ALU.mult))
            own(v.tensor_tensor(filt_sum[:, pt, half * 512:(half + 1) * 512], ftap[:, 0, :], ftap[:, 1, :], ALU.add))
            v.tensor_tensor(filt_dif[:, pt, half * 512:(half + 1) * 512], ftap[:, 0, :], ftap[:, 1, :],
                            ALU.subtract).then_inc(S(st, "taps"), 1)

    pos[0] = era
    oall, silu_og, gate_a, gate_b, yb, merged = (carve(HH, T) for _ in range(6))
    sig_q, sig_og, qh, ksum = (carve(T) for _ in range(4))
    sig_f, sig_n = carve(2, T), carve(2, T)
    forget = carve(3, T)
    qa, kb = carve(2, T), carve(2, T)
    totals = [forget.rearrange("p a t -> p (a t)")] + [carve(3 * (T >> l)) for l in range(1, LEVELS)]
    kmix = carve(T)
    sT = carve(TT, T)
    hv = carve(TT, P)
    lbd, lbe, lbs, lb, oml = carve(2, HH), carve(2, HH), carve(HH), carve(HH), carve(HH)
    diag = strided(sT, 0, [[T + P, 2], [1, P]])

    def halves(v, h, off, n):
        return strided(v, off, [[2 * h, n], [T + h, 2], [1, h]])

    def mix_keys(v, h):
        n = T // (2 * h)
        return v.tensor_copy(strided(kmix, 0, [[2 * h, n], [h, 2], [1, h]]), halves(kb, h, 0, n))

    def hgrn_slab(pe, st, s, k, i):
        if k == 3:
            return project_rows(pe, ps[:, 1, T:2 * T].rearrange("p (a c) -> p a c", a=TT), s + 3, hT, i, 6).then_inc(S(st, "in1"), 1)
        mm = project(pe, ps[:, k // 2, (k % 2) * T:(k % 2 + 1) * T], s + k, hT, i, 6)
        if k in (1, 5):
            mm.then_inc(S(st, f"in{k // 2}"), 1)

    def hgrn_head_tensor(pe, st, s0, i, last):
        pe.wait_ge(S(st, "prep"), i + 1)
        pe.wait_ge(S(st, "staged"), i + 1)
        for k in range(LEVELS + 2):
            dst = ps[:, 3 + 2 * (k % 2), 0:T].rearrange("p (a c) -> p a c", a=2)
            if k >= 2:
                pe.wait_ge(S(st, "grown"), i * LEVELS + (k - 1))
            for a in range(2):
                if k == 0:
                    mm = pe.matmul(dst[:, a, :], ksum[:, a * P:(a + 1) * P], qh[:, a * P:(a + 1) * P], start=True, stop=True)
                elif k <= LEVELS:
                    h = 1 << (k - 1)
                    mm = pe.matmul(dst[:, a, :], kmix[:, a * P:(a + 1) * P], halves(qa, h, a * P, P // (2 * h)),
                                   start=True, stop=True)
                else:
                    mm = pe.matmul(dst[:, a, :], kb[:, a, a * P:(a + 1) * P], qa[:, 1 - a, (1 - a) * P:(2 - a) * P],
                                   start=True, stop=True)
            mm.then_inc(S(st, "level"), 1)
            if not last and 1 <= k <= 6:
                if k == 3:
                    pe.wait_ge(S(st, "v_sb"), i + 1)
                hgrn_slab(pe, st, s0 + 6, k - 1, i)
        pe.wait_ge(S(st, "scores"), i + 1)
        pe.wait_ge(S(st, "v_sb"), i + 1)
        for a in range(TT):
            mm = pe.matmul(ps[:, 4, 0:T], hv[:, a, :], sT[:, a, :], start=(a == 0), stop=(a == 1))
        mm.then_inc(S(st, "o"), 1)

    def hgrn_tensor(pe, st, pre, s0):
        wait_h(pe, pre)
        for k in range(6):
            hgrn_slab(pe, st, s0, k, None)
        with pe.Fori(0, HH - 1) as i:
            hgrn_head_tensor(pe, st, s0, i, False)
        hgrn_head_tensor(pe, st, s0, HH - 1, True)

    def hgrn_stage_scalar(act, st, n):
        act.wait_ge(S(st, "in0"), n + 1)
        act.activation(sig_q[:, :], ps[:, 0, 0:T], ACT.Sigmoid)
        act.activation(sig_f[:, 1, :], ps[:, 0, T:2 * T], ACT.Sigmoid)
        act.activation(sig_n[:, 0, :], ps[:, 0, T:2 * T], ACT.Sigmoid, scale=-1.0)
        act.wait_ge(S(st, "in1"), n + 1)
        act.activation(sig_f[:, 0, :], ps[:, 1, 0:T], ACT.Sigmoid)
        act.activation(sig_n[:, 1, :], ps[:, 1, 0:T], ACT.Sigmoid, scale=-1.0)
        act.wait_ge(S(st, "in2"), n + 1)
        act.activation(sig_og[:, :], ps[:, 2, 0:T], ACT.Sigmoid)
        act.activation(gate_a[:, bass.ds(n, 1), :].rearrange("p a t -> p (a t)"), ps[:, 2, T:2 * T],
                       ACT.Sigmoid).then_inc(S(st, "staged"), 1)

    def hgrn_value_scalar(act, st):
        act.activation(hv[:, :, :].rearrange("p a c -> p (a c)"), ps[:, 1, T:2 * T], ACT.Copy).then_inc(S(st, "v_sb"), 1)

    def hgrn_out_scalar(act, st, n):
        act.wait_ge(S(st, "o"), n + 1)
        act.activation(oall[:, bass.ds(n, 1), :].rearrange("p a t -> p (a t)"), ps[:, 4, 0:T], ACT.Copy).then_inc(S(st, "o_sb"), 1)

    def hgrn_scalar(act, st):
        act.wait_ge(S(st, "lbd"), 1)
        act.activation(lbe[:, :, :], lbd[:, :, :], ACT.Exp).then_inc(S(st, "lbe"), 1)
        hgrn_stage_scalar(act, st, 0)
        hgrn_value_scalar(act, st)
        with act.Fori(0, HH - 1) as i:
            hgrn_stage_scalar(act, st, i + 1)
            hgrn_out_scalar(act, st, i)
            hgrn_value_scalar(act, st)
        hgrn_out_scalar(act, st, HH - 1)

    def hgrn_head_vector(v, st, i):
        own = Own(v, S(st, "own"), i, 3 + LEVELS)
        v.wait_ge(S(st, "staged"), i + 1)
        l_, m_ = lb[:, bass.ds(i, 1)], oml[:, bass.ds(i, 1)]
        v.tensor_tensor(qh[:, :], ps[:, 0, 0:T], sig_q[:, :], ALU.mult)
        v.tensor_scalar(forget[:, 0:2, :], sig_f[:, :, :], m_, l_, ALU.mult, ALU.add)
        v.tensor_scalar(forget[:, 2, :], sig_f[:, 0, :], m_, l_, ALU.mult, ALU.add)
        own(v.tensor_scalar(kb[:, :, :], sig_n[:, :, :], m_, None, ALU.mult))
        own(v.tensor_tensor(silu_og[:, bass.ds(i, 1), :].rearrange("p a t -> p (a t)"), ps[:, 2, 0:T], sig_og[:, :], ALU.mult))
        mix_keys(v, 1)
        own(v.tensor_tensor(ksum[:, :], kb[:, 0, :], kb[:, 1, :], ALU.add))
        v.tensor_tensor(qa[:, :, :], forget[:, 0:2, :], qh[:, :].unsqueeze(1).to_broadcast([P, 2, T]),
                        ALU.mult).then_inc(S(st, "prep"), 1)
        v.wait_ge(S(st, "level"), i * (LEVELS + 2) + 1)
        own(v.tensor_tensor(diag, ps[:, 3, 0:T].rearrange("p (a c) -> p a c", a=2), eye.unsqueeze(1).to_broadcast([P, 2, P]), ALU.mult))
        for l in range(LEVELS):
            h = 1 << l
            n, nt = T // (2 * h), T // h
            bank = 3 + 2 * ((l + 1) % 2)
            v.wait_ge(S(st, "level"), i * (LEVELS + 2) + (l + 2))
            t_ = totals[l]
            q_, k_ = (strided(x_, 0, [[T + h, 2], [2 * h, n], [1, h]]) for x_ in (qa, kb))
            v.tensor_tensor(q_, q_, strided(t_, 1, [[nt - 1, 2], [2, n], [0, h]]), ALU.mult)
            v.copy_predicated(diag, level_masks[:, l, :].unsqueeze(1).to_broadcast([P, 2, P]),
                              ps[:, bank, 0:T].rearrange("p (a c) -> p a c", a=2))
            ins = v.tensor_tensor(k_, k_, strided(t_, nt + 1, [[nt - 1, 2], [2, n], [0, h]]), ALU.mult)
            if l < LEVELS - 1:
                own(v.tensor_tensor(strided(totals[l + 1], 0, [[n, 3], [1, n]]), strided(t_, 0, [[nt, 3], [2, n]]),
                                    strided(t_, 1, [[nt, 3], [2, n]]), ALU.mult))
                ins = mix_keys(v, 2 * h)
            ins.then_inc(S(st, "grown"), 1)
        v.wait_ge(S(st, "level"), i * (LEVELS + 2) + (LEVELS + 2))
        v.tensor_copy(strided(sT, P, [[1, T]]), ps[:, 3 + 2 * ((LEVELS + 1) % 2), 0:T]).then_inc(S(st, "scores"), 1)
        own.end()

    def hgrn_vector(v, st):
        pre = Own(v, S(st, "lb"))
        l2 = small_("lbl").rearrange("p (a h) -> p a h", a=2)
        pre(v.tensor_tensor(lbs[:, :], l2[:, 0, :], l2[:, 1, :], ALU.max))
        v.tensor_tensor(lbd[:, :, :], l2, lbs[:, :].unsqueeze(1).to_broadcast([P, 2, HH]), ALU.subtract).then_inc(S(st, "lbd"), 1)
        v.wait_ge(S(st, "lbe"), 1)
        pre(v.tensor_tensor(lbs[:, :], lbe[:, 0, :], lbe[:, 1, :], ALU.add))
        pre(v.reciprocal(lbs[:, :], lbs[:, :]))
        pre(v.tensor_tensor(lb[:, :], lbe[:, 0, :], lbs[:, :], ALU.mult))
        pre(v.tensor_scalar(oml[:, :], lb[:, :], -1.0, 1.0, ALU.mult, ALU.add))
        with v.Fori(0, HH) as i:
            hgrn_head_vector(v, st, i)

    def hgrn_norm_scalar(act, st):
        act.wait_ge(S("hgrn", "o_sb"), HH)
        act.activation(sq[:, :, :], oall[:, :, :], ACT.Square).then_inc(S(st, "squares"), 1)
        act.wait_ge(S(st, "sums"), 1)
        act.activation(merged[:, :, :], YB, ACT.Sqrt, scale=1.0 / P, bias=eps_col).then_inc(S(st, "root"), 1)

    def hgrn_norm_tensor(pe, st):
        pe.wait_ge(S(st, "squares"), 1)
        for c in range(4):
            mm = pe.matmul(ps[:, 4 + c, :], ones[:, :], sq[:, 2 * c:2 * c + 2, :].rearrange("p a t -> p (a t)"), start=True, stop=True)
        mm.then_inc(S(st, "sums"), 1)

    def hgrn_norm_vector(v, st):
        own = Own(v, S(st, "own"))
        v.wait_ge(S(st, "root"), 1)
        own(v.reciprocal(merged[:, :, :], merged[:, :, :]))
        f = lambda z: z[:, :, :].rearrange("p a t -> p (a t)")
        own(v.scalar_tensor_tensor(f(oall), f(oall), small_("hg"), f(merged), ALU.mult, ALU.mult))
        v.tensor_tensor(f(oall), f(oall), f(silu_og), ALU.mult).then_inc(S(st, "o"), 1)

    pos[0] = era + 6 * HH * T
    hy = carve(3, T + 2)
    conv = carve(3, T)
    u = carve(T)
    uT = carve(TT, P)
    taps_now = carve(2, 2, P)
    kspec = carve(3, T)
    prod_a, prod_b = carve(2, T), carve(2, T)
    yspec = carve(4, P)
    yspecT = carve(4, P)
    conv_y = carve(T)
    dft = table("dft").rearrange("p (a f) -> p a f", a=2)
    idft = table("idft").rearrange("p (a f) -> p a f", a=4)

    def hyena_slab(pe, st, s, k, i):
        mm = project(pe, ps[:, k // 2, (k % 2) * T:(k % 2 + 1) * T], s + k, hT, i, 12)
        if k % 2:
            mm.then_inc(S(st, f"in{k // 2}"), 1)

    def hyena_tile_tensor(pe, st, s0, i, u_, last):
        n = i * 3 + u_
        s = s0 + 4 * (u_ + 1)
        pe.wait_ge(S(st, "u"), n + 1)
        for a in range(TT):
            mm = pe.transpose(ps[:, 2, a * P:(a + 1) * P], u[:, a * P:(a + 1) * P], eye)
        mm.then_inc(S(st, "uT"), 1)
        if not last:
            hyena_slab(pe, st, s, 0, i)
        pe.wait_ge(S(st, "uT_sb"), n + 1)
        pe.wait_ge(S(st, "taps"), n + 1)
        for a in range(TT):
            pe.matmul(ps[:, 3, :], uT[:, a, :], dft[:, a, :], start=(a == 0), stop=(a == 1))
        for part in range(2):
            for a in range(2):
                mm = pe.matmul(ps[:, 4, part * T:(part + 1) * T], taps_now[:, part, a, :], dft[:, a, part * T:(part + 1) * T],
                               start=(a == 0), stop=(a == 1))
        mm.then_inc(S(st, "spectra"), 1)
        if not last:
            hyena_slab(pe, st, s, 1, i)
            hyena_slab(pe, st, s, 2, i)
        pe.wait_ge(S(st, "yspec"), n + 1)
        for f in range(4):
            mm = pe.transpose(ps[:, 5, f * P:(f + 1) * P], yspec[:, f, :], eye)
        mm.then_inc(S(st, "yspecT"), 1)
        if not last:
            hyena_slab(pe, st, s, 3, i)
        pe.wait_ge(S(st, "yspecT_sb"), n + 1)
        for f in range(4):
            mm = pe.matmul(ps[:, 6, 0:T], yspecT[:, f, :], idft[:, f, :], start=(f == 0), stop=(f == 3))
        mm.then_inc(S(st, "conv"), 1)

    def hyena_tensor(pe, st, s0):
        pe.wait_ge(S("hgrn", "o_sb"), HH)
        for k in range(4):
            hyena_slab(pe, st, s0, k, None)
        hgrn_norm_tensor(pe, "hnorm")
        pe.wait_ge(S("hnorm", "root"), 1)
        with pe.Fori(0, 2) as i:
            for u_ in range(3):
                hyena_tile_tensor(pe, st, s0, i, u_, False)
        hyena_tile_tensor(pe, st, s0, 2, 0, False)
        hyena_tile_tensor(pe, st, s0, 2, 1, True)

    def hyena_stage_scalar(act, st, n, part):
        act.wait_ge(S(st, f"in{part}"), n + 1)
        if part == 0:
            act.activation(hy[:, 0:2, 1:T + 1], ps[:, 0, :].rearrange("p (a t) -> p a t", a=2), ACT.Copy)
        else:
            act.activation(hy[:, 2, 1:T + 1], ps[:, 1, 0:T], ACT.Copy)
            act.activation(gate_b[:, bass.ds(n, 1), :].rearrange("p a t -> p (a t)"), ps[:, 1, T:2 * T],
                           ACT.Sigmoid).then_inc(S(st, "staged"), 1)

    def hyena_scalar(act, st):
        act.wait_ge(S(st, "pads"), 1)
        hyena_stage_scalar(act, st, 0, 0)
        hyena_stage_scalar(act, st, 0, 1)
        hgrn_norm_scalar(act, "hnorm")

        def tile(n, last):
            act.wait_ge(S(st, "uT"), n + 1)
            act.activation(uT[:, :, :].rearrange("p a c -> p (a c)"), ps[:, 2, 0:T], ACT.Copy).then_inc(S(st, "uT_sb"), 1)
            act.wait_ge(S(st, "spectra"), n + 1)
            act.activation(kspec[:, 0:2, :].rearrange("p a t -> p (a t)"), ps[:, 4, :], ACT.Copy)
            act.activation(kspec[:, 2, :], ps[:, 4, 0:T], ACT.Copy).then_inc(S(st, "kspec"), 1)
            if not last:
                hyena_stage_scalar(act, st, n + 1, 0)
            act.wait_ge(S(st, "yspecT"), n + 1)
            act.activation(yspecT[:, :, :].rearrange("p a c -> p (a c)"), ps[:, 5, :], ACT.Copy).then_inc(S(st, "yspecT_sb"), 1)
            if not last:
                hyena_stage_scalar(act, st, n + 1, 1)
        with act.Fori(0, HH - 1) as n:
            tile(n, False)
        tile(HH - 1, True)

    def hyena_gpsimd(pool, st):
        pool.wait_ge(S(st, "pads"), 1)
        with pool.Fori(0, KC) as n:
            pool.tensor_copy(taps_now[:, 0, :, :], filt_sum[:, :, bass.ds(n * P, P)])
            pool.tensor_copy(taps_now[:, 1, :, :], filt_dif[:, :, bass.ds(n * P, P)]).then_inc(S(st, "taps"), 1)
            pool.wait_ge(S(st, "spectra"), n + 1)

    def hyena_pads_vector(v, st):
        v.memset(hy[:, :, :], 0.0).then_inc(S(st, "pads"), 1)

    def hyena_vector(v, st):
        with v.Fori(0, KC) as n:
            own = Own(v, S(st, "own"), n, 6)
            v.wait_ge(S(st, "staged"), n + 1)

            def w(q, j):
                return sm[:, bass.ds(n * 3 + (SMALL["convw"][0] + q * 24 + j), 1)]
            for q in range(3):
                b_ = sm[:, bass.ds(n + (SMALL["convb"][0] + q * KC), 1)]
                ins = v.tensor_scalar(conv[:, q, :], hy[:, q, 1:T + 1], w(q, 1), b_, ALU.mult, ALU.add)
            own(ins)
            for q in range(3):
                ins = v.scalar_tensor_tensor(conv[:, q, :], hy[:, q, 0:T], w(q, 0), conv[:, q, :], ALU.mult, ALU.add)
            own(ins)
            for q in range(3):
                ins = v.scalar_tensor_tensor(conv[:, q, :], hy[:, q, 2:T + 2], w(q, 2), conv[:, q, :], ALU.mult, ALU.add)
            own(ins)
            v.tensor_tensor(u[:, :], conv[:, 2, :], conv[:, 1, :], ALU.mult).then_inc(S(st, "u"), 1)
            v.wait_ge(S(st, "kspec"), n + 1)
            uspec = ps[:, 3, :].rearrange("p (a t) -> p a t", a=2)
            v.tensor_tensor(prod_a[:, :, :], uspec, kspec[:, 0:2, :], ALU.mult)
            own(v.tensor_tensor(prod_b[:, :, :], uspec, kspec[:, 1:3, :], ALU.mult))
            f = yspec[:, :, :].rearrange("p a c -> p (a c)")
            v.tensor_tensor(f[:, 0:T], prod_a[:, 0, :], prod_a[:, 1, :], ALU.subtract)
            v.tensor_tensor(f[:, T:2 * T], prod_b[:, 0, :], prod_b[:, 1, :], ALU.add).then_inc(S(st, "yspec"), 1)
            v.wait_ge(S(st, "conv"), n + 1)
            own(v.scalar_tensor_tensor(conv_y[:, :], u[:, :], sm[:, bass.ds(n + SMALL["hbias"][0], 1)], ps[:, 6, 0:T],
                                       ALU.mult, ALU.add))
            own(v.tensor_tensor(yb[:, bass.ds(n, 1), :].rearrange("p a t -> p (a t)"), conv_y[:, :], conv[:, 0, :], ALU.mult))
            own.end()

    def merge_tensor(pe, st, sa, sbb, so):
        pe.wait_ge(S("hnorm", "o"), 1)
        out_project(pe, sa, oall, Y, S(st, "ya"))
        pe.wait_ge(S("hyena", "own"), KC * 6)
        out_project(pe, sbb, yb, YB, S(st, "yb"))
        pe.wait_ge(S(st, "merged"), KC)
        out_project(pe, so, merged, Y, S(st, "y"))

    def merge_vector(v, st):
        own = Own(v, S(st, "own"))
        for j in range(0, KC, 2):
            v.wait_ge(S(st, "ya"), j + 2)
            own(v.tensor_tensor(merged[:, j:j + 2, :], gate_a[:, j:j + 2, :], Y[:, j:j + 2, :], ALU.mult))
        for j in range(0, KC, 2):
            v.wait_ge(S(st, "yb"), j + 2)
            own(v.tensor_tensor(prod_a[:, :, :], gate_b[:, j:j + 2, :], YB[:, j:j + 2, :], ALU.mult))
            v.tensor_tensor(merged[:, j:j + 2, :], merged[:, j:j + 2, :], prod_a[:, :, :], ALU.add).then_inc(S(st, "merged"), 2)
            v.wait_ge(S(st, "merged"), j + 2)
        v.wait_ge(S(st, "y"), KC)
        v.tensor_tensor(xT[:, :, :], xT[:, :, :], Y, ALU.add).then_inc(S(st, "x"), 1)
    pos[0] = era
    s_all = carve(TT, 16, NKEYS)
    s_left = carve(NKEYS)
    best = carve(TT, 16, TOPK)
    best_at = carve(TT, 16, TOPK, dt=U32)
    best_key = carve(TT, 16, TOPK)
    cand = carve(TT, 8, TOPK * TOPK)
    c_left = carve(TOPK * TOPK)
    pick_s = carve(TT, 8, TOPK)
    pick_at = carve(TT, 8, TOPK, dt=U32)
    rank_u = carve(2, TT * 8 * TOPK, dt=U32)
    rank = carve(2, TT * 8 * TOPK)
    match = carve(TT * 8 * TOPK, TOPK)
    pick = carve(3, TT, 8 * TOPK)
    psum_ = carve(TT * 8)
    qsb = carve(2, T)
    assert pos[0] <= NKEYS * T
    hots = sq[:, :, :].rearrange("p a t -> p (a t)").rearrange("p (b c k n) -> p b c k n", b=2, c=2, k=4)
    peer_w = work[:, :].rearrange("p (n t) -> p n t", t=T)

    def pq_tensor(pe, st, pre, s0):
        wait_h(pe, pre)
        pe.wait_ge(S("load", "sub"), 16)

        def query(i, u):
            project(pe, ps[:, 4 + u % 2, 0:T], s0 + u, hT, i, 6).then_inc(S(st, "q"), 1)

        def score(i, u):
            pe.wait_ge(S(st, "q_sb"), i * 6 + (u + 1))
            for tt in range(TT):
                mm = pe.matmul(ps[:, 6 + u % 2, tt * P:(tt + 1) * P], qsb[:, u % 2, tt * P:(tt + 1) * P],
                               sub[:, bass.ds(i * 6 + u, 1), :].rearrange("p a k -> p (a k)"), start=True, stop=True)
            mm.then_inc(S(st, "s"), 1)

        def turn(i, n):
            query(i, 0)
            for u in range(1, n):
                query(i, u)
                score(i, u - 1)
            score(i, n - 1)
        with pe.Fori(0, 2) as i:
            turn(i, 6)
        turn(2, 4)

    def pq_scalar(act, st):
        def query(i, u):
            act.wait_ge(S(st, "q"), i * 6 + (u + 1))
            act.activation(qsb[:, u % 2, :], ps[:, 4 + u % 2, 0:T], ACT.Copy).then_inc(S(st, "q_sb"), 1)

        def score(i, u):
            act.wait_ge(S(st, "s"), i * 6 + (u + 1))
            act.activation(s_all[:, :, bass.ds(i * 6 + u, 1), :].rearrange("p t a k -> p t (a k)"),
                           ps[:, 6 + u % 2, 0:T].rearrange("p (t k) -> p t k", t=TT), ACT.Copy).then_inc(S(st, "s_sb"), 1)

        def turn(i, n):
            query(i, 0)
            for u in range(1, n):
                query(i, u)
                score(i, u - 1)
            score(i, n - 1)
        with act.Fori(0, 2) as i:
            turn(i, 6)
        turn(2, 4)

    def best16(v, own, values, left, out_v, out_at):
        own(v.max(out=out_v[:, 0:8], in_=values))
        own(v.max_index(out=out_at[:, 0:8], in_max=out_v[:, 0:8], in_values=values))
        own(v.match_replace(out=left, in_to_replace=out_v[:, 0:8], in_values=values, imm_value=-3e38))
        own(v.max(out=out_v[:, 8:16], in_=left))
        own(v.max_index(out=out_at[:, 8:16], in_max=out_v[:, 8:16], in_values=left))

    def picks_vector(v, st):
        own = Own(v, S(st, "own"))
        for hp in range(16):
            v.wait_ge(S("pq", "s_sb"), hp + 1)
            for tt in range(TT):
                best16(v, own, s_all[:, tt, hp, :], s_left[:, :], best[:, tt, hp, :], best_at[:, tt, hp, :])
        own(v.tensor_copy(best_key[:, :, :, :], best_at[:, :, :, :]))
        for tt in range(TT):
            own(v.tensor_tensor(cand[:, tt, :, :].rearrange("p h (a b) -> p h a b", b=TOPK),
                                strided(best, tt * 256, [[32, 8], [1, 16], [0, 16]]),
                                strided(best, tt * 256 + 16, [[32, 8], [0, 16], [1, 16]]), ALU.add))
        for tt in range(TT):
            for h in range(8):
                best16(v, own, cand[:, tt, h, :], c_left[:, :], pick_s[:, tt, h, :], pick_at[:, tt, h, :])
        at = pick_at[:, :, :, :].rearrange("p t h k -> p (t h k)")
        own(v.tensor_scalar(rank_u[:, 0, :], at, 4, None, ALU.logical_shift_right))
        own(v.tensor_scalar(rank_u[:, 1, :], at, 15, None, ALU.bitwise_and))
        own(v.tensor_copy(rank[:, :, :], rank_u[:, :, :]))
        n = TT * 8 * TOPK
        for half in range(2):
            own(v.tensor_tensor(match[:, :, :], strided(rank, half * n, [[1, n], [0, TOPK]]), strided(iota, 0, [[0, n], [1, TOPK]]),
                                ALU.is_equal))
            m4 = strided(match, 0, [[256, 16], [16, 16], [1, 16]])
            own(v.tensor_tensor(m4, m4, strided(best_key, 16 * half, [[32, 16], [0, 16], [1, 16]]), ALU.mult))
            own(v.tensor_reduce(pick[:, half, :, :].rearrange("p t k -> p (t k)"), match[:, :, :], AX_X, ALU.add))
        w4 = pick[:, 2, :, :].rearrange("p t (h k) -> p (t h) k", k=TOPK)
        s4 = pick_s[:, :, :, :].rearrange("p t h k -> p (t h) k")
        v.tensor_tensor(w4, s4, s4[:, :, 0:1].to_broadcast([P, 16, TOPK]), ALU.subtract).then_inc(S(st, "shifted"), 1)
        v.wait_ge(S(st, "exp"), 1)
        own(v.tensor_reduce(psum_[:, :], w4, AX_X, ALU.add))
        own(v.reciprocal(psum_[:, :], psum_[:, :]))
        v.tensor_tensor(w4, w4, psum_[:, :].unsqueeze(2).to_broadcast([P, 16, TOPK]), ALU.mult).then_inc(S(st, "picks"), 1)
        v.wait_ge(S(st, "picksT"), 1)
        v.tensor_copy(picks[:, 0:2, :].rearrange("p a t -> p (a t)"), ps[:, 4, :])
        v.tensor_copy(picks[:, 2, :], ps[:, 5, 0:T]).then_inc(S(st, "picksT_sb"), 1)
        v.wait_ge(S(st, "picksT_sb"), 1)

    def picks_scalar(act, st):
        act.wait_ge(S(st, "shifted"), 1)
        w_ = pick[:, 2, :, :].rearrange("p t k -> p (t k)")
        act.activation(w_, w_, ACT.Exp).then_inc(S(st, "exp"), 1)

    def picks_tensor(pe, st):
        pe.wait_ge(S(st, "picks"), 1)
        for a in range(3):
            for tt in range(TT):
                mm = pe.transpose(ps[:, 4 + a // 2, (a % 2) * T + tt * P:(a % 2) * T + (tt + 1) * P], pick[:, a, tt, :], eye)
        mm.then_inc(S(st, "picksT"), 1)

    BATCHES = T // 4

    def spread(eng, step):
        for u in range(2):
            step(0, u, True)
        with eng.Fori(1, BATCHES // 2) as i:
            for u in range(2):
                step(i, u, False)

    def spread_vector(v, st):
        def step(i, u, first):
            if not first:
                v.wait_ge(S(st, "weights"), i * 2 + (u - 1))
            for k in range(4):
                t = i * 8 + (u * 4 + k)
                v.tensor_scalar(hots[:, u, 1, k, :], iota, picks[:, 1, bass.ds(t, 1)], None, ALU.is_equal)
                ins = v.tensor_scalar(hots[:, u, 0, k, :], iota, picks[:, 0, bass.ds(t, 1)], picks[:, 2, bass.ds(t, 1)],
                                      ALU.is_equal, ALU.mult)
            ins.then_inc(S(st, "hot"), 1)
        spread(v, step)

    def spread_tensor(pe, st):
        def step(i, u, first):
            pe.wait_ge(S(st, "hot"), i * 2 + (u + 1))
            if not first:
                pe.wait_ge(S(st, "weights_sb"), i * 2 + (u - 1))
            for k in range(4):
                mm = pe.matmul(ps[:, 6 + u, k * P:(k + 1) * P], hots[:, u, 1, k, :], hots[:, u, 0, k, :], start=True, stop=True)
            mm.then_inc(S(st, "weights"), 1)
        spread(pe, step)

    def spread_scalar(act, st):
        def step(i, u, first):
            act.wait_ge(S(st, "weights"), i * 2 + (u + 1))
            act.activation(peer_w[:, :, bass.ds(i * 8 + u * 4, 4)], ps[:, 6 + u, :].rearrange("p (k n) -> p n k", k=4),
                           ACT.Copy).then_inc(S(st, "weights_sb"), 1)
        spread(act, step)

    def peer_tensor(pe, st):
        def hidden(k, i, slot):
            split_project(pe, ps[:, 4 + slot, 0:T], st, k, i).then_inc(S(st, "hidden"), 1)

        def output(k, i, slot, value):
            pe.wait_ge(S(st, "act"), value)
            split_output(pe, st, k, slot, i)

        for y in range(4):
            pe.matmul(ps[:, y, :], zeros[:, :], zero_rows(), start=True, stop=False, skip_group_check=True)
        wait_h_split(pe, "n5")
        pe.wait_ge(S("spread", "weights_sb"), BATCHES)
        hidden(0, 0, 0)
        hidden(1, 0, 1)
        with pe.Fori(0, (NKEYS - 2) // 3) as i:
            for u in range(3):
                output(2 + 2 * u, i, u, i * 3 + (u + 1))
                hidden(3 + 2 * u, i, (u + 2) % 3)
        output(2 * NKEYS - 2, 0, 0, NKEYS - 1)
        output(2 * NKEYS - 1, 0, 1, NKEYS)
        for y in range(4):
            mm = pe.matmul(ps[:, y, :], zeros[:, :], zero_rows(), start=False, stop=True, skip_group_check=True)
        mm.then_inc(S(st, "y"), 1)

    def peer_chunks(eng, split, step):
        split(0, 0)
        split(1, 0)
        with eng.Fori(0, (NKEYS - 2) // 3) as i:
            for u in range(3):
                step(i, u)
                split(2 + 2 * u, i)
                split(3 + 2 * u, i)
        i = (NKEYS - 2) // 3
        step(i, 0)
        split(2, i)
        split(3, i)
        step(i, 1)

    def peer_scalar(act, st):
        def split(k, i):
            lead_scalar(act, st, k, i)

        def step(i, u):
            act.wait_ge(S(st, "hidden"), i * 3 + (u + 1))
            act.activation(act_in[:, u, :], ps[:, 4 + u, 0:T], ACT.Gelu_apprx_tanh).then_inc(S(st, "gelu"), 1)
        peer_chunks(act, split, step)

    def peer_vector(v, st):
        def split(k, i):
            rest_vector(v, st, k, i)

        def step(i, u):
            own = Own(v, S(st, "own"), i, 6, 2 * u)
            v.wait_ge(S(st, "gelu"), i * 3 + (u + 1))
            gate_vector(v, own, u, peer_w[:, bass.ds(i * 3 + u, 1), :].rearrange("p a t -> p (a t)"), S(st, "act"))
        peer_chunks(v, split, step)
        v.wait_ge(S(st, "y"), 1)
        v.tensor_tensor(xT[:, :, :], xT[:, :, :], Y, ALU.add).then_inc(S(st, "x"), 1)
    eps_tile = sb("eps_tile", [P, 1])
    eps_col = eps_tile[:, 0:1]
    block = ctx.enter_context(nc.Block())
    B0 = START

    @block.sync
    def _(sp):
        def load(dst, src, name):
            sp.dma_start(dst, src).then_inc(S("load", name), 16)

        def load_slab(s, src):
            sp.dma_start(ring[:, s % RING, :], src).then_inc(landed[s % RING], 16)

        def stream(first, last, sem, ahead):
            end = first + (last - first) // RING * RING
            if end > first:
                with sp.Fori(0, (end - first) // RING) as i:
                    for s in range(first, first + RING):
                        sp.wait_ge(sem, i * RING + (s - ahead))
                        load_slab(s, weights[bass.ds(i * RING + s, 1)].rearrange("a p n -> (a p) n"))
            for s in range(max(end, first), last):
                sp.wait_ge(sem, s - ahead)
                load_slab(s, weights[s])

        load(tab, tables, "tables")
        load(sm, small, "small")
        load(xT[:, :, :], x, "x")
        load(w3_sb[0:64, :], w3, "w3")
        load(decay_sb[0:1, :], decay, "decay")
        for s in range(RING):
            load_slab(s, weights[s])
        load(level_masks, masks, "masks")
        load(sub, subkeys, "sub")
        at = RING
        for name in ("ffn0", "ffn1", "peer"):
            first = min(START[name] + RING, N_SLABS)
            stream(at, first, ring_used, 1)
            at = min(START[name] + RING + (N_PEER if name == "peer" else N_FFN), N_SLABS)
            if at > first:
                stream(first, at, S("split", "rest"), START[name] + RING - SPLIT[name] - 1)
        if at < N_SLABS:
            stream(at, N_SLABS, ring_used, 1)
        wait_h(sp, "n6")
        sp.dma_start(out, hT).then_inc(S("store", "out"), 16)
        sp.wait_ge(S("store", "out"), 16)

    @block.tensor
    def _(pe):
        pe.wait_ge(S("load", "eye"), 1)
        filters_tensor(pe, "filters")
        norm_tensor(pe, "n0")
        fox_tensor(pe, "fox", "n0", B0["fox"])
        nsa_tensor(pe, "nsa", B0["nsa"])
        pe.wait_ge(S("nsa", "o_sb"), 4)
        out_project(pe, B0["out0"], attnT, Y, S("out", "y"))
        norm_tensor(pe, "p0")
        norm_tensor(pe, "n1")
        ffn_tensor(pe, 0, "n1")
        norm_tensor(pe, "p1")
        norm_tensor(pe, "n2")
        moba_tensor(pe, "moba", "n2", B0["moba"])
        pe.wait_ge(S("pair", "o_sb"), 4 + 8)
        out_project(pe, B0["out1"], attnT, Y, S("out", "y"))
        norm_tensor(pe, "p2")
        norm_tensor(pe, "n3")
        ffn_tensor(pe, 1, "n3")
        norm_tensor(pe, "p3")
        norm_tensor(pe, "n4")
        hgrn_tensor(pe, "hgrn", "n4", B0["hgrn"])
        hyena_tensor(pe, "hyena", B0["hyena"])
        merge_tensor(pe, "merge", B0["wa"], B0["wb"], B0["out2"])
        norm_tensor(pe, "n5")
        pq_tensor(pe, "pq", "n5", B0["pq"])
        picks_tensor(pe, "picks")
        spread_tensor(pe, "spread")
        peer_tensor(pe, "peer")
        norm_tensor(pe, "n6")

    @block.scalar
    def _(act):
        filters_scalar(act, "filters")
        norm_scalar(act, "n0", xT[:, :, :], S("load", "x"), 16)
        fox_scalar(act, "fox")
        nsa_scalar(act, "nsa")
        norm_scalar(act, "p0", Y, S("out", "y"), KC)
        norm_scalar(act, "n1", xT[:, :, :], S("norm", "x"), 1)
        ffn_scalar(act, 0, "n1")
        norm_scalar(act, "p1", Y, S("ffn", "y"), 1)
        norm_scalar(act, "n2", xT[:, :, :], S("norm", "x"), 2)
        moba_scalar(act, "moba")
        norm_scalar(act, "p2", Y, S("out", "y"), 2 * KC)
        norm_scalar(act, "n3", xT[:, :, :], S("norm", "x"), 3)
        ffn_scalar(act, 1, "n3")
        norm_scalar(act, "p3", Y, S("ffn", "y"), 2)
        norm_scalar(act, "n4", xT[:, :, :], S("norm", "x"), 4)
        hgrn_scalar(act, "hgrn")
        hyena_scalar(act, "hyena")
        norm_scalar(act, "n5", xT[:, :, :], S("merge", "x"), 1)
        lead_h_scalar(act, "n5")
        pq_scalar(act, "pq")
        picks_scalar(act, "picks")
        spread_scalar(act, "spread")
        peer_scalar(act, "peer")
        norm_scalar(act, "n6", xT[:, :, :], S("peer", "x"), 1)

    @block.vector
    def _(v):
        v.memset(ones[:, :], 1.0)
        v.memset(zeros[:, :], 0.0)
        v.memset(eps_tile[:, :], EPS)
        v.wait_ge(S("load", "tables"), 16)
        v.wait_ge(S("load", "small"), 16)
        v.tensor_copy(gains_sb[:, :], small_("gains"))
        v.tensor_copy(eyeiota[:, :], tab[:, 0:2 * P]).then_inc(S("load", "eye"), 1)
        v.wait_ge(S("load", "eye"), 1)
        filters_vector(v, "filters")
        pre_norm_vector(v, "n0", G_MIX_PRE)
        fox_vector(v, "fox")
        nsa_vector(v, "nsa")
        post_norm_vector(v, "p0", G_MIX_POST)
        pre_norm_vector(v, "n1", G_FFN_PRE)
        ffn_vector(v, 0, "n1")
        post_norm_vector(v, "p1", G_FFN_POST)
        pre_norm_vector(v, "n2", G_MIX_PRE + 1)
        moba_vector(v, "moba")
        post_norm_vector(v, "p2", G_MIX_POST + 1)
        pre_norm_vector(v, "n3", G_FFN_PRE + 1)
        ffn_vector(v, 1, "n3")
        post_norm_vector(v, "p3", G_FFN_POST + 1)
        pre_norm_vector(v, "n4", G_MIX2)
        v.wait_ge(S("load", "masks"), 16)
        hgrn_vector(v, "hgrn")
        hyena_pads_vector(v, "hyena")
        hgrn_norm_vector(v, "hnorm")
        hyena_vector(v, "hyena")
        merge_vector(v, "merge")
        pre_norm_vector(v, "n5", G_FFN2)
        rest_h_vector(v, "n5")
        picks_vector(v, "picks")
        spread_vector(v, "spread")
        peer_vector(v, "peer")
        pre_norm_vector(v, "n6", G_FINAL)

    @block.gpsimd
    def _(pool):
        hyena_gpsimd(pool, "hyena")

    ctx.close()



def shape_tables():
    t = {}
    pp = np.arange(P)
    t["eye"] = np.eye(P)
    t["iota"] = np.tile(np.arange(P), (P, 1))
    inv = (np.float32(10000.0) ** (-np.arange(0, HD, 2, dtype=np.float32) / np.float32(HD))).astype(np.float32)
    ang = np.arange(T, dtype=np.float32)[:, None] * inv[None, :]
    cos, sin = np.cos(ang.astype(np.float64)).T, np.sin(ang.astype(np.float64)).T
    c4, s4 = np.tile(cos, (4, 1)), np.tile(sin, (4, 1))
    q = HD ** -0.5
    t["cos"] = np.concatenate([c4 * q, c4], 1)
    t["sin"] = np.concatenate([s4 * q, s4], 1)
    rot = np.zeros((P, P))
    for h in range(2):
        for d in range(32):
            rot[h * 64 + 32 + d, h * 64 + d] = -1.0
            rot[h * 64 + d, h * 64 + 32 + d] = 1.0
    t["rot"] = rot
    causal = np.zeros((P, 384))
    causal[:, 0:T] = np.where(np.arange(T)[None] <= P + pp[:, None], 0, NEG)
    causal[:, T:] = np.where(pp[None] <= pp[:, None], 0, NEG)
    t["causal"] = causal
    add, mul = np.zeros((P, 4, 16)), np.zeros((P, 4, 16))
    for g, tt in enumerate((1, 0)):
        ok = (np.arange(NC)[None] * 16 + 31) <= (tt * P + pp[:, None])
        for hh in range(2):
            add[:, g * 2 + hh, :NC] = np.where(ok, 0, NEG)
            mul[:, g * 2 + hh, :NC] = ok
    t["cmpadd"], t["cmpmul"] = add.reshape(P, -1), mul.reshape(P, -1)
    th = 2 * np.pi * ((np.arange(T)[:, None] * np.arange(T)[None, :]) % NFFT) / NFFT
    f = np.concatenate([np.cos(th), -np.sin(th)], 1)
    t["dft"] = f.reshape(2, P, 2 * T).transpose(1, 0, 2).reshape(P, -1)
    wgt = np.where(np.arange(T) == 0, 1.0, 2.0)[:, None] / NFFT
    g = np.concatenate([np.cos(th) * wgt, -np.sin(th) * wgt], 0)
    t["idft"] = g.reshape(4, P, T).transpose(1, 0, 2).reshape(P, -1)
    posn = np.arange(T, dtype=np.float32)
    tpos = posn / np.float32(T - 1)
    bands = np.linspace(1e-4, 15, 16, dtype=np.float32)
    a2 = (np.float32(2.0 * np.pi / T) * posn)[:, None] * bands[None, :]
    z = np.concatenate([tpos[:, None], np.cos(a2), -np.sin(a2)], 1)
    t["zT"] = np.pad(z.T, ((0, P - 33), (0, 0)))
    t["taprow"] = np.pad(tpos[None], ((0, P - 1), (0, 0)))
    cm = np.zeros((P, 2))
    cm[0:8, 0], cm[8:16, 1] = 1, -1
    t["cmask"] = cm
    eb, et = np.zeros((P, 8)), np.zeros((P, 8))
    for h in range(8):
        eb[8 + h, h], et[h, h] = 1, 1
    t["ebot"], t["etop"] = eb, et
    tm = np.ones((P, 2))
    tm[0, 0] = 0
    t["tapmask"] = tm
    out = np.zeros((P, N_TABLE), np.float32)
    for k, (a, n) in TABLE.items():
        out[:, a:a + n] = t[k]
    s, c = np.meshgrid(pp, pp, indexing="ij")
    m = [((s >> (l + 1)) == (c >> (l + 1))) & ((s >> l) != (c >> l)) for l in range(LEVELS)]
    return out, np.stack(m, 1).astype(np.int32)


def pack(a):
    f = lambda k: np.asarray(a[k])
    parts = []

    def cols(w):
        m = w.shape[1] // P
        parts.append(w.reshape(KC, P, m, P).transpose(2, 1, 0, 3).reshape(m, P, D))

    def rows(w):
        parts.append(w.reshape(-1, P, D))

    win = f("ev_w_in")[0]
    e = 0
    o = {}
    for name, n in (("fq", 512), ("fk", 512), ("fv", 512), ("f", 8), ("nq", 512), ("kc", 128), ("vc", 128), ("ks", 128),
                    ("vs", 128), ("kw", 128), ("vw", 128), ("g", 24)):
        o[name] = win[:, e:e + n]
        e += n
    for p in range(4):
        for name in ("fq", "fk", "fv"):
            cols(o[name][:, p * P:(p + 1) * P])
    pairs = np.concatenate([np.r_[j * HD:(j + 1) * HD, (j + 4) * HD:(j + 5) * HD] for j in range(4)])
    for name in ("kc", "vc"):
        for g in range(2):
            cols(np.concatenate([o[name][:, g * HD:(g + 1) * HD]] * 2, 1))
    for name in ("ks", "kw", "vs", "vw"):
        cols(o[name])
    cols(o["nq"][:, pairs])
    for name in ("ev_cmp_w1_k", "ev_cmp_w1_v"):
        parts.append(f(name)[0].reshape(4, 4, P, T).transpose(0, 2, 1, 3).reshape(4, P, D))
    cols(f("ev_w_out")[0][np.concatenate([np.arange(512), 512 + pairs])])

    def ffn(layer):
        g, u, dn = f("ffn_w_gate")[layer], f("ffn_w_up")[layer], f("ffn_w_down")[layer]
        for c in range(0, FC, 2):
            for cc in (c, c + 1):
                cols(g[:, cc * P:(cc + 1) * P])
                cols(u[:, cc * P:(cc + 1) * P])
            rows(dn[c * P:(c + 2) * P])

    ffn(0)
    wo = f("od_w_in")[0]
    for p in range(8):
        for n in range(3):
            cols(wo[:, n * D + p * P:n * D + (p + 1) * P])
    cols(f("od_w_out")[0])
    ffn(1)
    w = f("w_in_2")[0]
    seg = lambda n, j: w[:, n * D + j * P:n * D + (j + 1) * P]
    for h in range(HH):
        for n in (0, 1, 2, 3, 4, 8):
            cols(seg(n, h))
    for j in range(KC):
        for n in (5, 6, 7, 9):
            cols(seg(n, j))
    for name in ("w_branch_a_2", "w_branch_b_2", "w_out_2"):
        cols(f(name)[0])
    cols(f("peer_w_q_2")[0])
    u = f("peer_u_2")[0].reshape(NKEYS, P, KC, P).transpose(0, 3, 2, 1).reshape(NKEYS, P, D)
    v = f("peer_v_2")[0].reshape(NKEYS, P, D)
    both = np.stack([u[2:], v[:-2]], 1)[:, ::-1].reshape(-1, P, D)
    parts += [u[0:2], both, v[-2:]]
    weights = np.concatenate(parts)

    small = np.zeros((P, N_SMALL), np.float32)

    def put(name, v):
        a0, n = SMALL[name]
        assert v.shape[1] == n, (name, v.shape)
        small[0:v.shape[0], a0:a0 + n] = v

    gp = np.concatenate([np.stack([o["g"][:, (j + 4 * hh) * 3 + b] for j in range(4) for hh in range(2)], 1) for b in range(3)], 1)
    wfg = np.concatenate([o["f"], o["f"], gp], 1)
    put("wfg", wfg.reshape(KC, P, 40).transpose(1, 0, 2).reshape(P, -1))
    for k in "kv":
        put("w2" + k, f("ev_cmp_w2_" + k)[0].reshape(2, P, HD).transpose(1, 0, 2).reshape(P, -1))
        put("pe" + k, f("ev_cmp_pe_" + k)[0].reshape(16, 2, HD).transpose(1, 2, 0).reshape(P, 16))
    put("bf", np.tile(f("ev_b_f")[0], 2)[:, None])
    gs = np.concatenate([f("g_mix_pre"), f("g_mix_post"), f("g_ffn_pre"), f("g_ffn_post"), f("norm_mix_g_2"),
                         f("norm_ffn_g_2"), f("norm_final_g_2")[None]])
    put("gains", gs.reshape(11, KC, P).transpose(2, 0, 1).reshape(P, -1))
    put("lbl", f("hgrn_lb_logits_2").reshape(2, HH, P).transpose(2, 0, 1).reshape(P, -1))
    put("hg", f("hgrn_norm_g_2").reshape(P, 1))
    put("convw", f("hyena_conv_w_2")[0].reshape(3, 24, P).transpose(2, 1, 0).reshape(P, -1))
    put("convb", f("hyena_conv_b_2")[0].reshape(24, P).T)
    put("hbias", f("hyena_bias_2")[0].reshape(KC, P).T)
    put("fw1", f("filt_w1_2")[0])
    put("fvec", np.stack([f("filt_b1_2")[0], f("filt_freq1_2")[0], f("filt_b2_2")[0], f("filt_freq2_2")[0]], 1))
    put("fw2", f("filt_w2_2")[0])
    tables, masks = shape_tables()
    return {
        "weights": weights, "small": small, "tables": tables, "masks": masks,
        "w3": f("filt_w3_2")[0], "decay": f("filt_decay_2"),
        "subkeys": f("peer_subkeys_2")[0].transpose(3, 0, 1, 2).reshape(P, 16, NKEYS),
        "x": f("x")[0].T.reshape(KC, P, T).transpose(1, 0, 2),
    }


def kernel(**inputs):
    import concourse.bacc as _bacc
    from concourse.bass_utils import run_bass_kernel_spmd as _run

    nc = _bacc.Bacc("TRN2", target_bir_lowering=False, num_devices=1)
    arrays, args = {}, {}
    for name, a in pack(inputs).items():
        a = np.ascontiguousarray(a)
        arrays[f"in_{name}"] = a
        args[name] = nc.dram_tensor(f"in_{name}", a.shape, mybir.dt.from_np(a.dtype), kind="ExternalInput").ap()
    out = nc.dram_tensor("out_x", (P, KC, T), F32, kind="ExternalOutput").ap()
    build(nc, out=out, **args)
    r = _run(nc, [arrays], core_ids=[0])
    y = np.asarray(r.results[0]["out_x"])
    return np.ascontiguousarray(y.transpose(2, 1, 0).reshape(1, T, D))
```

```python
from contextlib import ExitStack

import numpy as np

import concourse.bass as bass
from concourse import mybir

ALU = mybir.AluOpType
ACT = mybir.ActivationFunctionType
F32 = mybir.dt.float32
F32R = mybir.dt.float32r
BF16 = mybir.dt.bfloat16
I32 = mybir.dt.int32
U32 = mybir.dt.uint32
AX_X = mybir.AxisListType.X

P = 128
D = 1024
KC = D // P
T = 256
TT = T // P
HD = 64
FF = 2816
FC = FF // P
RING = 3
TERMS = ((0, 0), (0, 1), (1, 0))
EPS = 1e-6
NEG = -1e30
NC = T // 16 - 1
NFFT = 511
HH = 8
LEVELS = 7
NKEYS = 128
TOPK = 16

N_FOX, N_NSA, N_OUT, N_FFN, N_MOBA = 4 * 3, 4 + 8 + 4 + 4, KC, 3 * FC, 8 * 3
EARLY = 30
N_HGRN, N_HYENA, N_PQ, N_PEER = HH * 6, KC * 4, 16 + EARLY, 2 * NKEYS - EARLY
_at = 0
START = {}
for _name, _n in (("fox", N_FOX), ("nsa", N_NSA), ("out0", N_OUT), ("ffn0", N_FFN), ("moba", N_MOBA),
                  ("out1", N_OUT), ("ffn1", N_FFN), ("hgrn", N_HGRN), ("hyena", N_HYENA), ("wb", N_OUT),
                  ("wa", N_OUT), ("out2", N_OUT), ("pq", N_PQ), ("peer", N_PEER)):
    START[_name] = _at
    _at += _n
N_SLABS = _at
SPLIT, RESTS = {}, {}
_at, _counted = 0, {"rest": 0, "rest_pool": 0}
for _name, _n, _which in (("ffn0", N_FFN, "rest"), ("ffn1", N_FFN, "rest"), ("hgrn", N_HGRN + N_HYENA, "rest_pool"),
                          ("pq", N_PQ, "rest_pool"), ("peer", N_PEER, "rest")):
    SPLIT[_name], RESTS[_name] = _at, (_which, _counted[_which])
    _at += _n
    _counted[_which] += _n

SMALL = {}
_at = 0
for _name, _n in (("wfg", KC * 40), ("w2k", 2 * HD), ("w2v", 2 * HD), ("pek", 16), ("pev", 16), ("bf", 1),
                  ("gains", 11 * KC), ("lbl", 2 * HH), ("hg", 1), ("convw", 24 * 3), ("convb", 24),
                  ("hbias", KC), ("fw1", 64), ("fvec", 4), ("fw2", 64)):
    SMALL[_name] = (_at, _n)
    _at += _n
N_SMALL = _at

TABLE = {}
_at = 0
for _name, _n in (("eye", P), ("iota", P), ("cos", 2 * T), ("sin", 2 * T), ("rot", P), ("causal", 384),
                  ("cmpadd", 4 * 16), ("cmpmul", 4 * 16), ("dft", 2 * 2 * T), ("idft", 4 * T),
                  ("zT", T), ("ntap", 2), ("cmask", 2), ("ebot", 8), ("etop", 8), ("tapmask", 2)):
    TABLE[_name] = (_at, _n)
    _at += _n
N_TABLE = _at

G_MIX_PRE, G_MIX_POST, G_FFN_PRE, G_FFN_POST, G_MIX2, G_FFN2, G_FINAL = 0, 2, 4, 6, 8, 9, 10


class Own:

    def __init__(self, eng, sem, i=None, per=0, base=0):
        self.eng, self.sem, self.n, self.i, self.per, self.base = eng, sem, base, i, per, base

    def __call__(self, ins):
        self.n += 1
        ins.then_inc(self.sem, 1)
        self.eng.wait_ge(self.sem, self.n if self.i is None else self.i * self.per + self.n)

    def end(self):
        assert self.i is None or self.n == self.per + self.base, (self.n, self.per)


def build(nc, weights, small, tables, masks, w3, decay, subkeys, x, out):
    ctx = ExitStack()
    sems = {}

    def S(stage, what):
        name = f"{stage}_{what}"
        if name not in sems:
            sems[name] = ctx.enter_context(nc.semaphore(name))
        return sems[name]

    def sb(name, shape, dt=F32):
        return ctx.enter_context(nc.sbuf_tensor(name, shape, dt))

    ring = sb("ring", [P, RING, D])
    wsplit = sb("wsplit", [P, RING, 2, D], F32R)
    hsplit = sb("hsplit", [P, 2, KC, T], F32R)
    gsplit = sb("gsplit", [P, 3, 2, T], F32R)
    xT = sb("xT", [P, KC, T])
    gains_sb = sb("gains_sb", [P, 11 * KC])
    ones = sb("ones", [P, P])
    zeros = sb("zeros", [1, P], BF16)
    eyeiota = sb("eyeiota", [P, 2 * P])
    sq = sb("sq", [P, KC, T])
    picks = sb("picks", [P, 3, T])
    root, rinv = picks[:, 0, :], picks[:, 1, :]
    act_in, gated = sq[:, 0:3, :], sq[:, 3:6, :]
    work = sb("work", [P, NKEYS * T])
    ps = ctx.enter_context(nc.psum_tensor("ps", [P, 8, 512], F32))

    pos = [0]

    def carve(*dims, dt=None):
        n = int(np.prod(dims))
        v = work[:, pos[0]:pos[0] + n]
        pos[0] += n
        if dt is not None:
            v = v.bitcast(dt)
        if len(dims) == 2:
            v = v.rearrange("p (a b) -> p a b", b=dims[1])
        if len(dims) == 3:
            v = v.rearrange("p (a b c) -> p a b c", b=dims[1], c=dims[2])
        if len(dims) == 4:
            v = v.rearrange("p (a b c d) -> p a b c d", b=dims[1], c=dims[2], d=dims[3])
        return v

    tab = carve(N_TABLE)
    sm = carve(N_SMALL)
    hT = carve(KC, T)
    level_masks = carve(LEVELS, P, dt=I32)
    filt_sum = carve(2, D)
    filt_dif = carve(2, D)
    sub = carve(16, P)
    era = pos[0]

    def small_(name, p=P):
        a, n = SMALL[name]
        return sm[0:p, a:a + n]

    def table(name, p=P):
        a, n = TABLE[name]
        return tab[0:p, a:a + n]

    eye, iota = eyeiota[:, 0:P], eyeiota[:, P:2 * P]

    def gain(g, c):
        return gains_sb[:, g * KC + c:g * KC + c + 1]

    def strided(v, offset, dims, p0=0, np_=P):
        base = v[p0:p0 + np_]
        return bass.AP(base.tensor, base.offset + offset, [list(base.ap[0])] + [list(d) for d in dims])

    Y = ps[:, 0:4, :].rearrange("p a (b t) -> p (a b) t", t=T)
    YB = ps[:, 4:8, :].rearrange("p a (b t) -> p (a b) t", t=T)

    landed = [S("ring", f"landed{s}") for s in range(RING)]
    ring_used = S("ring", "used")

    def slab_here(eng, s, i=None, n=0):
        v = 16 * (s // RING + 1)
        eng.wait_ge(landed[s % RING], v if i is None else i * (16 * n // RING) + v)

    def slab(s):
        return ring[:, s % RING, :]

    def zero_rows():
        return strided(zeros, 0, [[0, 4], [1, P]], 0, 1)

    def project(pe, dst, s, src, i=None, n=0, h_ready=None, hv=None):
        slab_here(pe, s, i, n)
        w = slab(s)
        for k in range(KC):
            if h_ready is not None:
                pe.wait_ge(h_ready, k + 1)
            mm = pe.matmul(dst, w[:, k * P:(k + 1) * P], src[:, k, :], start=(k == 0), stop=(k == KC - 1))
            if k == 0:
                mm.then_inc(ring_used, 1)
        return mm

    def project_rows(pe, dst, s, src, i=None, n=0):
        slab_here(pe, s, i, n)
        w = slab(s)
        for tt in range(TT):
            for k in range(KC):
                mm = pe.matmul(dst[:, tt, :], src[:, k, tt * P:(tt + 1) * P], w[:, k * P:(k + 1) * P],
                               start=(k == 0), stop=(k == KC - 1))
                if tt == 0 and k == 0:
                    mm.then_inc(ring_used, 1)
        return mm

    def split_index(stream, k):
        return SPLIT[stream] + k

    def lead_scalar(act, stream, k, i=0, per=6):
        s, n = START[stream] + k, split_index(stream, k)
        slab_here(act, s, i, per)
        act.wait_ge(ring_used, i * per + (s - 1))
        act.activation(wsplit[:, n % RING, 0, :], slab(s), ACT.Copy).then_inc(S("split", "lead"), 1)

    def rest_of(eng, stream, k, i=0, per=6):
        s, n = START[stream] + k, split_index(stream, k)
        eng.wait_ge(S("split", "lead"), i * per + (n + 1))
        eng.tensor_tensor(wsplit[:, n % RING, 1, :], slab(s), wsplit[:, n % RING, 0, :],
                          ALU.subtract).then_inc(S("split", RESTS[stream][0]), 1)

    def slab_split(pe, stream, k, i, per=6):
        which, before = RESTS[stream]
        pe.wait_ge(S("split", which), i * per + (before + k + 1))
        return split_index(stream, k) % RING

    def split_project(pe, dst, stream, k, i=0, per=6, pre=None):
        n = slab_split(pe, stream, k, i, per)
        for c in range(KC):
            if pre is not None and c % 2 == 0:
                wait_h_split(pe, pre, c // 2 + 1)
            for t, (a, b) in enumerate(TERMS):
                mm = pe.matmul(dst, wsplit[:, n, a, c * P:(c + 1) * P], hsplit[:, b, c, :],
                               start=(c == 0 and t == 0), stop=(c == KC - 1 and t == 2))
                if c == 0 and t == 0:
                    mm.then_inc(ring_used, 1)
        return mm

    def split_project_rows(pe, dst, stream, k, i=0, per=6):
        n = slab_split(pe, stream, k, i, per)
        for tt in range(TT):
            for c in range(KC):
                for t, (a, b) in enumerate(TERMS):
                    mm = pe.matmul(dst[:, tt, :], hsplit[:, b, c, tt * P:(tt + 1) * P], wsplit[:, n, a, c * P:(c + 1) * P],
                                   start=(c == 0 and t == 0), stop=(c == KC - 1 and t == 2))
                    if tt == 0 and c == 0 and t == 0:
                        mm.then_inc(ring_used, 1)
        return mm

    def split_output(pe, stream, k, slot, i=0):
        n = slab_split(pe, stream, k, i)
        for j in range(KC):
            for t, (a, b) in enumerate(TERMS):
                mm = pe.matmul(Y[:, j, :], wsplit[:, n, a, j * P:(j + 1) * P], gsplit[:, slot, b, :],
                               start=False, stop=False, skip_group_check=True)
                if j == 0 and t == 0:
                    mm.then_inc(ring_used, 1)

    def gate_vector(v, own, slot, up, sem):
        own(v.tensor_tensor(gated[:, slot, :], act_in[:, slot, :], up, ALU.mult))
        split_hidden_vector(v, own, slot, gated[:, slot, :], sem)

    def split_hidden_vector(v, own, slot, src, sem):
        own(v.tensor_copy(gsplit[:, slot, 0, :], src))
        v.tensor_tensor(gsplit[:, slot, 1, :], src, gsplit[:, slot, 0, :], ALU.subtract).then_inc(sem, 1)

    HSPLITS = ("n1", "n3", "n4", "n5")

    def lead_h_scalar(act, st):
        for c in range(0, KC, 2):
            wait_h(act, st, c + 2)
            act.activation(hsplit[:, 0, c:c + 2, :], hT[:, c:c + 2, :], ACT.Copy).then_inc(S("split", "h_lead"), 1)

    def rest_h_vector(v, st, c):
        v.wait_ge(S("split", "h_lead"), HSPLITS.index(st) * 4 + c // 2 + 1)
        v.tensor_tensor(hsplit[:, 1, c:c + 2, :], hT[:, c:c + 2, :], hsplit[:, 0, c:c + 2, :],
                        ALU.subtract).then_inc(S("split", "h_rest"), 1)

    def wait_h_split(pe, st, steps=4):
        pe.wait_ge(S("split", "h_rest"), HSPLITS.index(st) * 4 + steps)

    def out_project(pe, s0, src, dst, sem):
        for j in range(KC):
            project(pe, dst[:, j, :], s0 + j, src).then_inc(sem, 1)

    NORMS = ("n0", "p0", "n1", "p1", "n2", "p2", "n3", "p3", "n4", "n5", "n6")

    def nth(st, kind=""):
        return sum(x.startswith(kind) for x in NORMS[:NORMS.index(st)])

    def own_steps(st):
        return nth(st, "n") + nth(st, "p") * (KC // 2 + 1)

    def wait_h(eng, st, k=KC):
        eng.wait_ge(S("norm", "h"), KC * nth(st, "n") + k)

    def norm_scalar(act, st, src, ready, base, each, bank=7, leads=None, leads_at=3):
        for g in range(KC // 2):
            if g == leads_at and leads is not None:
                lead_scalar(act, leads, 0)
                lead_scalar(act, leads, 1)
            if g == 0 or each:
                act.wait_ge(ready, base + g * each)
            act.activation(sq[:, 2 * g:2 * g + 2, :], src[:, 2 * g:2 * g + 2, :], ACT.Square).then_inc(S("norm", "squares"), 1)
        act.wait_ge(S("norm", "sums"), nth(st) + 1)
        act.activation(root, ps[:, bank, 0:T], ACT.Sqrt, scale=1.0 / D, bias=eps_col).then_inc(S("norm", "root"), 1)

    def norm_tensor(pe, st, bank=7):
        for k in range(KC):
            if k % 2 == 0:
                pe.wait_ge(S("norm", "squares"), nth(st) * (KC // 2) + k // 2 + 1)
            mm = pe.matmul(ps[:, bank, 0:T], ones[:, :], sq[:, k, :], start=(k == 0), stop=(k == KC - 1))
        mm.then_inc(S("norm", "sums"), 1)

    def pre_norm_vector(v, st, g):
        own = Own(v, S("norm", "own"), base=own_steps(st))
        v.wait_ge(S("norm", "root"), nth(st) + 1)
        own(v.reciprocal(rinv, root))
        for c in range(KC):
            v.scalar_tensor_tensor(hT[:, c, :], xT[:, c, :], gain(g, c), rinv, ALU.mult,
                                   ALU.mult).then_inc(S("norm", "h"), 1)
            if st in HSPLITS and c % 2 and c > 1:
                rest_h_vector(v, st, c - 3)
        if st in HSPLITS:
            rest_h_vector(v, st, KC - 2)

    def post_norm_vector(v, st, g, rests=None):
        if rests is not None:
            rest_of(v, rests, 0)
            rest_of(v, rests, 1)
        own = Own(v, S("norm", "own"), base=own_steps(st))
        v.wait_ge(S("norm", "root"), nth(st) + 1)
        own(v.reciprocal(rinv, root))
        for c in range(0, KC, 2):
            v.scalar_tensor_tensor(sq[:, c, :], Y[:, c, :], gain(g, c), rinv, ALU.mult, ALU.mult)
            own(v.scalar_tensor_tensor(sq[:, c + 1, :], Y[:, c + 1, :], gain(g, c + 1), rinv, ALU.mult, ALU.mult))
            v.tensor_tensor(xT[:, c:c + 2, :], xT[:, c:c + 2, :], sq[:, c:c + 2, :], ALU.add).then_inc(S("norm", "x"), 1)

    def ffn_tensor(pe, layer, pre):
        stream = f"ffn{layer}"
        wait_h(pe, pre, 1)
        for y in range(4):
            pe.matmul(ps[:, y, :], zeros[:, :], zero_rows(), start=True, stop=False, skip_group_check=True)
        with pe.Fori(0, FC // 2) as i:
            for u in range(2):
                split_project(pe, ps[:, 4 + u, 0:T], stream, 2 * u, i, pre=pre)
                split_project(pe, ps[:, 4 + u, T:2 * T], stream, 2 * u + 1, i).then_inc(S("ffn", "gate_up"), 1)
            for u in range(2):
                pe.wait_ge(S("ffn", "act"), i * 2 + (layer * FC + u + 1))
                split_output(pe, stream, 4 + u, u, i)
        for y in range(4):
            mm = pe.matmul(ps[:, y, :], zeros[:, :], zero_rows(), start=False, stop=True, skip_group_check=True)
        mm.then_inc(S("ffn", "y"), 1)

    def ffn_turn(layer, i, split, act, last):
        for k in (2, 3):
            split(k, i)
        act(i, 0)
        for k in (4, 5):
            split(k, i)
        act(i, 1)
        if not last:
            for k in (6, 7):
                split(k, i)

    def ffn_scalar(act, layer, pre):
        lead_h_scalar(act, pre)

        def split(k, i=0):
            lead_scalar(act, f"ffn{layer}", k, i)

        def silu(i, u):
            act.wait_ge(S("ffn", "gate_up"), i * 2 + (layer * FC + u + 1))
            act.activation(act_in[:, u, :], ps[:, 4 + u, 0:T], ACT.Silu).then_inc(S("ffn", "silu"), 1)
        with act.Fori(0, FC // 2 - 1) as i:
            ffn_turn(layer, i, split, silu, False)
        ffn_turn(layer, FC // 2 - 1, split, silu, True)

    def ffn_vector(v, layer):
        def split(k, i=0):
            rest_of(v, f"ffn{layer}", k, i)

        def turn(i, last):
            own = Own(v, S("ffn", "own"), i, 4, layer * (FC // 2) * 4)

            def gate(i, u):
                v.wait_ge(S("ffn", "silu"), i * 2 + (layer * FC + u + 1))
                gate_vector(v, own, u, ps[:, 4 + u, T:2 * T], S("ffn", "act"))
            ffn_turn(layer, i, split, gate, last)
            own.end()
        with v.Fori(0, FC // 2 - 1) as i:
            turn(i, False)
        turn(FC // 2 - 1, True)

    SEGS = ((1, 0, T), (0, T, P))
    pos[0] = era
    attnT = carve(KC, T)
    qk_raw, qk_turn, qk_tmp = carve(2, T), carve(2, T), carve(2, T)
    vrows = carve(TT, P)
    sc_sb, pr = carve(2, 2, 384), carve(2, 2, 384)
    prT = carve(2, 2, 384)
    top, ntop, total, scale_ = carve(8), carve(8), carve(8), carve(8)
    logit, labs, lexp, lln, lf, csum = (carve(T) for _ in range(6))
    gates = carve(TT, 24)
    shared = pos[0]
    bias_q, bias_k = carve(8, T), carve(8, T)
    pos[0] = shared
    nraw, nrope = carve(4, 2 * T), carve(4, 2 * T)
    vcomp_raw = carve(2, T)
    nv = carve(4, P)
    Xk, Xv = carve(16, 2, NC), carve(16, 2, NC)
    hid, hidT = carve(2, T), carve(4, 32)
    kcT, vcmp = carve(16), carve(HD)
    cs, cp = carve(4, 16), carve(TT, 2, 32)
    ctop, csumc, cscale = carve(4), carve(4), carve(4)
    pcT = carve(T)
    att_end = pos[0]
    causal = table("causal").unsqueeze(1).to_broadcast([P, 2, 384])
    cos2 = table("cos").rearrange("p (a t) -> p a t", a=2)
    sin2 = table("sin").rearrange("p (a t) -> p a t", a=2)

    def scores_tensor(pe, q, k, bank0, bias=None):
        for hh in range(2):
            h_ = slice(HD * hh, HD * hh + HD)
            for tt, c0, keys in SEGS:
                dst = ps[:, bank0 + hh, c0:c0 + keys]
                mm = pe.matmul(dst, q[h_, tt * P:(tt + 1) * P], k[h_, 0:keys], start=True, stop=bias is None)
                if bias is not None:
                    head = bias * 2 + hh
                    mm = pe.matmul(dst, bias_q[0:16, head, tt * P:(tt + 1) * P], bias_k[0:16, head, 0:keys],
                                   start=False, stop=True)
        return mm

    def turn_probs_tensor(pe, br, bank0):
        for hh in range(2):
            for c_out, c_in in ((0, T), (P, 0), (T, P)):
                mm = pe.transpose(ps[:, bank0 + hh, c_out:c_out + P], pr[:, br, hh, c_in:c_in + P], eye)
        return mm

    def values_tensor(pe, br, v0, v1, first, last):
        for hh in range(2):
            h_ = slice(HD * hh, HD * hh + HD)
            pe.matmul(ps[h_, 7, 0:T], v0[:, h_], prT[:, br, hh, 0:T], start=first, stop=False)
            mm = pe.matmul(ps[h_, 7, P:T], v1[:, h_], prT[:, br, hh, T:T + P], start=False, stop=last)
        return mm

    BEFORE = {"fox": 0, "moba": 4}

    def pair_tensor(pe, st, s0, i, u, last, rope):
        n = i * 2 + u
        m = i * 2 + (u + BEFORE[st])
        if rope:
            pe.wait_ge(S("pair", "qk_sb"), m + 1)
            pe.matmul(ps[:, 2, :], table("rot"), qk_raw[:, :, :].rearrange("p a t -> p (a t)"), start=True,
                      stop=True).then_inc(S(st, "turned"), 1)
        project_rows(pe, ps[:, 1, 0:T].rearrange("p (a c) -> p a c", a=TT), s0 + 3 * u + 2, hT, i,
                     6).then_inc(S("pair", "v"), 1)
        pe.wait_ge(S(st, "qk_turn") if rope else S("pair", "qk_sb"), (n if rope else m) + 1)
        scores_tensor(pe, qk_turn[:, 0, :], qk_turn[:, 1, :], 3, None if rope else n).then_inc(S("pair", "scores"), 1)
        if not last:
            query_key_tensor(pe, st, s0 + 3 * (u + 1), i)
        pe.wait_ge(S("pair", "probs"), m + 1)
        turn_probs_tensor(pe, 0, 5).then_inc(S("pair", "probsT"), 1)
        pe.wait_ge(S("pair", "v_sb"), m + 1)
        pe.wait_ge(S("pair", "probsT_sb"), m + 1)
        values_tensor(pe, 0, vrows[:, 0, :], vrows[:, 1, :], True, True).then_inc(S("pair", "o"), 1)

    def query_key_tensor(pe, st, s, i):
        project(pe, ps[:, 0, 0:T], s, hT, i, 6)
        project(pe, ps[:, 0, T:2 * T], s + 1, hT, i, 6).then_inc(S("pair", "qk"), 1)

    def query_key_scalar(act, st, n, rope):
        m = n + BEFORE[st]
        act.wait_ge(S("pair", "qk"), m + 1)
        if rope:
            act.activation(qk_raw[:, :, :].rearrange("p a t -> p (a t)"), ps[:, 0, :], ACT.Copy).then_inc(S("pair", "qk_sb"), 1)
        else:
            act.activation(qk_turn[:, 0, :], ps[:, 0, 0:T], ACT.Copy, scale=HD ** -0.5)
            act.activation(qk_turn[:, 1, :], ps[:, 0, T:2 * T], ACT.Copy).then_inc(S("pair", "qk_sb"), 1)

    def exps_scalar(act, br):
        for hh in range(2):
            for g, (tt, c0, keys) in enumerate(SEGS):
                m = (br * 2 + hh) * 2 + g
                ins = act.activation(pr[:, br, hh, c0:c0 + keys], sc_sb[:, br, hh, c0:c0 + keys], ACT.Exp,
                                     bias=ntop[:, m:m + 1], accum_out=total[:, m:m + 1])
        return ins

    def pair_scalar(act, st, i, u, last, rope, chunk0):
        n = i * 2 + u
        m = i * 2 + (u + BEFORE[st])
        act.wait_ge(S("pair", "v"), m + 1)
        act.activation(vrows[:, :, :].rearrange("p a c -> p (a c)"), ps[:, 1, 0:T], ACT.Copy).then_inc(S("pair", "v_sb"), 1)
        act.wait_ge(S("pair", "tops"), m + 1)
        exps_scalar(act, 0).then_inc(S("pair", "exps"), 1)
        if not last:
            query_key_scalar(act, st, n + 1, rope)
        act.wait_ge(S("pair", "o"), m + 1)
        act.activation(attnT[:, bass.ds(n + chunk0, 1), :].rearrange("p a t -> p (a t)"), ps[:, 7, 0:T],
                       ACT.Copy).then_inc(S("pair", "o_sb"), 1)

    def tops_vector(v, own, br, bank0):
        own(v.tensor_tensor(sc_sb[:, br, :, :], ps[:, bank0:bank0 + 2, 0:384], causal, ALU.add))
        m = 4 * br
        for g, (tt, c0, keys) in enumerate(SEGS):
            ins = v.tensor_reduce(top[:, m + g:m + 4:2], sc_sb[:, br, :, c0:c0 + keys], AX_X, ALU.max)
            own(ins)
        return v.tensor_scalar(ntop[:, m:m + 4], top[:, m:m + 4], -1.0, None, ALU.mult)

    def scale_probs_vector(v, br):
        for hh in range(2):
            for g, (tt, c0, keys) in enumerate(SEGS):
                m = (br * 2 + hh) * 2 + g
                p_ = pr[:, br, hh, c0:c0 + keys]
                ins = v.tensor_scalar(p_, p_, scale_[:, m:m + 1], None, ALU.mult)
        return ins

    def pair_vector(v, st, own, i, u, rope):
        n = i * 2 + u
        m = i * 2 + (u + BEFORE[st])
        if rope:
            v.wait_ge(S(st, "turned"), n + 1)
            own(v.tensor_tensor(qk_turn[:, :, :], qk_raw[:, :, :], cos2, ALU.mult))
            own(v.tensor_tensor(qk_tmp[:, :, :], ps[:, 2, :].rearrange("p (a t) -> p a t", a=2), sin2, ALU.mult))
            v.tensor_tensor(qk_turn[:, :, :], qk_turn[:, :, :], qk_tmp[:, :, :], ALU.add).then_inc(S(st, "qk_turn"), 1)
        v.wait_ge(S("pair", "scores"), m + 1)
        tops_vector(v, own, 0, 3).then_inc(S("pair", "tops"), 1)
        v.wait_ge(S("pair", "exps"), m + 1)
        own(v.reciprocal(scale_[:, 0:4], total[:, 0:4]))
        scale_probs_vector(v, 0).then_inc(S("pair", "probs"), 1)
        v.wait_ge(S("pair", "probsT"), m + 1)
        v.tensor_copy(prT[:, 0, :, :], ps[:, 5:7, 0:384]).then_inc(S("pair", "probsT_sb"), 1)

    def fox_tensor(pe, st, pre, s0):
        pe.wait_ge(S("load", "small"), 16)
        for k in range(KC):
            wait_h(pe, pre, k + 1)
            mm = pe.matmul(ps[0:16, 6, 0:T], small_("wfg")[:, k * 40:k * 40 + 16], hT[:, k, :], start=(k == 0), stop=(k == KC - 1))
        for g, tt in enumerate((1, 0)):
            for k in range(KC):
                mm = pe.matmul(ps[:, 6, T + 32 * g:T + 32 * g + 24], hT[:, k, tt * P:(tt + 1) * P],
                               small_("wfg")[:, k * 40 + 16:k * 40 + 40], start=(k == 0), stop=(k == KC - 1))
        mm.then_inc(S(st, "logits"), 1)
        query_key_tensor(pe, st, s0, 0)
        pe.wait_ge(S(st, "biases"), 1)
        for i in range(2):
            for u in range(2):
                pair_tensor(pe, st, s0, i, u, i == 1 and u == 1, False)

    def fox_scalar(act, st):
        act.wait_ge(S(st, "logits"), 1)
        act.activation(logit[0:16, :], ps[0:16, 6, 0:T], ACT.Identity, bias=small_("bf", 16)).then_inc(S(st, "logit_sb"), 1)
        act.activation(gates[:, :, :], ps[:, 6, T:T + 64].rearrange("p (a c) -> p a c", a=2)[:, :, 0:24], ACT.Sigmoid)
        act.activation(labs[0:16, :], ps[0:16, 6, 0:T], ACT.Abs, bias=small_("bf", 16)).then_inc(S(st, "labs"), 1)
        act.wait_ge(S(st, "labs"), 1)
        act.activation(lexp[0:16, :], labs[0:16, :], ACT.Exp, scale=-1.0).then_inc(S(st, "lexp"), 1)
        act.wait_ge(S(st, "lexp1"), 1)
        act.activation(lln[0:16, :], lexp[0:16, :], ACT.Ln).then_inc(S(st, "lln"), 1)
        query_key_scalar(act, st, 0, False)
        for i in range(2):
            for u in range(2):
                pair_scalar(act, st, i, u, i == 1 and u == 1, False, 0)

    def fox_vector(v, st):
        own = Own(v, S(st, "own"))
        v.wait_ge(S(st, "logit_sb"), 1)
        v.wait_ge(S(st, "lexp"), 1)
        v.tensor_scalar(lexp[0:16, :], lexp[0:16, :], 1.0, None, ALU.add).then_inc(S(st, "lexp1"), 1)
        own(v.tensor_scalar(logit[0:16, :], logit[0:16, :], 0.0, None, ALU.min))
        v.wait_ge(S(st, "lln"), 1)
        own(v.tensor_tensor(lf[0:16, :], logit[0:16, :], lln[0:16, :], ALU.subtract))
        own(v.memset(labs[0:16, :], 1.0))
        own(v.tensor_tensor_scan(csum[0:16, :], labs[0:16, :], lf[0:16, :], 0.0, ALU.mult, ALU.add))
        for h in range(8):
            v.tensor_scalar(bias_q[0:16, h, :], csum[0:16, :], table("cmask", 16)[:, 0:1], table("ebot", 16)[:, h:h + 1],
                            ALU.mult, ALU.add)
            ins = v.tensor_scalar(bias_k[0:16, h, :], csum[0:16, :], table("cmask", 16)[:, 1:2],
                                  table("etop", 16)[:, h:h + 1], ALU.mult, ALU.add)
        ins.then_inc(S(st, "biases"), 1)
        for i in range(2):
            for u in range(2):
                pair_vector(v, st, own, i, u, False)

    def moba_tensor(pe, st, pre, s0):
        wait_h(pe, pre)
        query_key_tensor(pe, st, s0, 0)
        with pe.Fori(0, 3) as i:
            for u in range(2):
                pair_tensor(pe, st, s0, i, u, False, True)
        for u in range(2):
            pair_tensor(pe, st, s0, 3, u, u == 1, True)

    def moba_scalar(act, st):
        query_key_scalar(act, st, 0, True)
        with act.Fori(0, 3) as i:
            for u in range(2):
                pair_scalar(act, st, i, u, False, True, 0)
        for u in range(2):
            pair_scalar(act, st, 3, u, u == 1, True, 0)

    def moba_vector(v, st):
        def turn(i):
            own = Own(v, S(st, "own"), i, 12)
            for u in range(2):
                pair_vector(v, st, own, i, u, True)
            own.end()
        with v.Fori(0, 3) as i:
            turn(i)
        turn(3)

    RAW = (0, "v", 1, 2, 3)

    def nsa_tensor(pe, st, s0):
        def two(bank, s, row):
            project(pe, ps[:, bank, 0:T], s, hT)
            project(pe, ps[:, bank, T:2 * T], s + 1, hT).then_inc(S(st, "raw"), 1)

        def turn(row, bank):
            pe.wait_ge(S(st, "raw_sb"), RAW.index(row) + 1)
            pe.matmul(ps[:, bank, :], table("rot"), nraw[:, row, :], start=True, stop=True).then_inc(S(st, "turned"), 1)

        pe.wait_ge(S("pair", "o_sb"), 4)
        two(0, s0, 0)
        two(1, s0 + 2, "v")
        two(2, s0 + 4, 1)
        turn(0, 6)
        project_rows(pe, ps[:, 3, 0:T].rearrange("p (a c) -> p a c", a=TT), s0 + 6, hT)
        project_rows(pe, ps[:, 3, T:2 * T].rearrange("p (a c) -> p a c", a=TT), s0 + 7, hT).then_inc(S(st, "nv"), 1)
        turn(1, 7)
        two(4, s0 + 8, 2)
        pe.wait_ge(S(st, "rope"), 2)
        two(5, s0 + 10, 3)
        turn(2, 6)
        turn(3, 7)
        for kv, X in ((0, Xk), (1, Xv)):
            pe.wait_ge(S(st, "X"), kv + 1)
            for j in range(16):
                s = s0 + 12 + 4 * kv + j // 4
                if j % 4 == 0:
                    slab_here(pe, s)
                w = slab(s)[:, (j % 4) * T:(j % 4 + 1) * T]
                mm = pe.matmul(ps[0:2 * NC, kv, 0:T], X[:, j, :, :].rearrange("p g c -> p (g c)"), w,
                               start=(j == 0), stop=(j == 15))
                if j % 4 == 0:
                    mm.then_inc(ring_used, 1)
            mm.then_inc(S(st, "hidden"), 1)
        for kv in range(2):
            pe.wait_ge(S(st, "gelu"), kv + 1)
            for kt in range(2):
                c = (kv * 2 + kt) * 32
                mm = pe.transpose(ps[:, 2, c:c + 2 * NC], hid[0:2 * NC, kv, kt * P:(kt + 1) * P], eye[0:2 * NC, 0:2 * NC])
        mm.then_inc(S(st, "hiddenT"), 1)
        pe.wait_ge(S(st, "hiddenT_sb"), 1)
        for g in range(2):
            for kt in range(2):
                pe.matmul(ps[HD * g:HD * g + HD, 3, 0:NC], small_("w2k")[:, kt * HD:(kt + 1) * HD],
                          hidT[:, kt, g * NC:(g + 1) * NC], start=(kt == 0), stop=(kt == 1))
        for g in range(2):
            for kt in range(2):
                mm = pe.matmul(ps[32 * g:32 * g + NC, 3, HD:2 * HD], hidT[:, 2 + kt, g * NC:(g + 1) * NC],
                               small_("w2v")[:, kt * HD:(kt + 1) * HD], start=(kt == 0), stop=(kt == 1))
        mm.then_inc(S(st, "comp"), 1)
        pe.wait_ge(S(st, "comp_sb"), 1)
        pe.wait_ge(S(st, "rope"), 4)
        for j in range(4):
            q = nrope[:, 2 + j // 2, (j % 2) * T:(j % 2 + 1) * T]
            for hh in range(2):
                h_ = slice(HD * hh, HD * hh + HD)
                for g, tt in enumerate((1, 0)):
                    mm = pe.matmul(ps[:, hh, 16 * g:16 * g + NC], q[h_, tt * P:(tt + 1) * P], kcT[h_, 0:NC], start=True, stop=True)
            mm.then_inc(S(st, "cscores"), 1)
            scores_tensor(pe, q, nrope[:, 1, 0:T], 3).then_inc(S(st, "scores"), 1)
            scores_tensor(pe, q, nrope[:, 1, T:2 * T], 5).then_inc(S(st, "scores"), 1)
            pe.wait_ge(S(st, "cprobs"), j + 1)
            for g, tt in enumerate((1, 0)):
                mm = pe.transpose(ps[0:HD, 0, T + tt * P:T + (tt + 1) * P], cp[:, g, :, :].rearrange("p h c -> p (h c)"), eye)
            mm.then_inc(S(st, "cprobsT"), 1)
            for br in range(2):
                pe.wait_ge(S(st, "probs"), 2 * j + br + 1)
                turn_probs_tensor(pe, br, 1 + 2 * br).then_inc(S(st, "probsT"), 1)
            for br in range(2):
                pe.wait_ge(S(st, "probsT_sb"), 2 * j + br + 1)
                if br == 0 and j > 0:
                    pe.wait_ge(S(st, "o_sb"), j)
                values_tensor(pe, br, nv[:, 2 * br, :], nv[:, 2 * br + 1, :], br == 0, False)
            pe.wait_ge(S(st, "cprobsT_sb"), j + 1)
            for hh in range(2):
                mm = pe.matmul(ps[HD * hh:HD * hh + HD, 7, 0:T], vcmp[32 * hh:32 * hh + NC, :],
                               pcT[32 * hh:32 * hh + NC, :], start=False, stop=True)
            mm.then_inc(S(st, "o"), 1)

    def nsa_scalar(act, st):
        def take(row, bank, dst):
            act.wait_ge(S(st, "raw"), RAW.index(row) + 1)
            act.activation(dst, ps[:, bank, :], ACT.Copy).then_inc(S(st, "raw_sb"), 1)

        take(0, 0, nraw[:, 0, :])
        take("v", 1, vcomp_raw[:, :, :].rearrange("p a t -> p (a t)"))
        take(1, 2, nraw[:, 1, :])
        act.wait_ge(S(st, "nv"), 1)
        act.activation(nv[:, :, :].rearrange("p a c -> p (a c)"), ps[:, 3, :], ACT.Copy)
        take(2, 4, nraw[:, 2, :])
        take(3, 5, nraw[:, 3, :])
        for kv in range(2):
            act.wait_ge(S(st, "hidden"), kv + 1)
            act.activation(hid[0:2 * NC, kv, :], ps[0:2 * NC, kv, 0:T], ACT.Gelu_apprx_tanh).then_inc(S(st, "gelu"), 1)
        act.wait_ge(S(st, "comp"), 1)
        act.activation(kcT[:, 0:NC], ps[:, 3, 0:NC], ACT.Copy)
        act.activation(vcmp[0:NC, :], ps[0:NC, 3, HD:2 * HD], ACT.Copy)
        act.activation(vcmp[32:32 + NC, :], ps[32:32 + NC, 3, HD:2 * HD], ACT.Copy).then_inc(S(st, "comp_sb"), 1)
        for j in range(4):
            act.wait_ge(S(st, "ctops"), j + 1)
            act.activation(cs[:, :, 0:NC], cs[:, :, 0:NC], ACT.Exp).then_inc(S(st, "cexps"), 1)
            for br in range(2):
                act.wait_ge(S(st, "tops"), 2 * j + br + 1)
                exps_scalar(act, br).then_inc(S(st, "exps"), 1)
            act.wait_ge(S(st, "cprobsT"), j + 1)
            act.activation(pcT[0:HD, :], ps[0:HD, 0, T:2 * T], ACT.Copy).then_inc(S(st, "cprobsT_sb"), 1)
            act.wait_ge(S(st, "o"), j + 1)
            act.activation(attnT[:, 4 + j, :], ps[:, 7, 0:T], ACT.Copy).then_inc(S(st, "o_sb"), 1)

    def nsa_vector(v, st):
        own = Own(v, S(st, "own"))
        own(v.memset(cp[:, :, :, :], 0.0))

        def rope(row, bank, half):
            v.wait_ge(S(st, "turned"), row + 1)
            co = cos2[:, half:half + 1, :].to_broadcast([P, 2, T])
            si = sin2[:, half:half + 1, :].to_broadcast([P, 2, T])
            y = nrope[:, row, :].rearrange("p (a t) -> p a t", a=2)
            own(v.tensor_tensor(y, nraw[:, row, :].rearrange("p (a t) -> p a t", a=2), co, ALU.mult))
            own(v.tensor_tensor(qk_tmp[:, :, :], ps[:, bank, :].rearrange("p (a t) -> p a t", a=2), si, ALU.mult))
            ins = v.tensor_tensor(y, y, qk_tmp[:, :, :], ALU.add)
            ins.then_inc(S(st, "rope"), 1)
            v.wait_ge(S(st, "rope"), row + 1)

        def unfold(X, src, pe_name):
            for half in range(2):
                for jh in range(2):
                    h_ = slice(HD * half, HD * half + HD)
                    for jj in range(0, 8):
                        j = 8 * jh + jj
                        a = SMALL[pe_name][0] + j
                        ins = v.tensor_scalar(X[h_, j, :, :], strided(src, 2 * j + half, [[T, 2], [16, NC]], HD * half, HD),
                                              sm[h_, a:a + 1], None, ALU.add)
            return ins

        rope(0, 6, 1)
        unfold(Xk, nrope[:, 0, :], "pek").then_inc(S(st, "X"), 1)
        v.wait_ge(S(st, "raw_sb"), RAW.index("v") + 1)
        unfold(Xv, vcomp_raw[:, :, :].rearrange("p a t -> p (a t)"), "pev").then_inc(S(st, "X"), 1)
        rope(1, 7, 1)
        rope(2, 6, 0)
        rope(3, 7, 0)
        v.wait_ge(S(st, "hiddenT"), 1)
        v.tensor_copy(hidT[:, :, 0:2 * NC], ps[:, 2, 0:P].rearrange("p (a c) -> p a c", a=4)[:, :, 0:2 * NC]).then_inc(S(st, "hiddenT_sb"), 1)
        for j in range(4):
            v.wait_ge(S(st, "cscores"), j + 1)
            add_ = table("cmpadd").rearrange("p (a c) -> p a c", a=4)[:, :, 0:NC]
            mul_ = table("cmpmul").rearrange("p (a c) -> p a c", a=4)[:, :, 0:NC]
            c4 = cs[:, :, 0:NC]
            own(v.tensor_tensor(c4.rearrange("p (g h) c -> p g h c", g=2),
                                ps[:, 0:2, 0:32].rearrange("p h (g c) -> p g h c", g=2)[:, :, :, 0:NC],
                                add_.rearrange("p (g h) c -> p g h c", g=2), ALU.add))
            own(v.tensor_reduce(ctop[:, :], c4, AX_X, ALU.max))
            v.tensor_tensor(c4, c4, ctop[:, :].unsqueeze(2).to_broadcast([P, 4, NC]), ALU.subtract).then_inc(S(st, "ctops"), 1)
            for br in range(2):
                v.wait_ge(S(st, "scores"), 2 * j + br + 1)
                tops_vector(v, own, br, 3 + 2 * br).then_inc(S(st, "tops"), 1)
            v.wait_ge(S(st, "cexps"), j + 1)
            own(v.tensor_tensor(c4, c4, mul_, ALU.mult))
            own(v.tensor_reduce(csumc[:, :], c4, AX_X, ALU.add))
            own(v.tensor_scalar(csumc[:, :], csumc[:, :], 1e-30, None, ALU.max))
            own(v.reciprocal(cscale[:, :], csumc[:, :]))
            own(v.tensor_tensor(cscale[:, :].rearrange("p (g h) -> p g h", g=2), cscale[:, :].rearrange("p (g h) -> p g h", g=2),
                                gates[:, :, 2 * j:2 * j + 2], ALU.mult))
            v.tensor_tensor(cp[:, :, :, 0:NC], cs[:, :, 0:NC].rearrange("p (g h) c -> p g h c", g=2),
                            cscale[:, :].rearrange("p (g h) -> p g h", g=2).unsqueeze(3).to_broadcast([P, 2, 2, NC]),
                            ALU.mult).then_inc(S(st, "cprobs"), 1)
            for br in range(2):
                v.wait_ge(S(st, "exps"), 2 * j + br + 1)
                m = scale_[:, 4 * br:4 * br + 4]
                own(v.reciprocal(m, total[:, 4 * br:4 * br + 4]))
                c = 8 * (br + 1) + 2 * j
                own(v.tensor_tensor(m.rearrange("p (h g) -> p g h", g=2), m.rearrange("p (h g) -> p g h", g=2),
                                    gates[:, :, c:c + 2], ALU.mult))
                scale_probs_vector(v, br).then_inc(S(st, "probs"), 1)
            for br in range(2):
                v.wait_ge(S(st, "probsT"), 2 * j + br + 1)
                v.tensor_copy(prT[:, br, :, :], ps[:, 1 + 2 * br:3 + 2 * br, 0:384]).then_inc(S(st, "probsT_sb"), 1)
    pos[0] = era
    w3_sb = carve(2 * D)
    decay_sb = carve(2 * D)
    farg, fk, fred, fhid = carve(T), carve(T), carve(T), carve(T)
    fwin, ftaps = carve(2, 2, 512), carve(2, 2, 512)
    MAGIC = 12582912.0
    TAU1 = 6.28125
    TAU2 = float(np.float32(np.round((2 * np.pi - TAU1) * 2 ** 20) / 2 ** 20))
    TAU3 = float(np.float32(2 * np.pi - TAU1 - TAU2))

    def filters_tensor(pe, st):
        pe.wait_ge(S("load", "small"), 16)
        pe.wait_ge(S("load", "tables"), 16)
        pe.matmul(ps[0:64, 0, 0:T], small_("fw1", 33), table("zT", 33), start=True, stop=True).then_inc(S(st, "pre"), 1)
        pe.wait_ge(S(st, "hid"), 1)
        pe.matmul(ps[0:64, 1, 0:T], small_("fw2", 64), fhid[0:64, :], start=True, stop=True).then_inc(S(st, "pre"), 1)
        pe.wait_ge(S(st, "hid"), 2)
        pe.wait_ge(S("load", "w3"), 16)
        for n in range(4):
            pt, half = n // 2, n % 2
            if n > 1:
                pe.wait_ge(S(st, "taps"), n - 1)
            for d in range(2):
                c = d * D + half * 512
                mm = pe.matmul(ps[:, 2 + 2 * (n % 2) + d, :], fhid[0:64, pt * P:(pt + 1) * P], w3_sb[0:64, c:c + 512],
                               start=True, stop=True)
            mm.then_inc(S(st, "filt"), 1)

    def filters_scalar(act, st):
        for n in range(2):
            act.wait_ge(S(st, "reduced"), n + 1)
            act.activation(fhid[0:64, :], fred[0:64, :], ACT.Sin).then_inc(S(st, "hid"), 1)
        act.wait_ge(S("load", "decay"), 16)
        act.activation(decay_sb, decay_sb, ACT.Abs).then_inc(S(st, "decay"), 1)
        act.wait_ge(S(st, "decay"), 1)
        for n in range(4):
            pt, half = n // 2, n % 2
            if n > 1:
                act.wait_ge(S(st, "taps"), n - 1)
            act.activation(fwin[:, n % 2, :, :], decay_sb.rearrange("p (d c) -> p d c", d=2)[:, :, half * 512:(half + 1) * 512],
                           ACT.Exp, scale=table("ntap")[:, pt:pt + 1]).then_inc(S(st, "window"), 1)

    def filters_vector(v, st):
        own = Own(v, S(st, "own"))
        for n in range(2):
            v.wait_ge(S(st, "pre"), n + 1)
            fv = small_("fvec", 64)
            own(v.tensor_scalar(farg[0:64, :], ps[0:64, n, 0:T], fv[:, 2 * n:2 * n + 1], fv[:, 2 * n + 1:2 * n + 2],
                                ALU.add, ALU.mult))
            own(v.tensor_scalar(fk[0:64, :], farg[0:64, :], 1 / (2 * np.pi), MAGIC, ALU.mult, ALU.add))
            own(v.tensor_scalar(fk[0:64, :], fk[0:64, :], -MAGIC, None, ALU.add))
            for tau in (TAU1, TAU2, TAU3):
                own(v.scalar_tensor_tensor(farg[0:64, :], fk[0:64, :], -tau, farg[0:64, :], ALU.mult, ALU.add))
            v.tensor_scalar(fred[0:64, :], farg[0:64, :], 3.1415925, -3.1415925, ALU.min,
                            ALU.max).then_inc(S(st, "reduced"), 1)
        for n in range(4):
            pt, half = n // 2, n % 2
            v.wait_ge(S(st, "window"), n + 1)
            v.wait_ge(S(st, "filt"), n + 1)
            if n > 1:
                v.wait_ge(S(st, "taps"), n - 1)
            ftap = ftaps[:, n % 2, :, :]
            w0, w1 = fwin[:, n % 2, 0, :], fwin[:, n % 2, 1, :]
            f0, f1 = ps[:, 2 + 2 * (n % 2), :], ps[:, 3 + 2 * (n % 2), :]
            own(v.tensor_tensor(ftap[:, 0, :], f0, w0, ALU.mult))
            own(v.scalar_tensor_tensor(ftap[:, 1, :], f1, table("tapmask")[:, pt:pt + 1], w1, ALU.mult, ALU.mult))
            own(v.tensor_tensor(filt_sum[:, pt, half * 512:(half + 1) * 512], ftap[:, 0, :], ftap[:, 1, :], ALU.add))
            v.tensor_tensor(filt_dif[:, pt, half * 512:(half + 1) * 512], ftap[:, 0, :], ftap[:, 1, :],
                            ALU.subtract).then_inc(S(st, "taps"), 1)
        v.wait_ge(S(st, "taps"), 4)

    pos[0] = era
    oall, silu_og, gate_a, gate_b, yb, merged = (carve(HH, T) for _ in range(6))
    sig_q, sig_og, qh, ksum = (carve(T) for _ in range(4))
    sig_f, sig_n = carve(2, T), carve(2, T)
    forget = carve(3, T)
    qa, kb = carve(2, T), carve(2, T)
    totals = [forget.rearrange("p a t -> p (a t)")] + [carve(3 * (T >> l)) for l in range(1, LEVELS)]
    kmix = carve(T)
    sT = carve(TT, T)
    hv = carve(TT, P)
    lbd, lbe, lbs, lb, oml = carve(2, HH), carve(2, HH), carve(HH), carve(HH), carve(HH)
    diag = strided(sT, 0, [[T + P, 2], [1, P]])

    def halves(v, h, off, n):
        return strided(v, off, [[2 * h, n], [T + h, 2], [1, h]])

    def mix_keys(v, h):
        n = T // (2 * h)
        return v.tensor_copy(strided(kmix, 0, [[2 * h, n], [h, 2], [1, h]]), halves(kb, h, 0, n))

    def hgrn_slab(pe, st, s, k, i):
        if k == 3:
            return split_project_rows(pe, ps[:, 1, T:2 * T].rearrange("p (a c) -> p a c", a=TT), st, s + 3,
                                      i).then_inc(S(st, "in1"), 1)
        mm = split_project(pe, ps[:, k // 2, (k % 2) * T:(k % 2 + 1) * T], st, s + k, i,
                           pre="n4" if s + k == 0 else None)
        if k in (1, 5):
            mm.then_inc(S(st, f"in{k // 2}"), 1)

    def hgrn_head_tensor(pe, st, i, last):
        pe.wait_ge(S(st, "prep"), i + 1)
        pe.wait_ge(S(st, "staged"), i + 1)
        for k in range(LEVELS + 2):
            dst = ps[:, 3 + 2 * (k % 2), 0:T].rearrange("p (a c) -> p a c", a=2)
            if k >= 2:
                pe.wait_ge(S(st, "grown"), i * LEVELS + (k - 1))
            for a in range(2):
                if k == 0:
                    mm = pe.matmul(dst[:, a, :], ksum[:, a * P:(a + 1) * P], qh[:, a * P:(a + 1) * P], start=True, stop=True)
                elif k <= LEVELS:
                    h = 1 << (k - 1)
                    mm = pe.matmul(dst[:, a, :], kmix[:, a * P:(a + 1) * P], halves(qa, h, a * P, P // (2 * h)),
                                   start=True, stop=True)
                else:
                    mm = pe.matmul(dst[:, a, :], kb[:, a, a * P:(a + 1) * P], qa[:, 1 - a, (1 - a) * P:(2 - a) * P],
                                   start=True, stop=True)
            mm.then_inc(S(st, "level"), 1)
            if not last and 1 <= k <= 6:
                if k == 3:
                    pe.wait_ge(S(st, "v_sb"), i + 1)
                hgrn_slab(pe, st, 6, k - 1, i)
        pe.wait_ge(S(st, "scores"), i + 1)
        pe.wait_ge(S(st, "v_sb"), i + 1)
        for a in range(TT):
            mm = pe.matmul(ps[:, 4, 0:T], hv[:, a, :], sT[:, a, :], start=(a == 0), stop=(a == 1))
        mm.then_inc(S(st, "o"), 1)

    def hgrn_tensor(pe, st):
        for k in range(6):
            hgrn_slab(pe, st, 0, k, 0)
        with pe.Fori(0, HH - 1) as i:
            hgrn_head_tensor(pe, st, i, False)
        hgrn_head_tensor(pe, st, HH - 1, True)

    def hgrn_stage_scalar(act, st, n, s, i):
        lead_scalar(act, st, s + 2, i)
        lead_scalar(act, st, s + 3, i)
        act.wait_ge(S(st, "in0"), n + 1)
        act.activation(sig_q[:, :], ps[:, 0, 0:T], ACT.Sigmoid)
        act.activation(sig_f[:, 1, :], ps[:, 0, T:2 * T], ACT.Sigmoid)
        act.activation(sig_n[:, 0, :], ps[:, 0, T:2 * T], ACT.Sigmoid, scale=-1.0)
        lead_scalar(act, st, s + 4, i)
        lead_scalar(act, st, s + 5, i)
        act.wait_ge(S(st, "in1"), n + 1)
        act.activation(sig_f[:, 0, :], ps[:, 1, 0:T], ACT.Sigmoid)
        act.activation(sig_n[:, 1, :], ps[:, 1, 0:T], ACT.Sigmoid, scale=-1.0).then_inc(S(st, "gates"), 1)
        act.wait_ge(S(st, "in2"), n + 1)
        act.activation(sig_og[:, :], ps[:, 2, 0:T], ACT.Sigmoid)
        act.activation(gate_a[:, bass.ds(n, 1), :].rearrange("p a t -> p (a t)"), ps[:, 2, T:2 * T],
                       ACT.Sigmoid).then_inc(S(st, "staged"), 1)
        lead_scalar(act, st, s + 6, i)
        lead_scalar(act, st, s + 7, i)

    def hgrn_value_scalar(act, st):
        act.activation(hv[:, :, :].rearrange("p a c -> p (a c)"), ps[:, 1, T:2 * T], ACT.Copy).then_inc(S(st, "v_sb"), 1)

    def hgrn_out_scalar(act, st, n):
        act.wait_ge(S(st, "o"), n + 1)
        act.activation(oall[:, bass.ds(n, 1), :].rearrange("p a t -> p (a t)"), ps[:, 4, 0:T], ACT.Copy).then_inc(S(st, "o_sb"), 1)

    def hgrn_scalar(act, st):
        act.wait_ge(S(st, "lbd"), 1)
        act.activation(lbe[:, :, :], lbd[:, :, :], ACT.Exp).then_inc(S(st, "lbe"), 1)
        hgrn_stage_scalar(act, st, 0, 0, 0)
        hgrn_value_scalar(act, st)
        with act.Fori(0, HH - 1) as i:
            hgrn_stage_scalar(act, st, i + 1, 6, i)
            hgrn_out_scalar(act, st, i)
            hgrn_value_scalar(act, st)
        hgrn_out_scalar(act, st, HH - 1)

    def hgrn_gates_vector(v, st, n):
        v.wait_ge(S(st, "gates"), n + 1)
        l_, m_ = lb[:, bass.ds(n, 1)], oml[:, bass.ds(n, 1)]
        v.tensor_tensor(qh[:, :], ps[:, 0, 0:T], sig_q[:, :], ALU.mult)
        v.tensor_scalar(forget[:, 0:2, :], sig_f[:, :, :], m_, l_, ALU.mult, ALU.add)
        v.tensor_scalar(forget[:, 2, :], sig_f[:, 0, :], m_, l_, ALU.mult, ALU.add).then_inc(S(st, "forget"), 1)
        v.wait_ge(S(st, "forget"), n + 1)

    def hgrn_head_vector(v, st, i, last):
        own = Own(v, S(st, "own"), i, 3 + LEVELS)
        m_ = oml[:, bass.ds(i, 1)]
        own(v.tensor_scalar(kb[:, :, :], sig_n[:, :, :], m_, None, ALU.mult))
        mix_keys(v, 1)
        own(v.tensor_tensor(ksum[:, :], kb[:, 0, :], kb[:, 1, :], ALU.add))
        v.tensor_tensor(qa[:, :, :], forget[:, 0:2, :], qh[:, :].unsqueeze(1).to_broadcast([P, 2, T]),
                        ALU.mult).then_inc(S(st, "prep"), 1)
        v.wait_ge(S(st, "staged"), i + 1)
        own(v.tensor_tensor(silu_og[:, bass.ds(i, 1), :].rearrange("p a t -> p (a t)"), ps[:, 2, 0:T], sig_og[:, :], ALU.mult))
        v.wait_ge(S(st, "level"), i * (LEVELS + 2) + 1)
        own(v.tensor_tensor(diag, ps[:, 3, 0:T].rearrange("p (a c) -> p a c", a=2), eye.unsqueeze(1).to_broadcast([P, 2, P]), ALU.mult))
        for l in range(LEVELS):
            h = 1 << l
            n, nt = T // (2 * h), T // h
            bank = 3 + 2 * ((l + 1) % 2)
            v.wait_ge(S(st, "level"), i * (LEVELS + 2) + (l + 2))
            t_ = totals[l]
            q_, k_ = (strided(x_, 0, [[T + h, 2], [2 * h, n], [1, h]]) for x_ in (qa, kb))
            v.tensor_tensor(q_, q_, strided(t_, 1, [[nt - 1, 2], [2, n], [0, h]]), ALU.mult)
            v.copy_predicated(diag, level_masks[:, l, :].unsqueeze(1).to_broadcast([P, 2, P]),
                              ps[:, bank, 0:T].rearrange("p (a c) -> p a c", a=2))
            ins = v.tensor_tensor(k_, k_, strided(t_, nt + 1, [[nt - 1, 2], [2, n], [0, h]]), ALU.mult)
            if l == LEVELS - 2 and not last:
                hgrn_gates_vector(v, st, i + 1)
            if l < LEVELS - 1:
                own(v.tensor_tensor(strided(totals[l + 1], 0, [[n, 3], [1, n]]), strided(t_, 0, [[nt, 3], [2, n]]),
                                    strided(t_, 1, [[nt, 3], [2, n]]), ALU.mult))
                ins = mix_keys(v, 2 * h)
            ins.then_inc(S(st, "grown"), 1)
        v.wait_ge(S(st, "level"), i * (LEVELS + 2) + (LEVELS + 2))
        v.tensor_copy(strided(sT, P, [[1, T]]), ps[:, 3 + 2 * ((LEVELS + 1) % 2), 0:T]).then_inc(S(st, "scores"), 1)
        own.end()

    def hgrn_vector(v, st):
        pre = Own(v, S(st, "lb"))
        l2 = small_("lbl").rearrange("p (a h) -> p a h", a=2)
        pre(v.tensor_tensor(lbs[:, :], l2[:, 0, :], l2[:, 1, :], ALU.max))
        v.tensor_tensor(lbd[:, :, :], l2, lbs[:, :].unsqueeze(1).to_broadcast([P, 2, HH]), ALU.subtract).then_inc(S(st, "lbd"), 1)
        v.wait_ge(S(st, "lbe"), 1)
        pre(v.tensor_tensor(lbs[:, :], lbe[:, 0, :], lbe[:, 1, :], ALU.add))
        pre(v.reciprocal(lbs[:, :], lbs[:, :]))
        pre(v.tensor_tensor(lb[:, :], lbe[:, 0, :], lbs[:, :], ALU.mult))
        pre(v.tensor_scalar(oml[:, :], lb[:, :], -1.0, 1.0, ALU.mult, ALU.add))
        hgrn_gates_vector(v, st, 0)
        with v.Fori(0, HH - 1) as i:
            hgrn_head_vector(v, st, i, False)
        hgrn_head_vector(v, st, HH - 1, True)

    def hgrn_norm_tensor(pe, st):
        pe.wait_ge(S(st, "squares"), 1)
        pe.wait_ge(S("hyena", "yspecT_sb"), HH)
        pe.wait_ge(S("hyena", "own"), KC * 3)
        pe.wait_ge(S("hyena", "gate_b"), HH)
        for c in range(4):
            mm = pe.matmul(ps[:, 4 + c, :], ones[:, :], sq[:, 2 * c:2 * c + 2, :].rearrange("p a t -> p (a t)"), start=True, stop=True)
        mm.then_inc(S(st, "sums"), 1)

    def hgrn_norm_vector(v, st):
        own = Own(v, S(st, "own"))
        v.wait_ge(S(st, "root"), 1)
        own(v.reciprocal(merged[:, :, :], merged[:, :, :]))
        f = lambda z: z[:, :, :].rearrange("p a t -> p (a t)")
        own(v.scalar_tensor_tensor(f(oall), f(oall), small_("hg"), f(merged), ALU.mult, ALU.mult))
        v.tensor_tensor(f(oall), f(oall), f(silu_og), ALU.mult).then_inc(S(st, "o"), 1)

    pos[0] = era + 6 * HH * T
    hy = carve(3, T + 2)
    u = carve(T)
    a_, n_ = TABLE["cos"]
    odd = tab[:, a_:a_ + 4 * T].rearrange("p (a t) -> p a t", t=T)
    even = carve(4, T)
    conv = (even[:, 0:3, :], odd[:, 0:3, :])
    u_bias = (even[:, 3, :], odd[:, 3, :])
    uT = carve(TT, P)
    taps_now = carve(2, 2, P)
    kspec = carve(3, T)
    prod_a, prod_b = carve(2, T), carve(2, T)
    yspec = carve(4, P)
    yspecT = carve(4, P)
    conv_y = carve(T)
    dft = table("dft").rearrange("p (a f) -> p a f", a=2)
    idft = table("idft").rearrange("p (a f) -> p a f", a=4)

    def hyena_slab(pe, st, s, k, i):
        mm = split_project(pe, ps[:, (0, 0, 1, 7)[k], (k % 2) * T:(k % 2 + 1) * T], "hgrn", N_HGRN + s + k, i, 12)
        if k:
            mm.then_inc(S(st, f"in{k - 1}"), 1)

    def hyena_tile_tensor(pe, st, i, u_, last):
        n = i * 3 + u_
        s = 4 * (u_ + 1)
        pe.wait_ge(S(st, "u"), n + 1)
        for a in range(TT):
            mm = pe.transpose(ps[:, 2, a * P:(a + 1) * P], u[:, a * P:(a + 1) * P], eye)
        mm.then_inc(S(st, "uT"), 1)
        if not last:
            hyena_slab(pe, st, s, 0, i)
        pe.wait_ge(S(st, "uT_sb"), n + 1)
        pe.wait_ge(S(st, "taps"), n + 1)
        for a in range(TT):
            pe.matmul(ps[:, 3, :], uT[:, a, :], dft[:, a, :], start=(a == 0), stop=(a == 1))
        for part in range(2):
            for a in range(2):
                mm = pe.matmul(ps[:, 4, part * T:(part + 1) * T], taps_now[:, part, a, :], dft[:, a, part * T:(part + 1) * T],
                               start=(a == 0), stop=(a == 1))
        mm.then_inc(S(st, "spectra"), 1)
        if not last:
            hyena_slab(pe, st, s, 1, i)
            hyena_slab(pe, st, s, 2, i)
        pe.wait_ge(S(st, "yspec"), n + 1)
        for f in range(4):
            mm = pe.transpose(ps[:, 5, f * P:(f + 1) * P], yspec[:, f, :], eye)
        mm.then_inc(S(st, "yspecT"), 1)
        if not last:
            hyena_slab(pe, st, s, 3, i)
        pe.wait_ge(S(st, "yspecT_sb"), n + 1)
        for f in range(4):
            mm = pe.matmul(ps[:, 6, 0:T], yspecT[:, f, :], idft[:, f, :], start=(f == 0), stop=(f == 3))
        mm.then_inc(S(st, "conv"), 1)

    def hyena_tensor(pe, st):
        pe.wait_ge(S("hgrn", "o_sb"), HH)
        for k in range(4):
            hyena_slab(pe, st, 0, k, 0)
        with pe.Fori(0, 2) as i:
            for u_ in range(3):
                hyena_tile_tensor(pe, st, i, u_, False)
        hyena_tile_tensor(pe, st, 2, 0, False)
        hyena_tile_tensor(pe, st, 2, 1, True)
        hgrn_norm_tensor(pe, "hnorm")

    def hyena_stage_scalar(act, st, n, part):
        act.wait_ge(S(st, f"in{part}"), n + 1)
        if part == 0:
            act.activation(hy[:, 0:2, 1:T + 1], ps[:, 0, :].rearrange("p (a t) -> p a t", a=2), ACT.Copy)
        if part == 1:
            act.activation(hy[:, 2, 1:T + 1], ps[:, 1, 0:T], ACT.Copy).then_inc(S(st, "staged"), 1)
        if part == 2:
            act.activation(gate_b[:, bass.ds(n, 1), :].rearrange("p a t -> p (a t)"), ps[:, 7, T:2 * T],
                           ACT.Sigmoid).then_inc(S(st, "gate_b"), 1)

    def hyena_scalar(act, st):
        def lead(k):
            lead_scalar(act, "hgrn", N_HGRN + k)

        act.wait_ge(S(st, "pads"), 1)
        for k in (2, 3):
            lead(k)
        hyena_stage_scalar(act, st, 0, 0)
        lead(4)
        hyena_stage_scalar(act, st, 0, 1)
        lead(5)
        hyena_stage_scalar(act, st, 0, 2)
        act.wait_ge(S("hgrn", "o_sb"), HH)
        act.activation(sq[:, :, :], oall[:, :, :], ACT.Square).then_inc(S("hnorm", "squares"), 1)

        def tile(n, turn, u_, more):
            def lead(k):
                if k - 6 < more:
                    lead_scalar(act, "hgrn", N_HGRN + 4 * u_ + k, turn, 12)

            last = more == 0
            act.wait_ge(S(st, "uT"), n + 1)
            act.activation(uT[:, :, :].rearrange("p a c -> p (a c)"), ps[:, 2, 0:T], ACT.Copy).then_inc(S(st, "uT_sb"), 1)
            lead(6)
            act.wait_ge(S(st, "spectra"), n + 1)
            act.activation(kspec[:, 0:2, :].rearrange("p a t -> p (a t)"), ps[:, 4, :], ACT.Copy)
            act.activation(kspec[:, 2, :], ps[:, 4, 0:T], ACT.Copy).then_inc(S(st, "kspec"), 1)
            lead(7)
            if not last:
                hyena_stage_scalar(act, st, n + 1, 0)
                lead(8)
                hyena_stage_scalar(act, st, n + 1, 1)
            act.wait_ge(S(st, "yspecT"), n + 1)
            act.activation(yspecT[:, :, :].rearrange("p a c -> p (a c)"), ps[:, 5, :], ACT.Copy).then_inc(S(st, "yspecT_sb"), 1)
            lead(9)
            if not last:
                hyena_stage_scalar(act, st, n + 1, 2)
        with act.Fori(0, 2) as turn:
            for u_ in range(3):
                tile(turn * 3 + u_, turn, u_, 4)
        tile(6, 2, 0, 2)
        tile(7, 2, 1, 0)
        act.wait_ge(S("hnorm", "sums"), 1)
        act.activation(merged[:, :, :], YB, ACT.Sqrt, scale=1.0 / P, bias=eps_col).then_inc(S("hnorm", "root"), 1)

    def hybrid_gpsimd(pool, st):
        with pool.Fori(0, HH) as i:
            for k in range(6):
                rest_of(pool, "hgrn", k, i)
        for k in range(6):
            rest_of(pool, "hgrn", N_HGRN + k)
        pool.wait_ge(S(st, "pads"), 1)

        def tile(n, turn, u_, more):
            pool.tensor_copy(taps_now[:, 0, :, :], filt_sum[:, :, bass.ds(n * P, P)])
            pool.tensor_copy(taps_now[:, 1, :, :], filt_dif[:, :, bass.ds(n * P, P)]).then_inc(S(st, "taps"), 1)
            for k in range(more):
                rest_of(pool, "hgrn", N_HGRN + 4 * u_ + 6 + k, turn, 12)
            pool.wait_ge(S(st, "spectra"), n + 1)
        with pool.Fori(0, 2) as turn:
            for u_ in range(3):
                tile(turn * 3 + u_, turn, u_, 4)
        tile(6, 2, 0, 2)
        tile(7, 2, 1, 0)

    def hyena_pads_vector(v, st):
        v.memset(hy[:, :, :], 0.0).then_inc(S(st, "pads"), 1)

    def hyena_vector(v, st):
        def gates(n, parity):
            own = Own(v, S(st, "conv_own"), n, 4)
            cv = conv[parity]
            v.wait_ge(S(st, "staged"), n + 1)

            def w(q, j):
                return sm[:, bass.ds(n * 3 + (SMALL["convw"][0] + q * 24 + j), 1)]
            for q in range(3):
                b_ = sm[:, bass.ds(n + (SMALL["convb"][0] + q * KC), 1)]
                ins = v.tensor_scalar(cv[:, q, :], hy[:, q, 1:T + 1], w(q, 1), b_, ALU.mult, ALU.add)
            own(ins)
            for q in range(3):
                ins = v.scalar_tensor_tensor(cv[:, q, :], hy[:, q, 0:T], w(q, 0), cv[:, q, :], ALU.mult, ALU.add)
            own(ins)
            for q in range(3):
                ins = v.scalar_tensor_tensor(cv[:, q, :], hy[:, q, 2:T + 2], w(q, 2), cv[:, q, :], ALU.mult, ALU.add)
            own(ins)
            v.tensor_tensor(u[:, :], cv[:, 2, :], cv[:, 1, :], ALU.mult).then_inc(S(st, "u"), 1)
            v.wait_ge(S(st, "u"), n + 1)
            own(v.tensor_scalar(u_bias[parity], u[:, :], sm[:, bass.ds(n + SMALL["hbias"][0], 1)], None, ALU.mult))
            own.end()

        def tile(n, parity, last):
            own = Own(v, S(st, "own"), n, 3)
            v.wait_ge(S(st, "kspec"), n + 1)
            uspec = ps[:, 3, :].rearrange("p (a t) -> p a t", a=2)
            v.tensor_tensor(prod_a[:, :, :], uspec, kspec[:, 0:2, :], ALU.mult)
            own(v.tensor_tensor(prod_b[:, :, :], uspec, kspec[:, 1:3, :], ALU.mult))
            f = yspec[:, :, :].rearrange("p a c -> p (a c)")
            v.tensor_tensor(f[:, 0:T], prod_a[:, 0, :], prod_a[:, 1, :], ALU.subtract)
            v.tensor_tensor(f[:, T:2 * T], prod_b[:, 0, :], prod_b[:, 1, :], ALU.add).then_inc(S(st, "yspec"), 1)
            if not last:
                gates(n + 1, 1 - parity)
            v.wait_ge(S(st, "conv"), n + 1)
            own(v.tensor_tensor(conv_y[:, :], u_bias[parity], ps[:, 6, 0:T], ALU.add))
            own(v.tensor_tensor(yb[:, bass.ds(n, 1), :].rearrange("p a t -> p (a t)"), conv_y[:, :], conv[parity][:, 0, :],
                                ALU.mult))
            own.end()

        gates(0, 0)
        with v.Fori(0, KC // 2 - 1) as i:
            for parity in range(2):
                tile(i * 2 + parity, parity, False)
        tile(KC - 2, 0, False)
        tile(KC - 1, 1, True)

    def merge_tensor(pe, st, sa, sbb, so):
        pe.wait_ge(S("hyena", "own"), KC * 3)
        out_project(pe, sbb, yb, Y, S(st, "yb"))
        pe.wait_ge(S("hnorm", "o"), 1)
        out_project(pe, sa, oall, YB, S(st, "ya"))
        pe.wait_ge(S(st, "merged"), KC)
        out_project(pe, so, merged, Y, S(st, "y"))

    def merge_vector(v, st):
        own = Own(v, S(st, "own"))
        for j in range(0, KC, 2):
            v.wait_ge(S(st, "yb"), j + 2)
            own(v.tensor_tensor(merged[:, j:j + 2, :], gate_b[:, j:j + 2, :], Y[:, j:j + 2, :], ALU.mult))
        for j in range(0, KC, 2):
            v.wait_ge(S(st, "ya"), j + 2)
            own(v.tensor_tensor(prod_a[:, :, :], gate_a[:, j:j + 2, :], YB[:, j:j + 2, :], ALU.mult))
            v.tensor_tensor(merged[:, j:j + 2, :], merged[:, j:j + 2, :], prod_a[:, :, :], ALU.add).then_inc(S(st, "merged"), 2)
            v.wait_ge(S(st, "merged"), j + 2)
        for j in range(0, KC, 2):
            v.wait_ge(S(st, "y"), j + 2)
            v.tensor_tensor(xT[:, j:j + 2, :], xT[:, j:j + 2, :], Y[:, j:j + 2, :], ALU.add).then_inc(S(st, "x"), 2)
    pos[0] = era
    s_all = carve(TT, 16, NKEYS)
    s_left = carve(NKEYS)
    best = carve(TT, 16, TOPK)
    best_at = carve(TT, 16, TOPK, dt=U32)
    best_key = carve(TT, 16, TOPK)
    cand = carve(TT, 8, TOPK * TOPK)
    c_left = carve(TOPK * TOPK)
    pick_s = carve(TT, 8, TOPK)
    pick_at = carve(TT, 8, TOPK, dt=U32)
    rank_u = carve(2, TT * 8 * TOPK, dt=U32)
    rank = carve(2, TT * 8 * TOPK)
    match = carve(TT * 8 * TOPK, TOPK)
    pick = carve(3, TT, 8 * TOPK)
    psum_ = carve(TT * 8)
    qsb = carve(2, T)
    assert pos[0] <= NKEYS * T
    hots = sq[:, :, :].rearrange("p a t -> p (a t)").rearrange("p (b c k n) -> p b c k n", b=2, c=2, k=4)
    peer_w = work[:, :].rearrange("p (n t) -> p n t", t=T)

    assert EARLY * T <= era and EARLY % 6 == 0

    def pq_tensor(pe, st, pre):
        pe.wait_ge(S("load", "sub"), 16)

        def query(i, u):
            split_project(pe, ps[:, 4 + u % 2, 0:T], st, u, i, pre=pre if u == 0 else None).then_inc(S(st, "q"), 1)

        def score(i, u):
            pe.wait_ge(S(st, "q_sb"), i * 6 + (u + 1))
            for tt in range(TT):
                mm = pe.matmul(ps[:, 6 + u % 2, tt * P:(tt + 1) * P], qsb[:, u % 2, tt * P:(tt + 1) * P],
                               sub[:, bass.ds(i * 6 + u, 1), :].rearrange("p a k -> p (a k)"), start=True, stop=True)
            mm.then_inc(S(st, "s"), 1)

        def turn(i, n):
            query(i, 0)
            for u in range(1, n):
                query(i, u)
                score(i, u - 1)
            score(i, n - 1)
        with pe.Fori(0, 2) as i:
            turn(i, 6)
        turn(2, 4)

    def pq_scalar(act, st):
        def query(i, u):
            lead_scalar(act, st, u + 2, i)
            act.wait_ge(S(st, "q"), i * 6 + (u + 1))
            act.activation(qsb[:, u % 2, :], ps[:, 4 + u % 2, 0:T], ACT.Copy).then_inc(S(st, "q_sb"), 1)

        def score(i, u):
            act.wait_ge(S(st, "s"), i * 6 + (u + 1))
            act.activation(s_all[:, :, bass.ds(i * 6 + u, 1), :].rearrange("p t a k -> p t (a k)"),
                           ps[:, 6 + u % 2, 0:T].rearrange("p (t k) -> p t k", t=TT), ACT.Copy).then_inc(S(st, "s_sb"), 1)

        def turn(i, n):
            query(i, 0)
            for u in range(1, n):
                query(i, u)
                score(i, u - 1)
            score(i, n - 1)
        with act.Fori(0, 2) as i:
            turn(i, 6)
        turn(2, 4)

    def rests_gpsimd(pool, st):
        n = N_PQ // 6
        with pool.Fori(0, n) as i:
            for k in range(6):
                rest_of(pool, st, k, i)
        for k in range(N_PQ - n * 6):
            rest_of(pool, st, k, n)

    def early_tensor(pe, st, stream):
        with pe.Fori(0, EARLY // 6) as i:
            for k in range(6):
                split_project(pe, ps[:, 4 + k % 3, 0:T], stream, 16 + k, i).then_inc(S(st, "hidden"), 1)
        pe.wait_ge(S(st, "gelu"), EARLY)

    def early_scalar(act, st, stream):
        def turn(i, last):
            for k in range(6):
                if not last or k < 4:
                    lead_scalar(act, stream, 18 + k, i)
                act.wait_ge(S(st, "hidden"), i * 6 + (k + 1))
                act.activation(peer_w[:, bass.ds(i * 6 + k, 1), :].rearrange("p a t -> p (a t)"), ps[:, 4 + k % 3, 0:T],
                               ACT.Gelu_apprx_tanh).then_inc(S(st, "gelu"), 1)
        with act.Fori(0, EARLY // 6 - 1) as i:
            turn(i, False)
        turn(EARLY // 6 - 1, True)

    def best16(v, own, values, left, out_v, out_at):
        own(v.max(out=out_v[:, 0:8], in_=values))
        own(v.max_index(out=out_at[:, 0:8], in_max=out_v[:, 0:8], in_values=values))
        own(v.match_replace(out=left, in_to_replace=out_v[:, 0:8], in_values=values, imm_value=-3e38))
        own(v.max(out=out_v[:, 8:16], in_=left))
        own(v.max_index(out=out_at[:, 8:16], in_max=out_v[:, 8:16], in_values=left))

    def picks_vector(v, st):
        own = Own(v, S(st, "own"))
        for hp in range(16):
            v.wait_ge(S("pq", "s_sb"), hp + 1)
            for tt in range(TT):
                best16(v, own, s_all[:, tt, hp, :], s_left[:, :], best[:, tt, hp, :], best_at[:, tt, hp, :])
        own(v.tensor_copy(best_key[:, :, :, :], best_at[:, :, :, :]))
        for tt in range(TT):
            own(v.tensor_tensor(cand[:, tt, :, :].rearrange("p h (a b) -> p h a b", b=TOPK),
                                strided(best, tt * 256, [[32, 8], [1, 16], [0, 16]]),
                                strided(best, tt * 256 + 16, [[32, 8], [0, 16], [1, 16]]), ALU.add))
        for tt in range(TT):
            for h in range(8):
                best16(v, own, cand[:, tt, h, :], c_left[:, :], pick_s[:, tt, h, :], pick_at[:, tt, h, :])
        at = pick_at[:, :, :, :].rearrange("p t h k -> p (t h k)")
        own(v.tensor_scalar(rank_u[:, 0, :], at, 4, None, ALU.logical_shift_right))
        own(v.tensor_scalar(rank_u[:, 1, :], at, 15, None, ALU.bitwise_and))
        own(v.tensor_copy(rank[:, :, :], rank_u[:, :, :]))
        n = TT * 8 * TOPK
        for half in range(2):
            own(v.tensor_tensor(match[:, :, :], strided(rank, half * n, [[1, n], [0, TOPK]]), strided(iota, 0, [[0, n], [1, TOPK]]),
                                ALU.is_equal))
            m4 = strided(match, 0, [[256, 16], [16, 16], [1, 16]])
            own(v.tensor_tensor(m4, m4, strided(best_key, 16 * half, [[32, 16], [0, 16], [1, 16]]), ALU.mult))
            own(v.tensor_reduce(pick[:, half, :, :].rearrange("p t k -> p (t k)"), match[:, :, :], AX_X, ALU.add))
        w4 = pick[:, 2, :, :].rearrange("p t (h k) -> p (t h) k", k=TOPK)
        s4 = pick_s[:, :, :, :].rearrange("p t h k -> p (t h) k")
        v.tensor_tensor(w4, s4, s4[:, :, 0:1].to_broadcast([P, 16, TOPK]), ALU.subtract).then_inc(S(st, "shifted"), 1)
        v.wait_ge(S(st, "exp"), 1)
        own(v.tensor_reduce(psum_[:, :], w4, AX_X, ALU.add))
        own(v.reciprocal(psum_[:, :], psum_[:, :]))
        v.tensor_tensor(w4, w4, psum_[:, :].unsqueeze(2).to_broadcast([P, 16, TOPK]), ALU.mult).then_inc(S(st, "picks"), 1)
        v.wait_ge(S(st, "picksT"), 1)
        v.tensor_copy(picks[:, 0:2, :].rearrange("p a t -> p (a t)"), ps[:, 4, :])
        v.tensor_copy(picks[:, 2, :], ps[:, 5, 0:T]).then_inc(S(st, "picksT_sb"), 1)
        v.wait_ge(S(st, "picksT_sb"), 1)

    def picks_scalar(act, st):
        act.wait_ge(S(st, "shifted"), 1)
        w_ = pick[:, 2, :, :].rearrange("p t k -> p (t k)")
        act.activation(w_, w_, ACT.Exp).then_inc(S(st, "exp"), 1)

    def picks_tensor(pe, st):
        pe.wait_ge(S(st, "picks"), 1)
        for a in range(3):
            for tt in range(TT):
                mm = pe.transpose(ps[:, 4 + a // 2, (a % 2) * T + tt * P:(a % 2) * T + (tt + 1) * P], pick[:, a, tt, :], eye)
        mm.then_inc(S(st, "picksT"), 1)

    BATCHES = T // 4

    def spread(eng, step):
        for u in range(2):
            step(0, u, True)
        with eng.Fori(1, BATCHES // 2) as i:
            for u in range(2):
                step(i, u, False)

    early_weights = eyeiota[:, 0:EARLY * 4].rearrange("p (n k) -> p n k", k=4)

    def spread_gpsimd(pool, st):
        def step(i, u, first):
            pool.wait_ge(S(st, "early_weights"), i * 2 + (u + 1))
            w = peer_w[:, 0:EARLY, bass.ds(i * 8 + u * 4, 4)]
            pool.tensor_tensor(w, w, early_weights, ALU.mult).then_inc(S(st, "early"), 1)
        pool.wait_ge(S("peer", "gelu"), EARLY)
        spread(pool, step)

    def spread_vector(v, st):
        def step(i, u, first):
            if not first:
                v.wait_ge(S(st, "weights"), i * 2 + (u - 1))
            v.tensor_tensor(hots[:, u, 1, :, :], strided(iota, 0, [[0, 4], [1, P]]),
                            picks[:, 1, bass.ds(i * 8 + u * 4, 4)].unsqueeze(2).to_broadcast([P, 4, P]), ALU.is_equal)
            for k in range(4):
                t = i * 8 + (u * 4 + k)
                ins = v.tensor_scalar(hots[:, u, 0, k, :], iota, picks[:, 0, bass.ds(t, 1)], picks[:, 2, bass.ds(t, 1)],
                                      ALU.is_equal, ALU.mult)
            ins.then_inc(S(st, "hot"), 1)
        spread(v, step)

    def spread_tensor(pe, st):
        def step(i, u, first):
            pe.wait_ge(S(st, "hot"), i * 2 + (u + 1))
            if not first:
                pe.wait_ge(S(st, "weights_sb"), i * 2 + (u - 1))
            for k in range(4):
                mm = pe.matmul(ps[:, 6 + u, k * P:(k + 1) * P], hots[:, u, 1, k, :], hots[:, u, 0, k, :], start=True, stop=True)
            mm.then_inc(S(st, "weights"), 1)
        spread(pe, step)

    def spread_scalar(act, st):
        def step(i, u, first):
            act.wait_ge(S(st, "weights"), i * 2 + (u + 1))
            if not (first and u == 0):
                act.wait_ge(S(st, "early"), i * 2 + u)
            act.activation(early_weights, ps[:, 6 + u, :].rearrange("p (k n) -> p n k", k=4)[:, 0:EARLY, :],
                           ACT.Copy).then_inc(S(st, "early_weights"), 1)
            act.activation(peer_w[:, EARLY:NKEYS, bass.ds(i * 8 + u * 4, 4)],
                           ps[:, 6 + u, :].rearrange("p (k n) -> p n k", k=4)[:, EARLY:NKEYS, :],
                           ACT.Copy).then_inc(S(st, "weights_sb"), 1)
        spread(act, step)

    LATE = EARLY + 2
    TURNS = (NKEYS - LATE) // 3
    assert LATE + 3 * TURNS == NKEYS

    def peer_tensor(pe, st):
        def hidden(k, i, slot):
            split_project(pe, ps[:, 4 + slot, 0:T], st, k, i).then_inc(S(st, "hidden"), 1)

        def output(k, i, slot, value):
            pe.wait_ge(S(st, "act"), value)
            split_output(pe, st, k, slot, i)

        for y in range(4):
            pe.matmul(ps[:, y, :], zeros[:, :], zero_rows(), start=True, stop=False, skip_group_check=True)
        pe.wait_ge(S("spread", "weights_sb"), BATCHES)
        with pe.Fori(0, EARLY // 6) as i:
            for k in range(6):
                output(k, i, k % 3, i * 6 + (k + 1))
        hidden(EARLY, 0, 0)
        hidden(EARLY + 1, 0, 1)
        with pe.Fori(0, TURNS) as i:
            for u in range(3):
                output(LATE + 2 * u, i, u, i * 3 + (EARLY + u + 1))
                hidden(LATE + 1 + 2 * u, i, (u + 2) % 3)
        output(LATE, TURNS, 0, NKEYS - 1)
        output(LATE + 1, TURNS, 1, NKEYS)
        for y in range(4):
            mm = pe.matmul(ps[:, y, :], zeros[:, :], zero_rows(), start=False, stop=True, skip_group_check=True)
        mm.then_inc(S(st, "y"), 1)

    def peer_first(split):
        split(0, 0)
        split(1, 0)

    def peer_chunks(eng, split, early_step, step):
        early_step(0, 0)
        with eng.Fori(0, EARLY // 6 - 1) as i:
            for k in range(6):
                early_step(i, k + 1)
                split(2 + k, i)
        for k in range(6):
            if k < 5:
                early_step(EARLY // 6 - 1, k + 1)
            split(2 + k, EARLY // 6 - 1)
        with eng.Fori(0, TURNS) as i:
            for u in range(3):
                step(i, u)
                split(LATE + 2 * u, i)
                split(LATE + 1 + 2 * u, i)
        step(TURNS, 0)
        split(LATE, TURNS)
        split(LATE + 1, TURNS)
        step(TURNS, 1)

    def peer_scalar(act, st):
        def split(k, i):
            lead_scalar(act, st, k, i)

        def step(i, u):
            act.wait_ge(S(st, "hidden"), i * 3 + (EARLY + u + 1))
            act.activation(act_in[:, u, :], ps[:, 4 + u, 0:T], ACT.Gelu_apprx_tanh).then_inc(S(st, "gelu"), 1)
        peer_chunks(act, split, lambda i, k: None, step)

    def peer_vector(v, st):
        def split(k, i):
            rest_of(v, st, k, i)

        def early_step(i, k):
            own = Own(v, S(st, "own"), i, 6, k)
            split_hidden_vector(v, own, k % 3, peer_w[:, bass.ds(i * 6 + k, 1), :].rearrange("p a t -> p (a t)"), S(st, "act"))

        def step(i, u):
            own = Own(v, S(st, "own"), i, 6, EARLY + 2 * u)
            v.wait_ge(S(st, "gelu"), i * 3 + (EARLY + u + 1))
            gate_vector(v, own, u, peer_w[:, bass.ds(i * 3 + (EARLY + u), 1), :].rearrange("p a t -> p (a t)"), S(st, "act"))
        v.wait_ge(S("spread", "early"), BATCHES)
        peer_chunks(v, split, early_step, step)
        v.wait_ge(S(st, "y"), 1)
        for c in range(0, KC, 2):
            v.tensor_tensor(xT[:, c:c + 2, :], xT[:, c:c + 2, :], Y[:, c:c + 2, :], ALU.add).then_inc(S(st, "x"), 1)
    eps_tile = sb("eps_tile", [P, 1])
    eps_col = eps_tile[:, 0:1]
    block = ctx.enter_context(nc.Block())
    B0 = START

    @block.sync
    def _(sp):
        def load(dst, src, name):
            sp.dma_start(dst, src).then_inc(S("load", name), 16)

        def load_slab(s, src):
            sp.dma_start(ring[:, s % RING, :], src).then_inc(landed[s % RING], 16)

        def stream(first, last, sem, ahead):
            end = first + (last - first) // RING * RING
            if end > first:
                with sp.Fori(0, (end - first) // RING) as i:
                    for s in range(first, first + RING):
                        sp.wait_ge(sem, i * RING + (s - ahead))
                        load_slab(s, weights[bass.ds(i * RING + s, 1)].rearrange("a p n -> (a p) n"))
            for s in range(max(end, first), last):
                sp.wait_ge(sem, s - ahead)
                load_slab(s, weights[s])

        load(xT[:, :, :], x, "x")
        load(sm, small, "small")
        load(tab, tables, "tables")
        load(w3_sb[0:64, :], w3, "w3")
        load(decay_sb, bass.AP(decay.tensor, decay.offset, [[0, P], [1, 2 * D]]), "decay")
        for s in range(RING):
            load_slab(s, weights[s])
        load(level_masks, masks, "masks")
        load(sub, subkeys, "sub")
        at = RING
        for name, n in (("ffn0", N_FFN), ("ffn1", N_FFN), ("hgrn", N_HGRN + N_HYENA), ("pq", N_PQ), ("peer", N_PEER)):
            first = min(START[name] + RING, N_SLABS)
            stream(at, first, ring_used, 1)
            at = min(START[name] + RING + n, N_SLABS)
            if at > first:
                which, before = RESTS[name]
                stream(first, at, S("split", which), START[name] + RING - before - 1)
        if at < N_SLABS:
            stream(at, N_SLABS, ring_used, 1)
        wait_h(sp, "n6")
        sp.dma_start(out, hT).then_inc(S("store", "out"), 16)
        sp.wait_ge(S("store", "out"), 16)

    @block.tensor
    def _(pe):
        pe.wait_ge(S("load", "ones"), 1)
        norm_tensor(pe, "n0")
        pe.wait_ge(S("load", "eye"), 1)
        filters_tensor(pe, "filters")
        fox_tensor(pe, "fox", "n0", B0["fox"])
        nsa_tensor(pe, "nsa", B0["nsa"])
        pe.wait_ge(S("nsa", "o_sb"), 4)
        out_project(pe, B0["out0"], attnT, Y, S("out", "y"))
        norm_tensor(pe, "p0")
        norm_tensor(pe, "n1")
        ffn_tensor(pe, 0, "n1")
        norm_tensor(pe, "p1")
        norm_tensor(pe, "n2")
        moba_tensor(pe, "moba", "n2", B0["moba"])
        pe.wait_ge(S("pair", "o_sb"), 4 + 8)
        out_project(pe, B0["out1"], attnT, Y, S("out", "y"))
        norm_tensor(pe, "p2")
        norm_tensor(pe, "n3")
        ffn_tensor(pe, 1, "n3")
        norm_tensor(pe, "p3")
        norm_tensor(pe, "n4")
        hgrn_tensor(pe, "hgrn")
        hyena_tensor(pe, "hyena")
        merge_tensor(pe, "merge", B0["wa"], B0["wb"], B0["out2"])
        norm_tensor(pe, "n5")
        pq_tensor(pe, "pq", "n5")
        early_tensor(pe, "peer", "pq")
        picks_tensor(pe, "picks")
        spread_tensor(pe, "spread")
        peer_tensor(pe, "peer")
        norm_tensor(pe, "n6")

    @block.scalar
    def _(act):
        act.wait_ge(S("load", "ones"), 1)
        norm_scalar(act, "n0", xT, S("load", "x"), 16, 0)
        act.wait_ge(S("load", "tables"), 16)
        filters_scalar(act, "filters")
        act.wait_ge(S("filters", "taps"), 4)
        fox_scalar(act, "fox")
        nsa_scalar(act, "nsa")
        norm_scalar(act, "p0", Y, S("out", "y"), 2, 2, leads="ffn0")
        norm_scalar(act, "n1", xT, S("norm", "x"), 1, 1)
        ffn_scalar(act, 0, "n1")
        norm_scalar(act, "p1", Y, S("ffn", "y"), 1, 0)
        norm_scalar(act, "n2", xT, S("norm", "x"), 5, 1)
        moba_scalar(act, "moba")
        norm_scalar(act, "p2", Y, S("out", "y"), KC + 2, 2, leads="ffn1")
        norm_scalar(act, "n3", xT, S("norm", "x"), 9, 1)
        ffn_scalar(act, 1, "n3")
        norm_scalar(act, "p3", Y, S("ffn", "y"), 2, 0, leads="hgrn", leads_at=0)
        norm_scalar(act, "n4", xT, S("norm", "x"), 13, 1)
        lead_h_scalar(act, "n4")
        hgrn_scalar(act, "hgrn")
        hyena_scalar(act, "hyena")
        norm_scalar(act, "n5", xT, S("merge", "x"), 2, 2, leads="pq")
        lead_h_scalar(act, "n5")
        pq_scalar(act, "pq")
        early_scalar(act, "peer", "pq")
        picks_scalar(act, "picks")
        peer_first(lambda k, i: lead_scalar(act, "peer", k, i))
        spread_scalar(act, "spread")
        peer_scalar(act, "peer")
        norm_scalar(act, "n6", xT, S("peer", "x"), 1, 1)

    @block.vector
    def _(v):
        v.memset(ones[:, :], 1.0)
        v.memset(zeros[:, :], 0.0)
        v.memset(eps_tile[:, :], EPS).then_inc(S("load", "ones"), 1)
        v.wait_ge(S("load", "small"), 16)
        v.tensor_copy(gains_sb[:, :], small_("gains")).then_inc(S("load", "gains"), 1)
        v.wait_ge(S("load", "gains"), 1)
        pre_norm_vector(v, "n0", G_MIX_PRE)
        v.wait_ge(S("load", "tables"), 16)
        v.tensor_copy(eyeiota[:, :], tab[:, 0:2 * P]).then_inc(S("load", "eye"), 1)
        v.wait_ge(S("load", "eye"), 1)
        filters_vector(v, "filters")
        fox_vector(v, "fox")
        nsa_vector(v, "nsa")
        post_norm_vector(v, "p0", G_MIX_POST, "ffn0")
        pre_norm_vector(v, "n1", G_FFN_PRE)
        ffn_vector(v, 0)
        post_norm_vector(v, "p1", G_FFN_POST)
        pre_norm_vector(v, "n2", G_MIX_PRE + 1)
        moba_vector(v, "moba")
        post_norm_vector(v, "p2", G_MIX_POST + 1, "ffn1")
        pre_norm_vector(v, "n3", G_FFN_PRE + 1)
        ffn_vector(v, 1)
        post_norm_vector(v, "p3", G_FFN_POST + 1)
        pre_norm_vector(v, "n4", G_MIX2)
        v.wait_ge(S("load", "masks"), 16)
        hgrn_vector(v, "hgrn")
        hyena_pads_vector(v, "hyena")
        hyena_vector(v, "hyena")
        hgrn_norm_vector(v, "hnorm")
        merge_vector(v, "merge")
        pre_norm_vector(v, "n5", G_FFN2)
        picks_vector(v, "picks")
        peer_first(lambda k, i: rest_of(v, "peer", k, i))
        spread_vector(v, "spread")
        peer_vector(v, "peer")
        pre_norm_vector(v, "n6", G_FINAL)

    @block.gpsimd
    def _(pool):
        hybrid_gpsimd(pool, "hyena")
        rests_gpsimd(pool, "pq")
        spread_gpsimd(pool, "spread")

    ctx.close()



def shape_tables():
    t = {}
    pp = np.arange(P)
    t["eye"] = np.eye(P)
    t["iota"] = np.tile(np.arange(P), (P, 1))
    inv = (np.float32(10000.0) ** (-np.arange(0, HD, 2, dtype=np.float32) / np.float32(HD))).astype(np.float32)
    ang = np.arange(T, dtype=np.float32)[:, None] * inv[None, :]
    cos, sin = np.cos(ang.astype(np.float64)).T, np.sin(ang.astype(np.float64)).T
    c4, s4 = np.tile(cos, (4, 1)), np.tile(sin, (4, 1))
    q = HD ** -0.5
    t["cos"] = np.concatenate([c4 * q, c4], 1)
    t["sin"] = np.concatenate([s4 * q, s4], 1)
    rot = np.zeros((P, P))
    for h in range(2):
        for d in range(32):
            rot[h * 64 + 32 + d, h * 64 + d] = -1.0
            rot[h * 64 + d, h * 64 + 32 + d] = 1.0
    t["rot"] = rot
    causal = np.zeros((P, 384))
    causal[:, 0:T] = np.where(np.arange(T)[None] <= P + pp[:, None], 0, NEG)
    causal[:, T:] = np.where(pp[None] <= pp[:, None], 0, NEG)
    t["causal"] = causal
    add, mul = np.zeros((P, 4, 16)), np.zeros((P, 4, 16))
    for g, tt in enumerate((1, 0)):
        ok = (np.arange(NC)[None] * 16 + 31) <= (tt * P + pp[:, None])
        for hh in range(2):
            add[:, g * 2 + hh, :NC] = np.where(ok, 0, NEG)
            mul[:, g * 2 + hh, :NC] = ok
    t["cmpadd"], t["cmpmul"] = add.reshape(P, -1), mul.reshape(P, -1)
    th = 2 * np.pi * ((np.arange(T)[:, None] * np.arange(T)[None, :]) % NFFT) / NFFT
    f = np.concatenate([np.cos(th), -np.sin(th)], 1)
    t["dft"] = f.reshape(2, P, 2 * T).transpose(1, 0, 2).reshape(P, -1)
    wgt = np.where(np.arange(T) == 0, 1.0, 2.0)[:, None] / NFFT
    g = np.concatenate([np.cos(th) * wgt, -np.sin(th) * wgt], 0)
    t["idft"] = g.reshape(4, P, T).transpose(1, 0, 2).reshape(P, -1)
    posn = np.arange(T, dtype=np.float32)
    tpos = posn / np.float32(T - 1)
    bands = np.linspace(1e-4, 15, 16, dtype=np.float32)
    a2 = (np.float32(2.0 * np.pi / T) * posn)[:, None] * bands[None, :]
    z = np.concatenate([tpos[:, None], np.cos(a2), -np.sin(a2)], 1)
    t["zT"] = np.pad(z.T, ((0, P - 33), (0, 0)))
    t["ntap"] = -tpos.reshape(2, P).T
    cm = np.zeros((P, 2))
    cm[0:8, 0], cm[8:16, 1] = 1, -1
    t["cmask"] = cm
    eb, et = np.zeros((P, 8)), np.zeros((P, 8))
    for h in range(8):
        eb[8 + h, h], et[h, h] = 1, 1
    t["ebot"], t["etop"] = eb, et
    tm = np.ones((P, 2))
    tm[0, 0] = 0
    t["tapmask"] = tm
    out = np.zeros((P, N_TABLE), np.float32)
    for k, (a, n) in TABLE.items():
        out[:, a:a + n] = t[k]
    s, c = np.meshgrid(pp, pp, indexing="ij")
    m = [((s >> (l + 1)) == (c >> (l + 1))) & ((s >> l) != (c >> l)) for l in range(LEVELS)]
    return out, np.stack(m, 1).astype(np.int32)


def pack(a):
    f = lambda k: np.asarray(a[k])
    parts = []

    def cols(w):
        m = w.shape[1] // P
        parts.append(w.reshape(KC, P, m, P).transpose(2, 1, 0, 3).reshape(m, P, D))

    def rows(w):
        parts.append(w.reshape(-1, P, D))

    win = f("ev_w_in")[0]
    e = 0
    o = {}
    for name, n in (("fq", 512), ("fk", 512), ("fv", 512), ("f", 8), ("nq", 512), ("kc", 128), ("vc", 128), ("ks", 128),
                    ("vs", 128), ("kw", 128), ("vw", 128), ("g", 24)):
        o[name] = win[:, e:e + n]
        e += n
    for p in range(4):
        for name in ("fq", "fk", "fv"):
            cols(o[name][:, p * P:(p + 1) * P])
    pairs = np.concatenate([np.r_[j * HD:(j + 1) * HD, (j + 4) * HD:(j + 5) * HD] for j in range(4)])
    for name in ("kc", "vc"):
        for g in range(2):
            cols(np.concatenate([o[name][:, g * HD:(g + 1) * HD]] * 2, 1))
    for name in ("ks", "kw", "vs", "vw"):
        cols(o[name])
    cols(o["nq"][:, pairs])
    for name in ("ev_cmp_w1_k", "ev_cmp_w1_v"):
        parts.append(f(name)[0].reshape(4, 4, P, T).transpose(0, 2, 1, 3).reshape(4, P, D))
    cols(f("ev_w_out")[0][np.concatenate([np.arange(512), 512 + pairs])])

    def ffn(layer):
        g, u, dn = f("ffn_w_gate")[layer], f("ffn_w_up")[layer], f("ffn_w_down")[layer]
        for c in range(0, FC, 2):
            for cc in (c, c + 1):
                cols(g[:, cc * P:(cc + 1) * P])
                cols(u[:, cc * P:(cc + 1) * P])
            rows(dn[c * P:(c + 2) * P])

    ffn(0)
    wo = f("od_w_in")[0]
    for p in range(8):
        for n in range(3):
            cols(wo[:, n * D + p * P:n * D + (p + 1) * P])
    cols(f("od_w_out")[0])
    ffn(1)
    w = f("w_in_2")[0]
    seg = lambda n, j: w[:, n * D + j * P:n * D + (j + 1) * P]
    for h in range(HH):
        for n in (0, 1, 2, 3, 4, 8):
            cols(seg(n, h))
    for j in range(KC):
        for n in (5, 6, 7, 9):
            cols(seg(n, j))
    for name in ("w_branch_b_2", "w_branch_a_2", "w_out_2"):
        cols(f(name)[0])
    cols(f("peer_w_q_2")[0])
    u = f("peer_u_2")[0].reshape(NKEYS, P, KC, P).transpose(0, 3, 2, 1).reshape(NKEYS, P, D)
    v = f("peer_v_2")[0].reshape(NKEYS, P, D)
    late = EARLY + 2
    both = np.stack([v[EARLY:-2], u[late:]], 1).reshape(-1, P, D)
    parts += [u[0:EARLY], v[0:EARLY], u[EARLY:late], both, v[-2:]]
    weights = np.concatenate(parts)

    small = np.zeros((P, N_SMALL), np.float32)

    def put(name, v):
        a0, n = SMALL[name]
        assert v.shape[1] == n, (name, v.shape)
        small[0:v.shape[0], a0:a0 + n] = v

    gp = np.concatenate([np.stack([o["g"][:, (j + 4 * hh) * 3 + b] for j in range(4) for hh in range(2)], 1) for b in range(3)], 1)
    wfg = np.concatenate([o["f"], o["f"], gp], 1)
    put("wfg", wfg.reshape(KC, P, 40).transpose(1, 0, 2).reshape(P, -1))
    for k in "kv":
        put("w2" + k, f("ev_cmp_w2_" + k)[0].reshape(2, P, HD).transpose(1, 0, 2).reshape(P, -1))
        put("pe" + k, f("ev_cmp_pe_" + k)[0].reshape(16, 2, HD).transpose(1, 2, 0).reshape(P, 16))
    put("bf", np.tile(f("ev_b_f")[0], 2)[:, None])
    gs = np.concatenate([f("g_mix_pre"), f("g_mix_post"), f("g_ffn_pre"), f("g_ffn_post"), f("norm_mix_g_2"),
                         f("norm_ffn_g_2"), f("norm_final_g_2")[None]])
    put("gains", gs.reshape(11, KC, P).transpose(2, 0, 1).reshape(P, -1))
    put("lbl", f("hgrn_lb_logits_2").reshape(2, HH, P).transpose(2, 0, 1).reshape(P, -1))
    put("hg", f("hgrn_norm_g_2").reshape(P, 1))
    put("convw", f("hyena_conv_w_2")[0].reshape(3, 24, P).transpose(2, 1, 0).reshape(P, -1))
    put("convb", f("hyena_conv_b_2")[0].reshape(24, P).T)
    put("hbias", f("hyena_bias_2")[0].reshape(KC, P).T)
    put("fw1", f("filt_w1_2")[0])
    put("fvec", np.stack([f("filt_b1_2")[0], f("filt_freq1_2")[0], f("filt_b2_2")[0], f("filt_freq2_2")[0]], 1))
    put("fw2", f("filt_w2_2")[0])
    tables, masks = shape_tables()
    return {
        "weights": weights, "small": small, "tables": tables, "masks": masks,
        "w3": f("filt_w3_2")[0], "decay": f("filt_decay_2"),
        "subkeys": f("peer_subkeys_2")[0].transpose(3, 0, 1, 2).reshape(P, 16, NKEYS),
        "x": f("x")[0].T.reshape(KC, P, T).transpose(1, 0, 2),
    }


def kernel(**inputs):
    import concourse.bacc as _bacc
    from concourse.bass_utils import run_bass_kernel_spmd as _run

    nc = _bacc.Bacc("TRN2", target_bir_lowering=False, num_devices=1)
    arrays, args = {}, {}
    for name, a in pack(inputs).items():
        a = np.ascontiguousarray(a)
        arrays[f"in_{name}"] = a
        args[name] = nc.dram_tensor(f"in_{name}", a.shape, mybir.dt.from_np(a.dtype), kind="ExternalInput").ap()
    out = nc.dram_tensor("out_x", (P, KC, T), F32, kind="ExternalOutput").ap()
    build(nc, out=out, **args)
    r = _run(nc, [arrays], core_ids=[0])
    y = np.asarray(r.results[0]["out_x"])
    return np.ascontiguousarray(y.transpose(2, 1, 0).reshape(1, T, D))
```
